# Optimizing a Trainium2 kernel written in Bass

```python
import math
import jax, jax.numpy as jnp
from jax import lax
import numpy as np

D_MODEL = 1024
BATCH = 1
SEQ = 512
DEPTH = 2
DEC_BATCH = 8
DEC_SEQ = 1
PAST_LEN = 256
PAGE_SIZE = 128

N_META = 16
D_MIX = D_MODEL
HEAD_DIM = 64
D_A = D_MIX // 2
N_HEADS_A = D_A // HEAD_DIM
ROPE_THETA = 500000.0
N_IDX_HEADS = 8
D_IDX = 32
TOPK_MAX = 256
Q_BLOCK = 128
D_B = D_MIX // 4
POOL_WINDOWS = (2, 4, 8, 16)
N_POOL_GROUPS = 4
POOL_GROUP = D_B // N_POOL_GROUPS
POOL_STATE = 16 - 1
D_C = D_MIX - D_A - D_B
CONV_WIDTH = 31
CONV_STATE = CONV_WIDTH - 1
EPS = 1e-6
IN_SPLITS = (D_A, D_A, D_A, D_A, N_IDX_HEADS * D_IDX, N_IDX_HEADS, D_IDX, D_B, D_B, D_C, D_C, D_C)
N_IN = 4 * D_A + N_IDX_HEADS * D_IDX + N_IDX_HEADS + D_IDX + 2 * D_B + 3 * D_C

kernel_name = 'hybrid_dsa_pool_conformer_step'

def rms_norm(x, g):
    xf = x.astype(jnp.float32)
    y = xf * lax.rsqrt(jnp.mean(xf * xf, axis=-1, keepdims=True) + EPS)
    return (y * g.astype(jnp.float32)).astype(x.dtype)

def layer_norm(x, g, b):
    xf = x.astype(jnp.float32)
    mu = jnp.mean(xf, axis=-1, keepdims=True)
    xc = xf - mu
    var = jnp.mean(xc * xc, axis=-1, keepdims=True)
    y = xc * lax.rsqrt(var + EPS) * g.astype(jnp.float32) + b.astype(jnp.float32)
    return y.astype(x.dtype)

def partial_rope(x, pos):
    rot = x.shape[-1] // 4
    half = rot // 2
    inv = ROPE_THETA ** (-(jnp.arange(half, dtype=jnp.float32) / half))
    ang = pos.astype(jnp.float32)[:, None] * inv[None, :]
    cos = jnp.cos(ang)[None, :, None, :]
    sin = jnp.sin(ang)[None, :, None, :]
    x1 = x[..., :half].astype(jnp.float32)
    x2 = x[..., half:rot].astype(jnp.float32)
    r = jnp.concatenate([x1 * cos - x2 * sin, x2 * cos + x1 * sin], axis=-1).astype(x.dtype)
    return jnp.concatenate([r, x[..., rot:]], axis=-1)

def split_columns(z):
    parts, start = [], 0
    for width in IN_SPLITS:
        parts.append(z[..., start:start + width])
        start += width
    return parts

def project(x, pos, norm_g_l, w_in_l, q_norm_g_l, k_norm_g_l):
    b, t = x.shape[0], x.shape[1]
    h = rms_norm(x, norm_g_l)
    z = jnp.einsum('btd,dn->btn', h, w_in_l)
    q, k, v, ga, qi, wi, ki, ub, gb, cv, cg, gc = split_columns(z)
    q = partial_rope(rms_norm(q.reshape(b, t, N_HEADS_A, HEAD_DIM), q_norm_g_l), pos)
    k = partial_rope(rms_norm(k.reshape(b, t, N_HEADS_A, HEAD_DIM), k_norm_g_l), pos)
    v = v.reshape(b, t, N_HEADS_A, HEAD_DIM)
    qi = partial_rope(qi.reshape(b, t, N_IDX_HEADS, D_IDX), pos)
    ki = partial_rope(ki[:, :, None, :], pos)[:, :, 0]
    uc = cv * jax.nn.sigmoid(cg)
    return q, k, v, ga, qi, wi, ki, ub, gb, uc, gc

def indexer_scores(qi, wi, ki):
    dots = jnp.einsum('bqhd,bsd->bqhs', qi, ki).astype(jnp.float32) * (D_IDX ** -0.5)
    w = wi.astype(jnp.float32) * (N_IDX_HEADS ** -0.5)
    return jnp.einsum('bqh,bqhs->bqs', w, jax.nn.relu(dots))

def gathered_attention(q, k_sel, v_sel, valid):
    s = jnp.einsum('bqhd,bqkhd->bqhk', q, k_sel).astype(jnp.float32) * (HEAD_DIM ** -0.5)
    s = jnp.where(valid[:, :, None, :], s, -jnp.inf)
    p = jax.nn.softmax(s, axis=-1)
    return jnp.einsum('bqhk,bqkhd->bqhd', p.astype(v_sel.dtype), v_sel)

def prompt_sparse_attention(q, k, v, qi, wi, ki, top_k):
    b, t = q.shape[0], q.shape[1]
    n_blk = -(-t // Q_BLOCK)
    pad = n_blk * Q_BLOCK - t

    def blocks(a):
        a = jnp.pad(a, [(0, 0), (0, pad)] + [(0, 0)] * (a.ndim - 2))
        return jnp.swapaxes(a.reshape((b, n_blk, Q_BLOCK) + a.shape[2:]), 0, 1)

    key_pos = jnp.arange(t, dtype=jnp.int32)

    def one_block(args):
        i, q_b, qi_b, wi_b = args
        q_pos = i * Q_BLOCK + jnp.arange(Q_BLOCK, dtype=jnp.int32)
        sc = indexer_scores(qi_b, wi_b, ki)
        adm = key_pos[None, :] <= q_pos[:, None]
        sc = jnp.where(adm[None], sc, -jnp.inf)
        _, idx = lax.top_k(sc, top_k)
        valid = idx <= q_pos[None, :, None]
        k_sel = jax.vmap(lambda kk, ii: kk[ii])(k, idx)
        v_sel = jax.vmap(lambda vv, ii: vv[ii])(v, idx)
        return gathered_attention(q_b, k_sel, v_sel, valid)

    o = lax.map(one_block, (jnp.arange(n_blk, dtype=jnp.int32), blocks(q), blocks(qi), blocks(wi)))
    o = jnp.swapaxes(o, 0, 1).reshape(b, n_blk * Q_BLOCK, N_HEADS_A, HEAD_DIM)[:, :t]
    return o.reshape(b, t, D_A)

def sample_sparse_attention(q, k_new, v_new, qi, wi, ki_new, cache_k_l, cache_v_l, cache_ki_l, page_table, top_k):
    db, ts = q.shape[0], q.shape[1]
    ki_past = cache_ki_l[page_table].reshape(db, PAST_LEN, D_IDX)
    ki_all = jnp.concatenate([ki_past, ki_new], axis=1)
    sc = indexer_scores(qi, wi, ki_all)
    q_pos = PAST_LEN + jnp.arange(ts, dtype=jnp.int32)
    key_pos = jnp.arange(PAST_LEN + ts, dtype=jnp.int32)
    sc = jnp.where((key_pos[None, :] <= q_pos[:, None])[None], sc, -jnp.inf)
    _, idx = lax.top_k(sc, top_k)
    valid = idx <= q_pos[None, :, None]
    in_past = idx < PAST_LEN
    pidx = jnp.minimum(idx, PAST_LEN - 1)
    phys = jax.vmap(lambda pt, ii: pt[ii])(page_table, pidx // PAGE_SIZE)
    off = pidx % PAGE_SIZE
    nidx = jnp.clip(idx - PAST_LEN, 0, ts - 1)
    k_sel = jnp.where(in_past[..., None, None], cache_k_l[phys, off],
                      jax.vmap(lambda kk, ii: kk[ii])(k_new, nidx))
    v_sel = jnp.where(in_past[..., None, None], cache_v_l[phys, off],
                      jax.vmap(lambda vv, ii: vv[ii])(v_new, nidx))
    o = gathered_attention(q, k_sel, v_sel, valid)
    return o.reshape(db, ts, D_A)

def pool_branch(u, prev, pos, w_groups, scale):
    b, t = u.shape[0], u.shape[1]
    p = prev.shape[1]
    ext = jnp.concatenate([prev, u], axis=1)
    cs = jnp.pad(jnp.cumsum(ext.astype(jnp.float32), axis=1), ((0, 0), (1, 0), (0, 0)))
    upto = cs[:, p + 1:p + 1 + t]
    groups = []
    for g, win in enumerate(POOL_WINDOWS):
        lo, hi = g * POOL_GROUP, (g + 1) * POOL_GROUP
        before = cs[:, p + 1 - win:p + 1 - win + t, lo:hi]
        cnt = jnp.minimum(pos + 1, win).astype(jnp.float32)[None, :, None]
        groups.append((upto[..., lo:hi] - before) / cnt - u[..., lo:hi].astype(jnp.float32))
    d = jnp.stack(groups, axis=2).astype(u.dtype)
    y = jnp.einsum('btgi,gio->btgo', d, w_groups).reshape(b, t, D_B)
    return y * scale, ext[:, -POOL_STATE:]

def conv_branch(u, prev, w, bias, g, beta):
    ext = jnp.concatenate([prev, u], axis=1)
    y = lax.conv_general_dilated(ext, w[:, None, :], window_strides=(1,), padding='VALID',
                                 dimension_numbers=('NWC', 'WIO', 'NWC'), feature_group_count=D_C)
    y = jax.nn.silu(layer_norm(y + bias, g, beta))
    return y, ext[:, -CONV_STATE:]

def merge_groups(att, ga, pool, gb, conv, gc, w_out_l):
    y = jnp.concatenate([att * jax.nn.silu(ga), pool * jax.nn.silu(gb), conv * jax.nn.silu(gc)], axis=-1)
    return jnp.einsum('btm,md->btd', y, w_out_l)

def setup_inputs(seed: int = 0) -> dict:
    key = jax.random.key(seed)
    ks = jax.random.split(key, 20)
    n_pages = PAST_LEN // PAGE_SIZE
    n_used = DEC_BATCH * n_pages
    n_phys = n_used + n_used // 4
    f32 = jnp.float32
    nrm = lambda k, shape, s: jax.random.normal(k, shape, f32) * s
    page_table = jax.random.permutation(ks[0], n_phys)[:n_used].reshape(DEC_BATCH, n_pages).astype(jnp.int32)
    return {
        'x_prompt': nrm(ks[1], (BATCH, SEQ, D_MODEL), 1.0),
        'x_sample': nrm(ks[2], (DEC_BATCH, DEC_SEQ, D_MODEL), 1.0),
        'cache_k': nrm(ks[3], (DEPTH, n_phys, PAGE_SIZE, N_HEADS_A, HEAD_DIM), 1.0),
        'cache_v': nrm(ks[4], (DEPTH, n_phys, PAGE_SIZE, N_HEADS_A, HEAD_DIM), 1.0),
        'cache_kidx': nrm(ks[5], (DEPTH, n_phys, PAGE_SIZE, D_IDX), 1.0),
        'state_pool': nrm(ks[6], (DEPTH, DEC_BATCH, POOL_STATE, D_B), 1.0),
        'state_conv': nrm(ks[7], (DEPTH, DEC_BATCH, CONV_STATE, D_C), 1.0),
        'page_table': page_table,
        'meta_tokens': nrm(ks[8], (N_META, D_MODEL), 1.0),
        'norm_g': 1.0 + nrm(ks[9], (DEPTH, D_MODEL), 0.02),
        'w_in': nrm(ks[10], (DEPTH, D_MODEL, N_IN), D_MODEL ** -0.5),
        'q_norm_g': 1.0 + nrm(ks[11], (DEPTH, HEAD_DIM), 0.02),
        'k_norm_g': 1.0 + nrm(ks[12], (DEPTH, HEAD_DIM), 0.02),
        'pool_w': nrm(ks[13], (DEPTH, N_POOL_GROUPS, POOL_GROUP, POOL_GROUP), POOL_GROUP ** -0.5),
        'pool_scale': 1.0 + nrm(ks[14], (DEPTH, D_B), 0.02),
        'conv_w': nrm(ks[15], (DEPTH, CONV_WIDTH, D_C), CONV_WIDTH ** -0.5),
        'conv_b': nrm(ks[16], (DEPTH, D_C), 0.02),
        'conv_norm_g': 1.0 + nrm(ks[17], (DEPTH, D_C), 0.02),
        'conv_norm_b': nrm(ks[18], (DEPTH, D_C), 0.02),
        'w_out': nrm(ks[19], (DEPTH, D_MIX, D_MODEL), D_MIX ** -0.5),
    }

def reference(x_prompt, x_sample, cache_k, cache_v, cache_kidx, state_pool, state_conv, page_table,
              meta_tokens, norm_g, w_in, q_norm_g, k_norm_g, pool_w, pool_scale,
              conv_w, conv_b, conv_norm_g, conv_norm_b, w_out):
    b = x_prompt.shape[0]
    t = SEQ + N_META
    meta = jnp.broadcast_to(meta_tokens[None].astype(x_prompt.dtype), (b, N_META, D_MODEL))
    hp = jnp.concatenate([meta, x_prompt], axis=1)
    hs = x_sample
    pos_p = jnp.arange(t, dtype=jnp.int32)
    pos_s = PAST_LEN + jnp.arange(DEC_SEQ, dtype=jnp.int32)
    topk_p = min(TOPK_MAX, t // 4)
    topk_s = min(TOPK_MAX, (PAST_LEN + DEC_SEQ) // 4)
    kp, vp, kip, plp, cvp = [], [], [], [], []
    kss, vss, kis, pls, cvs = [], [], [], [], []
    for l in range(DEPTH):
        q, k, v, ga, qi, wi, ki, ub, gb, uc, gc = project(hp, pos_p, norm_g[l], w_in[l], q_norm_g[l], k_norm_g[l])
        att = prompt_sparse_attention(q, k, v, qi, wi, ki, topk_p)
        pool, pool_st = pool_branch(ub, jnp.zeros((b, POOL_STATE, D_B), ub.dtype), pos_p, pool_w[l], pool_scale[l])
        conv, conv_st = conv_branch(uc, jnp.zeros((b, CONV_STATE, D_C), uc.dtype), conv_w[l], conv_b[l],
                                    conv_norm_g[l], conv_norm_b[l])
        hp = hp + merge_groups(att, ga, pool, gb, conv, gc, w_out[l])
        kp.append(k); vp.append(v); kip.append(ki); plp.append(pool_st); cvp.append(conv_st)
        q, k, v, ga, qi, wi, ki, ub, gb, uc, gc = project(hs, pos_s, norm_g[l], w_in[l], q_norm_g[l], k_norm_g[l])
        att = sample_sparse_attention(q, k, v, qi, wi, ki, cache_k[l], cache_v[l], cache_kidx[l], page_table, topk_s)
        pool, pool_st = pool_branch(ub, state_pool[l], pos_s, pool_w[l], pool_scale[l])
        conv, conv_st = conv_branch(uc, state_conv[l], conv_w[l], conv_b[l], conv_norm_g[l], conv_norm_b[l])
        hs = hs + merge_groups(att, ga, pool, gb, conv, gc, w_out[l])
        kss.append(k); vss.append(v); kis.append(ki); pls.append(pool_st); cvs.append(conv_st)
    y_prompt = hp[:, N_META:]
    y_sample = hs
    new_k_prompt = jnp.stack(kp, axis=0)
    new_v_prompt = jnp.stack(vp, axis=0)
    new_kidx_prompt = jnp.stack(kip, axis=0)
    new_pool_prompt = jnp.stack(plp, axis=0)
    new_conv_prompt = jnp.stack(cvp, axis=0)
    new_k_sample = jnp.stack(kss, axis=0)
    new_v_sample = jnp.stack(vss, axis=0)
    new_kidx_sample = jnp.stack(kis, axis=0)
    new_pool_sample = jnp.stack(pls, axis=0)
    new_conv_sample = jnp.stack(cvs, axis=0)
    return (y_prompt, y_sample, new_k_prompt, new_v_prompt, new_kidx_prompt, new_pool_prompt, new_conv_prompt,
            new_k_sample, new_v_sample, new_kidx_sample, new_pool_sample, new_conv_sample)


_drawn_inputs = setup_inputs


def setup_inputs(seed=0):
    import zlib

    import numpy as np

    out = dict(_drawn_inputs(seed))
    spreads = {}
    factors = {'q_norm_g': 8.0,
     'k_norm_g': 3.055,
     'pool_scale': 5.687,
     'conv_b': 5.561,
     'conv_norm_g': 7.799,
     'conv_norm_b': 16.023}
    for name, (base, spread) in spreads.items():
        noise = np.random.default_rng([zlib.crc32(name.encode()), seed]).standard_normal(out[name].shape)
        drawn = base * np.exp(spread * noise) if base else spread * noise
        out[name] = __import__('jax').numpy.asarray(drawn.astype(out[name].dtype))
    for name, factor in factors.items():
        out[name] = (out[name] * factor).astype(out[name].dtype)
    return out
```

```python
from contextlib import ExitStack

import numpy as np

import concourse.bass as bass
from concourse import mybir

F32 = mybir.dt.float32
I32 = mybir.dt.int32
ALU = mybir.AluOpType
ACT = mybir.ActivationFunctionType
AX = mybir.AxisListType

D_MODEL, SEQ, N_META, DEPTH = 1024, 512, 16, 2
N_SAMPLE, PAST, PAGE = 8, 256, 128
N_PAGES = PAST // PAGE
HEADS, HD = 8, 64
IH, ID = 8, 32
TOPK_P, TOPK_S = 132, 64
THETA = 500000.0
EPS = 1e-6
WINDOWS = (2, 4, 8, 16)
POOL_STATE, CONV_STATE, CONV_W = 15, 30, 31
D_B = D_C = 256

NTOK = SEQ + N_META
TOK = NTOK + N_SAMPLE
HALF = TOK // 2
KC = D_MODEL // 128
START = [0, 107, 214, 320, 426]
ROWS = [107, 107, 106, 106, 102]
NT = len(START)
ROWS_P = ROWS[:4] + [ROWS[4] + N_SAMPLE]
S0 = ROWS[4]
MAXR = 107
SR = 110
WIDTH = [START[i] + ROWS[i] for i in range(NT)]
SENT = (-TOPK_P) % 8
ROUNDS = (TOPK_P + SENT) // 8
NEG, GONE, CUT, BIG = -1e30, -3e38, -2e38, 3e38

C_Q, C_K, C_V, C_GA, C_I, C_UB, C_GB, C_CV, C_GC = 0, 512, 1024, 1536, 2048, 2344, 2600, 2856, 3368
GROUPS = [("in", C_I, 296), ("in", C_CV, 512), ("in", C_K, 512), ("in", C_V, 512), ("in", C_Q, 512),
          ("in", C_UB, 512), ("in", C_GC, 256), ("in", C_GA, 512), ("out", 0, 512), ("out", 512, 512)]
W_SLOTS = 5

UNITS = ([("idx", i, 0) for i in range(NT)]
         + [("conv", m, h) for m in (0, 2, 1, 3) for h in range(2)]
         + [(n, i, 0) for n in ("k", "v", "q") for i in range(NT)]
         + [("ub", m, h) for m in range(4) for h in range(2)]
         + [("gc", m, h) for m in range(2) for h in range(2)]
         + [("mean", 0, h) for h in range(2)]
         + [("ga", m, h) for m in range(4) for h in range(2)]
         + [("pool", m, h) for m in range(2) for h in range(2)]
         + [("out", m, h) for m in range(KC) for h in range(2)])
NUM = {u: n for n, u in enumerate(UNITS)}
ON_ACT = ("idx", "k", "v", "q")
ACT_ORDER = ([("idx", i, 0) for i in range(NT)] + [("k", i, 0) for i in range(4)] + [("v", 0, 0), ("k", 4, 0)]
             + [("v", i, 0) for i in range(1, NT)] + [("q", i, 0) for i in range(NT)])
GROUP_OF = {"idx": 0, "conv": 1, "k": 2, "v": 3, "q": 4, "ub": 5, "gc": 6, "ga": 7}
LAST_UNIT = [("idx", 4, 0), ("conv", 3, 1), ("k", 4, 0), ("v", 4, 0), ("q", 4, 0), ("ub", 3, 1),
             ("gc", 1, 1), ("ga", 3, 1), ("out", 3, 1), ("out", 7, 1)]

PIECES = [(i, h, a, b) for pair in ((1, 2), (3, 4)) for h in range(IH) for i in pair
          for a, b in ([(0, WIDTH[i])] if WIDTH[i] <= 512 else [(0, WIDTH[i] // 2), (WIDTH[i] // 2, WIDTH[i])])]
ITEMS = [(i, h) for i in range(NT) for h in range(HEADS)]

K_ID, K_ROT, K_CNT, K_WIN, K_E, K_ET, K_TRI = 0, 128, 128 + 48 * NT, 160 + 48 * NT, 162 + 48 * NT, 226 + 48 * NT, 234 + 48 * NT
K_END = K_TRI + MAXR


GATES = ([(("ub", m, h), 2 + m) for m in (2, 3) for h in range(2)]
         + [(("gc", m, h), 6 + m) for m in range(2) for h in range(2)]
         + [(("ga", m, h), m) for m in range(4) for h in range(2)])
IX_V, IX_Q = [2, 3, 3, 4, 4], [5, 5, 5, 5, 4]
CONV_END, PD_END, LN_END = 2 * CONV_W + 6, 14, 8
SD = {"isc": 3, "logit_in": 29, "negmax": 31, "etp": 34}
SX = {"logits": 2, "max": 3, "exp": 4, "norm": 6, "turn": 8, "keep": 9, "pv": 11, "gate": 20}


def constants():
    c = np.zeros((128, K_END), np.float32)
    c[:, :128] = np.eye(128)
    for i in range(NT):
        pos = np.full(128, float(PAST), np.float32)
        pos[:ROWS[i]] = START[i] + np.arange(ROWS[i])
        o = K_ROT + 48 * i
        for half, off in ((8, 0), (4, 32)):
            inv = np.float32(THETA) ** (-(np.arange(half, dtype=np.float32) / np.float32(half)))
            ang = pos[:, None] * inv[None, :].astype(np.float32)
            cos, sin = np.cos(ang), np.sin(ang)
            c[:, o + off:o + off + 4 * half] = np.concatenate([cos, cos, -sin, sin], 1)
    for m in range(2):
        for g in range(2):
            win = WINDOWS[2 * m + g]
            rows = slice(64 * g, 64 * g + 64)
            c[rows, K_CNT + 16 * m:K_CNT + 16 * m + 16] = 1.0 / np.minimum(np.arange(16) + 1, win)
            c[rows, K_WIN + m] = 1.0 / win
    for b in range(8):
        c[b, K_E + 8 * b:K_E + 8 * b + 8] = 1
        c[8 * b:8 * b + 8, K_ET + b] = 1
    t = np.arange(MAXR)
    c[:MAXR, K_TRI:K_TRI + MAXR] = np.where(t[None, :] <= t[:, None], 0, NEG)
    return c


class Stage:

    def __init__(self, sem):
        self.sem, self.n = sem, 0

    def did(self, ins):
        ins.then_inc(self.sem, 1)
        self.n += 1
        return ins


def program(nc, a, o):
    ctx = ExitStack()
    with ctx:
        def sb(name, *shape, dt=F32):
            return ctx.enter_context(nc.sbuf_tensor(name, list(shape), dt))

        def ps(name, *shape):
            return ctx.enter_context(nc.psum_tensor(name, list(shape), F32))

        layer_sems, loads = [], []

        def sem(name):
            s = ctx.enter_context(nc.semaphore(name))
            layer_sems.append(s)
            return s

        def stage(name):
            return Stage(sem(name))

        cst = sb("cst", 128, K_END)
        ident = cst[:, 0:128]
        E8 = cst[0:8, K_E:K_E + 64]
        ET8 = cst[0:64, K_ET:K_ET + 8]
        tri = cst[:, K_TRI:K_TRI + MAXR]
        ones = sb("ones", 128, 128)
        pow_e = sb("pow_e", 128, 8)
        table = sb("table", 1, N_SAMPLE * N_PAGES, dt=I32)
        params = sb("params", 128, DEPTH, 78)
        prm = sb("prm", 128, 78)
        prm_h = sb("prm_h", 128, 8)
        xT = sb("xT", 128, KC, TOK)
        xg = sb("xg", 128, KC, TOK)
        yT = sb("yT", 128, KC, TOK)
        W = sb("W", 128, W_SLOTS, 4, 512)
        kT = sb("kT", 128, 4, TOK)
        qT = sb("qT", 128, 4, TOK)
        V = sb("V", 128, NT, 512)
        bias = sb("bias", 128, NT - 1, SENT + NTOK)
        zi = sb("zi", 128, NT, 392)
        qkT = sb("qkT", 128, 3, TOK)
        kz = sb("kz", 128, 3, 512)
        ksq = sb("ksq", 128, 2, 512)
        gam = sb("gam", 128, 2, 64)
        uext = sb("uext", 128, 2, CONV_STATE + NTOK)
        uxs = sb("uxs", 128, 2, N_SAMPLE, CONV_W)
        bufA = sb("bufA", 128, 2, 552)
        bufB = sb("bufB", 128, 2, 552)
        cc = sb("cc", 128, 2, TOK)
        ubx = sb("ubx", 128, 2, POOL_STATE + NTOK)
        ubs = sb("ubs", 128, 2, N_SAMPLE, 16)
        pwb = sb("pwb", 128, 2, 128)
        row = sb("row", 128, TOK)
        rel = sb("rel", 128, 2, 552)
        gt = sb("gt", 128, 2, HALF)
        small = sb("small", 128, 192)
        kic = sb("kic", 128, N_SAMPLE, N_PAGES, ID)
        KV = sb("KV", 128, 4, 512)
        rows8 = sb("rows8", 8, 3 * 512)
        zis = sb("zis", 8, 392)
        sc8 = sb("sc8", 8, 272)
        ixp = ubx[:, :, :].rearrange("p a b -> p (a b)")[:, 0:512]
        smp = kz[:, 0, :]
        pn = ksq[0:64, 1, 0:260]
        p64 = ksq[0:8, 1, 260:452]
        rot_tmp = sb("rot_tmp", 128, 256)
        ds = smp[:, 0:128].rearrange("p (g b h) -> p g b h", g=2, b=8)
        ssm = smp[:, 128:256].rearrange("p (g x) -> p g x", g=2)
        wbc = smp[:, 256:320]
        pts = smp[:, 320:448].rearrange("p (g x) -> p g x", g=2)
        sn = p64[:, 0:64]
        pd = p64[:, 64:128]
        qb = uext[:, :, :].rearrange("p a b -> p (a b)")[:, 0:1024].rearrange("p (a b) -> p a b", a=2)
        lnrow = rel[:, 0, 0:TOK]
        conv_new = kz[:, 1, :]
        pool_new = kz[:, 2, :]
        st_in = bufA[:, :, 0:256]
        stp_in = bufB[:, 0, 0:256]
        ssum = small[:, 0:8]
        rinv = small[:, 8:16]
        mn = small[:, 16:18]
        rsum = small[:, 18:34].rearrange("p (a b) -> p a b", a=2)
        rrec = small[:, 34:42]
        kss = small[:, 42:58].rearrange("p (a b) -> p a b", a=2)
        krn = small[:, 58:74].rearrange("p (a b) -> p a b", a=2)
        m8 = small[:, 74:90].rearrange("p (a b) -> p a b", a=2)
        lnv = small[:, 90:98]
        lnr = small[:, 98:106]
        wsum = small[:, 106:122].rearrange("p (a b) -> p a b", a=2)
        smx = small[0:64, 122:123]
        snm = small[0:64, 123:124]
        srs = small[0:64, 124:125]
        srr = small[0:64, 125:126]
        d8 = small[0:8, 126:134]
        e8 = small[0:8, 134:142]
        etp = small[0:64, 142:150]
        snw = small[0:8, 150:158]
        m8s = small[0:8, 158:166]
        isc = small[:, 166:182]
        diag = ksq[:, :, :].rearrange("p a b -> p (a b)")[:, 0:NT * SR].rearrange("p (a b) -> p a b", a=NT)

        R = ps("R", 128, 4, 512)
        A = ps("A", 128, 4, 512)

        xin = W[:, :, :, :].rearrange("p s k n -> p (s k n)")[:, 0:NT * D_MODEL].rearrange("p (i n) -> p i n", i=NT)
        yout = xin

        pre = {n: ctx.enter_context(nc.semaphore(n)) for n in
               ("pre_const", "pre_table", "pre_x", "pre_params", "pre_ones", "pre_turned", "pre_kept", "pre_par_t",
                "pre_par_k", "post_turned", "post_act", "post_dve", "post_out")}
        pin = kz[:, 0, 0:DEPTH * 128].rearrange("p (l n) -> p l n", l=DEPTH)
        pcw = kz[:, 1, 0:DEPTH * 256].rearrange("p (l n) -> p l n", l=DEPTH)
        with nc.Block() as block:
            @block.sync
            def _(sp):
                sp.dma_start(cst[:], a["consts"]).then_inc(pre["pre_const"], 16)
                x = a["x_prompt"][0]
                sp.dma_start(xin[0:N_META, 0, :], a["meta_tokens"]).then_inc(pre["pre_x"], 16)
                for i in range(NT):
                    lo = max(START[i] - N_META, 0)
                    n = START[i] + ROWS[i] - N_META - lo
                    off = ROWS[i] - n
                    sp.dma_start(xin[off:ROWS[i], i, :], x[lo:lo + n, :]).then_inc(pre["pre_x"], 16)
                sp.dma_start(xin[S0:S0 + N_SAMPLE, 4, :], a["x_sample"].rearrange("b t d -> (b t) d")).then_inc(pre["pre_x"], 16)
                for l in range(DEPTH):
                    for name, r0, n in (("norm_g", 0, 8), ("pool_scale", 8, 2), ("conv_b", 10, 2),
                                        ("conv_norm_g", 12, 2), ("conv_norm_b", 14, 2)):
                        sp.dma_start(pin[r0:r0 + n, l, :], a[name][l].rearrange("(c p) -> c p", p=128)).then_inc(pre["pre_params"], 16)
                    sp.dma_start(pcw[0:CONV_W, l, :], a["conv_w"][l]).then_inc(pre["pre_params"], 16)
                sp.dma_start(table[:, :], a["page_table"].rearrange("b n -> (b n)").unsqueeze(0)).then_inc(pre["pre_table"], 16)
                sp.wait_ge(pre["pre_table"], 16)

            @block.gpsimd
            def _(pool):
                pool.memset(ones[:], 1.0).then_inc(pre["pre_ones"], 1)
                pool.memset(pow_e[:], -0.5).then_inc(pre["pre_ones"], 1)
                pool.wait_ge(pre["pre_ones"], 2)

            @block.tensor
            def _(pe):
                pe.wait_ge(pre["pre_const"], 16)
                pe.wait_ge(pre["pre_x"], 16 * (NT + 2))
                n = 0
                for i in range(NT):
                    for g in range(2):
                        if n >= 4:
                            pe.wait_ge(pre["pre_kept"], n - 3)
                        for j in range(4):
                            m = pe.transpose(R[:, n % 4, SR * j:SR * j + ROWS_P[i]],
                                             xin[0:ROWS_P[i], i, 128 * (4 * g + j):128 * (4 * g + j) + 128],
                                             ident[0:ROWS_P[i], 0:ROWS_P[i]])
                        m.then_inc(pre["pre_turned"], 1)
                        n += 1
                pe.wait_ge(pre["pre_params"], 16 * 6 * DEPTH)
                for l in range(DEPTH):
                    pe.transpose(A[:, l, 0:16], pin[0:16, l, :], ident[0:16, 0:16])
                    for m in range(2):
                        t = pe.transpose(A[:, l, 16 + 31 * m:47 + 31 * m], pcw[0:CONV_W, l, 128 * m:128 * m + 128],
                                         ident[0:CONV_W, 0:CONV_W])
                t.then_inc(pre["pre_par_t"], 1)

            @block.vector
            def _(dve):
                n = 0
                for i in range(NT):
                    for g in range(2):
                        dve.wait_ge(pre["pre_turned"], n + 1)
                        src = R[:, n % 4, 0:4 * SR].rearrange("p (j t) -> p j t", j=4)[:, :, 0:ROWS_P[i]]
                        dve.tensor_copy(xT[:, 4 * g:4 * g + 4, START[i]:START[i] + ROWS_P[i]], src).then_inc(pre["pre_kept"], 1)
                        n += 1
                dve.wait_ge(pre["pre_par_t"], 1)
                for l in range(DEPTH):
                    dve.tensor_copy(params[:, l, :], A[:, l, 0:78]).then_inc(pre["pre_par_k"], 1)
                dve.wait_ge(pre["pre_par_k"], DEPTH)

        w_in_s = [sem(f"w_loaded{s}") for s in range(W_SLOTS)]
        gam_s, pw_s, kic_s, state_s = sem("gamma_loaded"), sem("pool_w_loaded"), sem("kidx_loaded"), sem("states_loaded")
        zero_s = stage("pool_w_zeroed")
        misc0 = stage("constants_set")
        kv_s = [sem(f"kv_loaded{s}") for s in range(4)]
        unit_s, evA, evD = stage("unit_done"), stage("evac_act"), stage("evac_dve")
        sq_s, xg_s, prm_s = stage("squares"), stage("x_scaled"), stage("params_set")
        stats_s, var_s, rinv_s, diag_s, row_t, row_s = (stage(n) for n in (
            "sumsq_done", "var_done", "rinv_done", "diag_done", "row_turned", "row_kept"))
        rope_s, idxz_s, idxt_s, idxk_s = stage("idx_rope"), stage("idx_ready"), stage("idx_turned"), stage("idx_kept")
        ix_s, rel_s, acc_s, tk_s = stage("idx_dots"), stage("idx_relu"), stage("idx_acc"), stage("topk_step")
        kss_s, krn_s, kzg_s, kz_s, kqt_s, kqk_s = (stage(n) for n in (
            "kq_sumsq", "kq_rinv", "kq_step", "kq_ready", "kq_turned", "kq_kept"))
        kq_mid = stage("kq_var")
        tanh_s, cv_s, conv_s = stage("tanh_done"), stage("conv_in_ready"), stage("conv_tap")
        gate_s = stage("gate_ready")
        st_t, st_k = stage("state_turned"), stage("state_kept")
        ps_s, pd_s = stage("pool_sum"), stage("pool_diff")
        ln_s, lnp_s, lnsq_s, lnst_s, lnt_s = (stage(n) for n in ("ln_step", "ln_rinv", "ln_square", "ln_sums", "ln_tanh"))
        nst_t, nst_k = stage("newstate_turned"), stage("newstate_kept")
        qb_t, qb_k, kp_s, kr_s = stage("qb_done"), stage("qb_kept"), stage("page_product"), stage("page_scores")
        ib_t, ib_k, sd_s = stage("idxb_done"), stage("idxb_w_kept"), stage("sample_step")
        sit_s, slog_s, sexp_s, spt_s, spk_s, spv_s = (stage(n) for n in (
            "s_idx_turned", "s_logits", "s_exp", "s_probs_turned", "s_probs_kept", "s_pv_done"))
        S_s, ttr_s, P_s, T_s, PTk_s, PV_s, on_s, oT_s, y_s, rec_s = (stage(n) for n in (
            "scores", "scores_biased", "probs", "probs_turned", "probs_kept", "pv_done", "o_normed", "o_turned",
            "att_gated", "rowsum_inv"))
        out_s = [sem(f"kz_stored{s}") for s in range(3)]
        store_s, row_q, row_k, row_v, row_z = sem("stored"), sem("q_rows"), sem("k_rows"), sem("v_rows"), sem("z_rows")
        gt_s, ixp_s, ixr_s, ys_s = stage("gate_tanh"), stage("idxb_product"), stage("idxb_dots"), stage("sample_gated")
        lnd_s, lnk_s, lth_s = stage("ln_diag"), stage("ln_row_kept"), stage("swish_tanh")

        ev_of = {u: (evA, n + 1) for n, u in enumerate(ACT_ORDER)}
        ev_of.update({u: (evD, n + 1) for n, u in enumerate(u for u in UNITS if u[0] not in ON_ACT)})

        def wait_evac(eng, u):
            s, n = ev_of[u]
            eng.wait_ge(s.sem, n)

        def bank(u):
            return NUM[u] % 4

        def wait_unit(eng, u):
            eng.wait_ge(unit_s.sem, NUM[u] + 1)

        with nc.Fori(0, DEPTH) as layer:
            L = bass.ds(layer, 1)

            def dr(name):
                t = a[name] if name in a else o[name]
                return t[L]

            with nc.Block(no_gpsimd_drain=True) as block:
                @block.sync
                def _(sp):
                    stores = 0

                    def w_load(m):
                        g, kh = divmod(m, 2)
                        kind, c0, n = GROUPS[g]
                        if m >= W_SLOTS:
                            wait_unit(sp, LAST_UNIT[(m - W_SLOTS) // 2])
                        src = dr("w_in" if kind == "in" else "w_out").rearrange("a (k p) n -> p (a k) n", p=128)
                        sp.dma_start(W[:, m % W_SLOTS, :, 0:n], src[:, 4 * kh:4 * kh + 4, c0:c0 + n]).then_inc(w_in_s[m % W_SLOTS], 16)

                    def kv_load(n):
                        name = "cache_k" if n < 16 else "cache_v"
                        if 4 <= n < 20:
                            sp.wait_ge(kr_s.sem, n - 3)
                        elif n >= 20:
                            sp.wait_ge(spv_s.sem, n - 19)
                        src = a[name][L, bass.ds(pages[n % 16], 1)].rearrange("a b p h d -> (a b p) (h d)")
                        sp.dma_start(KV[:, n % 4, :], src).then_inc(kv_s[n % 4], 16)

                    def store(dst, src):
                        nonlocal stores
                        sp.dma_start(dst, src).then_inc(store_s, 16)
                        stores += 1

                    for m in range(4):
                        w_load(m)
                    sp.dma_start(gam[:, 0, :], dr("k_norm_g").broadcast_to([128, HD])).then_inc(gam_s, 16)
                    sp.dma_start(gam[:, 1, :], dr("q_norm_g").broadcast_to([128, HD])).then_inc(gam_s, 16)
                    w_load(4)
                    sc = dr("state_conv").rearrange("a (g b) j c -> (a g) (b j) c", g=2)
                    for g in range(2):
                        sp.dma_start(st_in[0:120, g, :], sc[g]).then_inc(state_s, 16)
                    sp.dma_start(stp_in[0:120, :], dr("state_pool").rearrange("a b j c -> (a b j) c")).then_inc(state_s, 16)
                    store(dr("new_conv_sample")[:, :, 0:CONV_STATE - 1, :], dr("state_conv")[:, :, 1:CONV_STATE, :])
                    store(dr("new_pool_sample")[:, :, 0:POOL_STATE - 1, :], dr("state_pool")[:, :, 1:POOL_STATE, :])
                    sp.wait_ge(zero_s.sem, 1)
                    for g in range(4):
                        lo = 64 * (g % 2)
                        sp.dma_start(pwb[lo:lo + 64, g // 2, lo:lo + 64], dr("pool_w")[:, g].rearrange("a i o -> (a i) o")).then_inc(pw_s, 16)
                    w_load(5)
                    w_load(6)
                    pages = [sp.value_load(table[0:1, n:n + 1], min_val=0, max_val=a["cache_k"].shape[1] - 1)
                             for n in range(N_SAMPLE * N_PAGES)]
                    for n in range(N_SAMPLE * N_PAGES):
                        sp.dma_start(kic[:, n // N_PAGES, n % N_PAGES, :],
                                     a["cache_kidx"][L, bass.ds(pages[n], 1)].rearrange("a b p d -> (a b p) d")).then_inc(kic_s, 16)
                    for n in range(4):
                        kv_load(n)
                    for i in range(NT):
                        sp.wait_ge(idxz_s.sem, i + 1)
                        store(dr("new_kidx_prompt").rearrange("a b t d -> (a b t) d")[START[i]:START[i] + ROWS[i]], zi[0:ROWS[i], i, 256:288])
                    store(dr("new_kidx_sample").rearrange("a b t d -> (a b t) d"), zi[S0:S0 + 8, 4, 256:288])
                    sp.dma_start(zis[:, :], zi[S0:S0 + 8, 4, :]).then_inc(row_z, 16)
                    w_load(7)
                    w_load(8)
                    for i in range(NT):
                        sp.wait_ge(kz_s.sem, i + 1)
                        sp.dma_start(dr("new_k_prompt").rearrange("a b t h d -> (a b t) (h d)")[START[i]:START[i] + ROWS[i]],
                                     kz[0:ROWS[i], i % 3, :]).then_inc(out_s[i % 3], 16)
                    sp.dma_start(dr("new_k_sample").rearrange("a b t h d -> (a b t) (h d)"), kz[S0:S0 + 8, 1, :]).then_inc(out_s[1], 16)
                    sp.dma_start(rows8[:, 512:1024], kz[S0:S0 + 8, 1, :]).then_inc(row_k, 16)
                    w_load(9)
                    w_load(10)
                    for i in range(NT):
                        wait_evac(sp, ("v", i, 0))
                        store(dr("new_v_prompt").rearrange("a b t h d -> (a b t) (h d)")[START[i]:START[i] + ROWS[i]], V[0:ROWS[i], i, :])
                    store(dr("new_v_sample").rearrange("a b t h d -> (a b t) (h d)"), V[S0:S0 + 8, 4, :])
                    sp.dma_start(rows8[:, 1024:1536], V[S0:S0 + 8, 4, :]).then_inc(row_v, 16)
                    w_load(11)
                    w_load(12)
                    sp.wait_ge(kz_s.sem, 2 * NT)
                    sp.dma_start(rows8[:, 0:512], kz[S0:S0 + 8, 9 % 3, :]).then_inc(row_q, 16)
                    for m in range(13, 2 * len(GROUPS)):
                        w_load(m)
                        if m == 18:
                            for n in range(4, 16):
                                kv_load(n)
                    for n in range(16, 20):
                        kv_load(n)
                    sp.wait_ge(nst_k.sem, 4)
                    new_cp = dr("new_conv_prompt").rearrange("a b j c -> (a b j) c")
                    new_pp = dr("new_pool_prompt").rearrange("a b j c -> (a b j) c")
                    store(new_cp, conv_new[0:CONV_STATE, 0:256])
                    store(dr("new_conv_sample")[:, :, CONV_STATE - 1, :].rearrange("a b c -> (a b) c"), conv_new[0:8, 256:512])
                    store(new_pp, pool_new[0:POOL_STATE, 0:256])
                    store(dr("new_pool_sample")[:, :, POOL_STATE - 1, :].rearrange("a b c -> (a b) c"), pool_new[0:8, 256:512])
                    for n in range(20, 32):
                        kv_load(n)
                    sp.wait_ge(store_s, 16 * stores)
                    for s in range(3):
                        sp.wait_ge(out_s[s], 16 * ([2, 3, 1][s]))

                @block.gpsimd
                def _(pool):
                    zero_s.did(pool.memset(pwb[:], 0.0))
                    misc0.did(pool.memset(bias[:, :, 0:SENT], BIG))
                    misc0.did(pool.memset(rel[:], 0.0))
                    misc0.did(pool.memset(uext[:, :, 0:CONV_STATE], 0.0))
                    misc0.did(pool.memset(ubx[:, :, 0:POOL_STATE], 0.0))
                    pool.wait_ge(var_s.sem, 1)
                    rinv_s.did(pool.tensor_tensor(rinv[0:SR, 0:NT], ssum[0:SR, 0:NT], pow_e[0:SR, 0:NT], ALU.pow))

                    def rotate(z, heads, hd, half, i, n, tab, tmp, s):
                        r = ROWS_P[i]
                        cos = cst[0:r, K_ROT + 48 * i + tab:K_ROT + 48 * i + tab + 2 * half].unsqueeze(1)
                        sin = cst[0:r, K_ROT + 48 * i + tab + 2 * half:K_ROT + 48 * i + tab + 4 * half].unsqueeze(1)
                        w = heads * 2 * half
                        ta = tmp[0:r, 0:w].rearrange("p (h x) -> p h x", h=heads)
                        tb = tmp[0:r, w:2 * w].rearrange("p (h x) -> p h x", h=heads)
                        s.did(pool.tensor_tensor(ta, z[:, :, 0:2 * half], cos.broadcast_to([r, heads, 2 * half]), ALU.mult))
                        s.did(pool.tensor_tensor(tb[:, :, 0:half], z[:, :, half:2 * half], sin[:, :, 0:half].broadcast_to([r, heads, half]), ALU.mult))
                        s.did(pool.tensor_tensor(tb[:, :, half:2 * half], z[:, :, 0:half], sin[:, :, half:2 * half].broadcast_to([r, heads, half]), ALU.mult))
                        pool.wait_ge(s.sem, s.n)
                        return ta, tb

                    for i in range(NT):
                        r = ROWS_P[i]
                        wait_evac(pool, ("idx", i, 0))
                        z = zi[0:r, i, 0:288].rearrange("p (h d) -> p h d", h=9)
                        if i:
                            pool.wait_ge(idxz_s.sem, i)
                        ta, tb = rotate(z, 9, ID, 4, i, 0, 32, rot_tmp, rope_s)
                        rope_s.did(pool.tensor_tensor(z[:, :, 0:8], ta, tb, ALU.add))
                        pool.wait_ge(rope_s.sem, rope_s.n)
                        idxz_s.did(pool.tensor_copy(zi[0:r, i, 288:384].rearrange("p (h d) -> p h d", h=3),
                                                    zi[0:r, i, 256:288].unsqueeze(1).broadcast_to([r, 3, ID])))

                    def kq_tile(n):
                        w, i = divmod(n, NT)
                        r = ROWS_P[i]
                        z = kz[0:r, n % 3, :].rearrange("p (h d) -> p h d", h=HEADS)
                        pool.wait_ge(kq_mid.sem, n + 1)
                        krn_s.did(pool.tensor_tensor(krn[0:r, n % 2, :], kss[0:r, n % 2, :], pow_e[0:r, :], ALU.pow))
                        pool.wait_ge(krn_s.sem, n + 1)
                        kzg_s.did(pool.tensor_tensor(z, z, krn[0:r, n % 2, :].unsqueeze(2).broadcast_to([r, HEADS, HD]), ALU.mult))
                        pool.wait_ge(kzg_s.sem, kzg_s.n)
                        kzg_s.did(pool.tensor_tensor(z, z, gam[0:r, w, :].unsqueeze(1).broadcast_to([r, HEADS, HD]), ALU.mult))
                        pool.wait_ge(kzg_s.sem, kzg_s.n)
                        ta, tb = rotate(z, HEADS, HD, 8, i, n, 0, rot_tmp, kzg_s)
                        kz_s.did(pool.tensor_tensor(z[:, :, 0:16], ta, tb, ALU.add))
                        pool.wait_ge(kz_s.sem, n + 1)

                    pool.wait_ge(gam_s, 32)
                    for n in range(2 * NT):
                        kq_tile(n)

                    pool.wait_ge(st_k.sem, 2)
                    pool.wait_ge(cv_s.sem, 4)
                    wait_evac(pool, ("ub", 1, 1))
                    n = POOL_STATE + NTOK
                    ps_s.did(pool.tensor_tensor(bufA[:, :, 1:n], ubx[:, :, 1:n], ubx[:, :, 0:n - 1], ALU.add))
                    pool.wait_ge(ps_s.sem, 1)
                    ps_s.did(pool.tensor_tensor(bufB[:, :, 3:n], bufA[:, :, 3:n], bufA[:, :, 1:n - 2], ALU.add))
                    pool.wait_ge(ps_s.sem, 2)
                    ps_s.did(pool.tensor_tensor(bufA[:, 1, 7:n], bufB[:, 1, 7:n], bufB[:, 1, 3:n - 4], ALU.add))
                    pool.wait_ge(ps_s.sem, 3)
                    ps_s.did(pool.tensor_tensor(bufB[64:128, 1, 15:n], bufA[64:128, 1, 15:n], bufA[64:128, 1, 7:n - 8], ALU.add))
                    pool.wait_ge(ps_s.sem, 4)

                    for n in range(16):
                        if n == 4:
                            pool.wait_ge(ln_s.sem, 1)
                            lnp_s.did(pool.tensor_tensor(lnr[0:SR, 0:NT], lnv[0:SR, 0:NT], pow_e[0:SR, 0:NT], ALU.pow))
                        pool.wait_ge(kv_s[n % 4], 16 * (n // 4 + 1))
                        pool.wait_ge(qb_k.sem, n // 2 + 1)
                        kp_s.did(pool.tensor_tensor(KV[:, n % 4, :], KV[:, n % 4, :], qb[:, (n // 2) % 2, :], ALU.mult))


                @block.scalar
                def _(act):
                    def copy(out, in_, scale=1.0):
                        return act.activation(out, in_, ACT.Copy, scale=scale)

                    for kc in range(KC):
                        sq_s.did(act.activation(yT[:, kc, :], xT[:, kc, :], ACT.Square))
                    act.wait_ge(st_t.sem, 1)
                    st_k.did(copy(uxs[:, :, :, 0:CONV_STATE], A[:, 0, 0:480].rearrange("p (c b j) -> p c b j", c=2, b=8)))
                    act.wait_ge(st_t.sem, 2)
                    st_k.did(copy(ubs[:, :, :, 0:POOL_STATE], A[:, 1, 0:240].rearrange("p (c b j) -> p c b j", c=2, b=8)))
                    act.wait_ge(rinv_s.sem, 1)

                    def idx_evac(i):
                        r, k = ROWS_P[i], bank(("idx", i, 0))
                        wait_unit(act, ("idx", i, 0))
                        copy(zi[0:r, i, 0:256], R[0:r, k, 0:256], rinv[0:r, i:i + 1])
                        copy(zi[0:r, i, 256:288], R[0:r, k, 264:296], rinv[0:r, i:i + 1])
                        evA.did(copy(zi[0:r, i, 384:392], R[0:r, k, 256:264], rinv[0:r, i:i + 1]))

                    for i in range(NT):
                        idx_evac(i)
                        if i == 2:
                            act.wait_ge(row_t.sem, 1)
                            row_s.did(copy(row[:, 0:START[4]], A[:, 2, 0:START[4]]))
                            row_s.did(copy(row[:, START[4]:TOK], A[:, 3, 16:16 + SR]))

                    def half_tanh(c):
                        wait_evac(act, ("conv", 2 + c, 1))
                        tanh_s.did(act.activation(bufB[:, c, 0:TOK], bufB[:, c, 0:TOK], ACT.Tanh, scale=0.5))

                    half_tanh(0)
                    for i in range(NT):
                        act.wait_ge(idxt_s.sem, i + 1)
                        idxk_s.did(copy(qkT[:, :, START[i]:START[i] + ROWS_P[i]],
                                        A[:, i % 2, 0:336].rearrange("p (c t) -> p c t", c=3)[:, :, 0:ROWS_P[i]]))
                        if i == 1:
                            half_tanh(1)

                    def kq_evac(n):
                        w, i = divmod(n, NT)
                        u, r = (("k", "q")[w], i, 0), ROWS_P[i]
                        wait_unit(act, u)
                        if n >= 3:
                            act.wait_ge(kqt_s.sem, n - 2)
                        if 3 <= n < 8:
                            act.wait_ge(out_s[n % 3], 16 * (n // 3) if n != 7 else 48)
                        if n == 7:
                            act.wait_ge(row_k, 16)
                        copy(kz[0:r, n % 3, :], R[0:r, bank(u), :], rinv[0:r, i:i + 1])
                        if n >= 2:
                            act.wait_ge(kss_s.sem, n - 1)
                        evA.did(act.activation(ksq[0:r, n % 2, :], R[0:r, bank(u), :], ACT.Square, scale=rinv[0:r, i:i + 1]))

                    def kq_keep(n):
                        i, dst = n % NT, (kT, qT)[n // NT]
                        act.wait_ge(kqt_s.sem, n + 1)
                        kqk_s.did(copy(dst[:, :, START[i]:START[i] + ROWS_P[i]],
                                       A[:, 2 + n % 2, 0:448].rearrange("p (c t) -> p c t", c=4)[:, :, 0:ROWS_P[i]]))

                    def relu(p):
                        i, h, lo, hi = PIECES[p]
                        act.wait_ge(ix_s.sem, p + 1)
                        if p >= 2:
                            act.wait_ge(acc_s.sem, p - 1 if p - 1 <= 16 else p + 1)
                        rel_s.did(act.activation(rel[0:ROWS[i], p % 2, 0:hi - lo], A[0:ROWS[i], p % 2, 0:hi - lo], ACT.Relu,
                                                 scale=1.0 / 16))

                    for n in range(4):
                        kq_evac(n)
                    act.wait_ge(misc0.sem, 2)
                    p = 0
                    for i in range(NT):
                        wait_unit(act, ("v", i, 0))
                        evA.did(copy(V[0:ROWS_P[i], i, :], R[0:ROWS_P[i], bank(("v", i, 0)), :], rinv[0:ROWS_P[i], i:i + 1]))
                        kq_keep(i)
                        if i == 0:
                            kq_evac(4)
                        for _ in range(IX_V[i]):
                            relu(p)
                            p += 1
                    for i in range(NT):
                        kq_evac(NT + i)
                        for _ in range(IX_Q[i]):
                            relu(p)
                            p += 1
                        if i >= 2:
                            kq_keep(NT + i - 2)

                    def gate_tanh(g):
                        u = GATES[g]
                        wait_evac(act, u[0])
                        if g >= 2:
                            act.wait_ge(gate_s.sem, g - 1)
                        gt_s.did(act.activation(gt[:, g % 2, :], yT[:, u[1], HALF * u[0][2]:HALF * u[0][2] + HALF], ACT.Tanh, scale=0.5))

                    for i in (3, 4):
                        kq_keep(NT + i)
                    for g in range(4):
                        gate_tanh(g)
                    act.wait_ge(nst_t.sem, 1)
                    nst_k.did(copy(conv_new[0:CONV_STATE, 0:256], A[0:CONV_STATE, 2, 0:256]))
                    nst_k.did(copy(conv_new[0:8, 256:512], A[0:8, 2, 256:512]))
                    act.wait_ge(nst_t.sem, 2)
                    nst_k.did(copy(pool_new[0:POOL_STATE, 0:256], A[0:POOL_STATE, 3, 0:256]))
                    nst_k.did(copy(pool_new[0:8, 256:512], A[0:8, 3, 256:512]))
                    for g in range(4, 8):
                        gate_tanh(g)
                    wait_evac(act, ("mean", 0, 1))
                    lnsq_s.did(act.activation(qkT[:, 0:2, :], cc[:, :, :], ACT.Square))
                    for b in range(8):
                        act.wait_ge(ib_t.sem, b + 1)
                        ib_k.did(copy(wbc[:, 8 * b:8 * b + 8], A[:, 0, 256:264]))
                        act.wait_ge(qb_t.sem, b + 1)
                        if b >= 2:
                            act.wait_ge(kp_s.sem, 2 * b - 2)
                        qb_k.did(copy(qb[:, b % 2, :], A[:, 1, :]))
                        gate_tanh(8 + b)
                        if b == 5:
                            act.wait_ge(lnt_s.sem, 1)
                            lnk_s.did(copy(lnrow[:, 0:START[4]], A[:, 2, 0:START[4]]))
                            lnk_s.did(copy(lnrow[:, START[4]:TOK], A[:, 3, 16:16 + SR]))
                    act.wait_ge(ln_s.sem, 2)
                    for c in range(2):
                        lth_s.did(act.activation(qkT[:, c, :], cc[:, c, :], ACT.Tanh, scale=prm_h[:, 4 + c:5 + c], bias=prm_h[:, 6 + c:7 + c]))

                    for n in range(len(ITEMS) + 3):
                        if n < len(ITEMS):
                            i, h = ITEMS[n]
                            r, w = ROWS[i], WIDTH[i]
                            act.wait_ge(ttr_s.sem, n + 1)
                            if n >= 2:
                                act.wait_ge(T_s.sem, n - 1)
                            if i >= 2 and h == 0:
                                act.wait_ge(rec_s.sem, i - 1)
                            P_s.did(act.activation(rel[0:r, n % 2, 0:w], bufA[0:r, n % 2, 0:w], ACT.Exp,
                                                   bias=mn[0:r, n % 2:n % 2 + 1], scale=-1.0, accum_out=rsum[0:r, i % 2, h:h + 1]))
                        if n == SX["exp"]:
                            act.wait_ge(sd_s.sem, SD["negmax"])
                            sexp_s.did(act.activation(pn[:, 0:257], R[0:64, 1, 0:257], ACT.Exp, bias=snm, scale=0.125, accum_out=srs))
                        if n == SX["keep"]:
                            act.wait_ge(spt_s.sem, 1)
                            spk_s.did(copy(pts[:, :, :], R[:, 3, 0:128].rearrange("p (g x) -> p g x", g=2)))
                            spk_s.did(copy(pd[:, :], R[0:8, 3, 128:192]))

                @block.tensor
                def _(pe):
                    def turn(out, in_, k):
                        return pe.transpose(out, in_, ident[0:k, 0:k])

                    def open_unit(u):
                        n = NUM[u]
                        if n >= 4:
                            wait_evac(pe, UNITS[n - 4])
                        return n % 4

                    def w_wait(g, kh):
                        m = 2 * g + kh
                        pe.wait_ge(w_in_s[m % W_SLOTS], 16 * (m // W_SLOTS + 1))
                        return m % W_SLOTS

                    def unit_tm(u, g, n, first=False):
                        i, k = u[1], open_unit(u)
                        r = ROWS_P[i]
                        for kc in range(KC):
                            slot = w_wait(g, kc // 4)
                            if first:
                                pe.wait_ge(xg_s.sem, kc + 1)
                            m = pe.matmul(R[0:r, k, 0:n], xg[:, kc, START[i]:START[i] + r], W[:, slot, kc % 4, 0:n],
                                          start=(kc == 0), stop=(kc == KC - 1))
                        unit_s.did(m)

                    def unit_fm(u, g, col, src):
                        k = open_unit(u)
                        for kc in range(KC):
                            slot = w_wait(g, kc // 4)
                            m = pe.matmul(R[:, k, 0:HALF], W[:, slot, kc % 4, col:col + 128], src[:, kc, HALF * u[2]:HALF * u[2] + HALF],
                                          start=(kc == 0), stop=(kc == KC - 1))
                        unit_s.did(m)

                    unit_tm(("idx", 0, 0), 0, 296, first=True)
                    pe.wait_ge(state_s, 48)
                    for c in range(2):
                        for g in range(2):
                            m = turn(A[:, 0, 240 * c + 120 * g:240 * c + 120 * g + 120], st_in[0:120, g, 128 * c:128 * c + 128], 120)
                    st_t.did(m)
                    for c in range(2):
                        m = turn(A[:, 1, 120 * c:120 * c + 120], stp_in[0:120, 128 * c:128 * c + 128], 120)
                    st_t.did(m)
                    pe.wait_ge(sq_s.sem, KC)
                    for i in range(NT):
                        for kc in range(KC):
                            m = pe.matmul(A[0:SR, 3, i:i + 1], yT[:, kc, START[i]:START[i] + SR], ones[:, 0:1],
                                          start=(kc == 0), stop=(kc == KC - 1))
                    stats_s.did(m)
                    unit_tm(("idx", 1, 0), 0, 296)
                    unit_tm(("idx", 2, 0), 0, 296)

                    def spread(src, stage):
                        for i in range(NT):
                            r = ROWS_P[i] if i == 4 else ROWS[i]
                            out = A[:, 2, START[i]:START[i] + r] if i < 4 else A[:, 3, 16:16 + r]
                            m = pe.matmul(out, ones[0:r, :], diag[0:r, i, 0:r], start=True, stop=True)
                        stage.did(m)

                    pe.wait_ge(diag_s.sem, NT)
                    spread(diag, row_t)
                    unit_tm(("idx", 3, 0), 0, 296)
                    unit_tm(("idx", 4, 0), 0, 296)
                    for m in (0, 2, 1, 3):
                        for h in range(2):
                            unit_fm(("conv", m, h), 1, 128 * m, xg)
                    for i in range(NT):
                        pe.wait_ge(idxz_s.sem, i + 1)
                        pe.wait_ge(st_k.sem, 2)
                        if i >= 2:
                            pe.wait_ge(idxk_s.sem, i - 1)
                        for j in range(3):
                            m = turn(A[:, i % 2, 112 * j:112 * j + ROWS_P[i]], zi[0:ROWS_P[i], i, 128 * j:128 * j + 128], ROWS_P[i])
                        idxt_s.did(m)
                    for i in range(NT):
                        unit_tm(("k", i, 0), 2, 512)

                    def kq_turn(n):
                        i = n % NT
                        r = ROWS_P[i]
                        pe.wait_ge(kz_s.sem, n + 1)
                        if n < 2:
                            pe.wait_ge(row_s.sem, 2)
                        else:
                            pe.wait_ge(kqk_s.sem, n - 1)
                        for j in range(4):
                            m = turn(A[:, 2 + n % 2, 112 * j:112 * j + r], kz[0:r, n % 3, 128 * j:128 * j + 128], r)
                        kqt_s.did(m)

                    def dots(p):
                        i, h, lo, hi = PIECES[p]
                        if p == 0:
                            pe.wait_ge(idxk_s.sem, NT)
                        if p >= 2:
                            pe.wait_ge(rel_s.sem, p - 1)
                        b = 32 * (h % 4)
                        ix_s.did(pe.matmul(A[0:ROWS[i], p % 2, 0:hi - lo], qkT[b:b + 32, h // 4, START[i]:START[i] + ROWS[i]],
                                           qkT[b:b + 32, 2, lo:hi], start=True, stop=True))

                    p = 0
                    for i in range(NT):
                        unit_tm(("v", i, 0), 3, 512)
                        kq_turn(i)
                        for _ in range(IX_V[i]):
                            dots(p)
                            p += 1
                    for i in range(NT):
                        unit_tm(("q", i, 0), 4, 512)
                        if i >= 2:
                            kq_turn(NT + i - 2)
                        for _ in range(IX_Q[i]):
                            dots(p)
                            p += 1
                    for m in range(4):
                        for h in range(2):
                            unit_fm(("ub", m, h), 5, 128 * m, xg)
                        if m < 2:
                            kq_turn(NT + 3 + m)
                    pe.wait_ge(kqk_s.sem, 2 * NT)
                    pe.wait_ge(cv_s.sem, 4)
                    for c in range(2):
                        turn(A[0:CONV_STATE, 2, 128 * c:128 * c + 128], uext[:, c, NTOK:NTOK + CONV_STATE], 128)
                        m = turn(A[0:8, 2, 256 + 128 * c:384 + 128 * c], uxs[:, c, :, CONV_STATE], 128)
                    nst_t.did(m)
                    for c in range(2):
                        turn(A[0:POOL_STATE, 3, 128 * c:128 * c + 128], ubx[:, c, NTOK:NTOK + POOL_STATE], 128)
                        m = turn(A[0:8, 3, 256 + 128 * c:384 + 128 * c], ubs[:, c, :, POOL_STATE], 128)
                    nst_t.did(m)
                    for m in range(2):
                        for h in range(2):
                            unit_fm(("gc", m, h), 6, 128 * m, xg)
                    pe.wait_ge(conv_s.sem, CONV_END)
                    for h in range(2):
                        k = open_unit(("mean", 0, h))
                        for c in range(2):
                            m = pe.matmul(R[:, k, 0:HALF], ones[:], cc[:, c, HALF * h:HALF * h + HALF], start=(c == 0), stop=(c == 1))
                        unit_s.did(m)
                    for b in range(8):
                        pick = ident[0:8, b:b + 1].to_broadcast([8, 128])
                        if b == 0:
                            pe.wait_ge(rel_s.sem, len(PIECES))
                            pe.wait_ge(row_z, 16)
                            pe.wait_ge(row_q, 16)
                        else:
                            pe.wait_ge(ib_k.sem, b)
                            pe.wait_ge(ixp_s.sem, b)
                        pe.matmul(A[:, 0, 0:256], pick, zis[:, 0:256], start=True, stop=True)
                        ib_t.did(pe.matmul(A[:, 0, 256:264], pick, zis[:, 384:392], start=True, stop=True))
                        if b:
                            pe.wait_ge(qb_k.sem, b)
                        qb_t.did(pe.matmul(A[:, 1, :], pick, rows8[:, 0:512], start=True, stop=True))
                        unit_fm(("ga", b // 2, b % 2), 7, 128 * (b // 2), xg)
                        if b == 1:
                            pe.wait_ge(lnsq_s.sem, 1)
                            pe.wait_ge(nst_k.sem, 4)
                            for i in range(NT):
                                for c in range(2):
                                    m = pe.matmul(A[0:SR, 3, i:i + 1], qkT[:, c, START[i]:START[i] + SR], ones[:, 0:1],
                                                  start=(c == 0), stop=(c == 1))
                            lnst_s.did(m)
                        if b == 4:
                            pe.wait_ge(lnd_s.sem, NT)
                            spread(diag, lnt_s)
                    pe.wait_ge(pd_s.sem, PD_END)
                    pe.wait_ge(pw_s, 64)
                    for m in range(2):
                        for h in range(2):
                            k = open_unit(("pool", m, h))
                            lo = POOL_STATE + HALF * h
                            unit_s.did(pe.matmul(R[:, k, 0:HALF], pwb[:, m, :], bufA[:, m, lo:lo + HALF], start=True, stop=True))
                    pe.wait_ge(sd_s.sem, SD["isc"])
                    pe.wait_ge(lnk_s.sem, 2)
                    for g in range(2):
                        m = turn(A[0:8, 2, 128 * g:128 * g + 128], isc[:, 8 * g:8 * g + 8], 128)
                    sit_s.did(m)

                    def scores(n):
                        i, h = ITEMS[n]
                        r, w, b, k = ROWS[i], WIDTH[i], 64 * (h % 2), 2 * (n % 2)
                        if n == 0:
                            wait_evac(pe, ("pool", 1, 1))
                            pe.wait_ge(kqk_s.sem, 2 * NT)
                        if n >= 2:
                            pe.wait_ge(ttr_s.sem, n - 1)
                        lhs = qT[b:b + 64, h // 2, START[i]:START[i] + r]
                        m = pe.matmul(R[0:r, k, 0:min(w, 512)], lhs, kT[b:b + 64, h // 2, 0:min(w, 512)], start=True, stop=True)
                        if w > 512:
                            m = pe.matmul(R[0:r, k + 1, 0:w - 512], lhs, kT[b:b + 64, h // 2, 512:w], start=True, stop=True)
                        S_s.did(m)

                    def turn_probs(n):
                        i, h = ITEMS[n]
                        pe.wait_ge(P_s.sem, n + 1)
                        if n >= 2:
                            pe.wait_ge(PTk_s.sem, n - 1)
                        for j in range(i + 1):
                            m = turn(A[0:MAXR, n % 2, ROWS[i] * j:ROWS[i] * (j + 1)], rel[0:ROWS[i], n % 2, START[j]:START[j] + MAXR], ROWS[i])
                        T_s.did(m)

                    def weigh(n):
                        i, h = ITEMS[n]
                        pe.wait_ge(PTk_s.sem, n + 1)
                        if h == 0 and i:
                            pe.wait_ge(on_s.sem, i)
                        pt = bufB[:, n % 2, 0:NT * MAXR].rearrange("p (j t) -> p j t", j=NT)
                        for j in range(i + 1):
                            m = pe.matmul(A[0:ROWS[i], 2, HD * h:HD * h + HD], pt[0:ROWS[j], j, 0:ROWS[i]],
                                          V[0:ROWS[j], j, HD * h:HD * h + HD], start=(j == 0), stop=(j == i))
                        PV_s.did(m)

                    def turn_out(i):
                        pe.wait_ge(on_s.sem, i + 1)
                        if i:
                            pe.wait_ge(y_s.sem, i)
                        for c in range(4):
                            m = turn(A[:, 3, MAXR * c:MAXR * c + ROWS[i]], ksq[0:ROWS[i], 0, 128 * c:128 * c + 128], ROWS[i])
                        oT_s.did(m)

                    for n in range(len(ITEMS) + 5):
                        if n < len(ITEMS):
                            scores(n)
                        if 2 <= n < len(ITEMS) + 2:
                            turn_probs(n - 2)
                        if 3 <= n < len(ITEMS) + 3:
                            weigh(n - 3)
                        if n >= 12 and (n - 12) % 8 == 0:
                            turn_out((n - 12) // 8)
                        if n == SX["logits"]:
                            pe.wait_ge(sd_s.sem, SD["logit_in"])
                            pe.wait_ge(kr_s.sem, 16)
                            out = R[0:64, 1, :]
                            pe.matmul(out[:, 0:257], E8, sc8[:, 0:257], start=True, stop=False)
                            for g in range(2):
                                pe.matmul(out[:, 128 * g:128 * g + 128], ssm[:, g, :], ident, start=False, stop=False)
                            slog_s.did(pe.matmul(out[:, 256:257], sn, ones[0:8, 0:1], start=False, stop=True))
                        if n == SX["turn"]:
                            pe.wait_ge(sd_s.sem, SD["etp"])
                            for g in range(2):
                                turn(R[:, 3, 64 * g:64 * g + 64], pn[:, 128 * g:128 * g + 128], 64)
                            spt_s.did(pe.matmul(R[0:8, 3, 128:192], etp, ident[0:64, 0:64], start=True, stop=True))
                        if SX["pv"] <= n < SX["pv"] + 8:
                            acc = R[:, 1, 0:64]
                            if n == SX["pv"]:
                                pe.wait_ge(spk_s.sem, 2)
                                pe.wait_ge(row_v, 16)
                                for c in range(4):
                                    new = pd[:, :].rearrange("p (b h) -> p b h", b=8)[:, :, 2 * c:2 * c + 2]
                                    pe.matmul(acc[:, 16 * c:16 * c + 16], rows8[:, 1024 + 128 * c:1152 + 128 * c], new,
                                              start=(c == 0), stop=False, skip_group_check=True)
                            b = n - SX["pv"]
                            for g in range(2):
                                page = 16 + 2 * b + g
                                pe.wait_ge(kv_s[page % 4], 16 * (page // 4 + 1))
                                for c in range(4):
                                    m = pe.matmul(acc[:, 16 * c + 2 * b:16 * c + 2 * b + 2], KV[:, page % 4, 128 * c:128 * c + 128],
                                                  pts[:, g, 8 * b + 2 * c:8 * b + 2 * c + 2], start=False,
                                                  stop=(page == 31 and c == 3), skip_group_check=True)
                                spv_s.did(m)
                    for m in range(KC):
                        for h in range(2):
                            if m == 0 and h == 0:
                                pe.wait_ge(y_s.sem, NT)
                                pe.wait_ge(ys_s.sem, 2)
                                pe.wait_ge(ln_s.sem, LN_END)
                            unit_fm(("out", m, h), 8 + m // 4, 128 * (m % 4), yT)

                @block.vector
                def _(dve):
                    def stt(out, a0, s, a1, op0=ALU.mult, op1=ALU.mult):
                        return dve.scalar_tensor_tensor(out=out, in0=a0, scalar=s, in1=a1, op0=op0, op1=op1)

                    prm_s.did(dve.tensor_copy(prm[:, :], params[:, L, :].rearrange("p a n -> p (a n)")))
                    dve.wait_ge(prm_s.sem, 1)
                    for kc in range(KC):
                        xg_s.did(dve.tensor_scalar(xg[:, kc, :], xT[:, kc, :], prm[:, kc:kc + 1], None, ALU.mult))
                    prm_s.did(dve.tensor_scalar(prm_h[:, :], prm[:, 8:16], 0.5, None, ALU.mult))
                    dve.wait_ge(stats_s.sem, 1)
                    var_s.did(dve.tensor_scalar(ssum[0:SR, 0:NT], A[0:SR, 3, 0:NT], 1.0 / D_MODEL, EPS, ALU.mult, ALU.add))
                    dve.wait_ge(rinv_s.sem, 1)
                    for i in range(NT):
                        r = ROWS_P[i]
                        diag_s.did(dve.tensor_scalar(diag[0:r, i, 0:r], ident[0:r, 0:r], rinv[0:r, i:i + 1], None, ALU.mult))
                    dve.wait_ge(row_s.sem, 2)
                    dve.wait_ge(st_t.sem, 2)
                    dve.wait_ge(misc0.sem, 4)
                    dve.wait_ge(st_k.sem, 2)

                    def tok(h):
                        return slice(HALF * h, HALF * h + HALF)

                    def conv_in(c):
                        dve.wait_ge(tanh_s.sem, c + 1)
                        cv_s.did(stt(uext[:, c, CONV_STATE:CONV_STATE + NTOK], bufB[:, c, 0:NTOK], 1.0, bufA[:, c, 0:NTOK], ALU.add))
                        cv_s.did(stt(uxs[:, c, :, CONV_STATE], bufB[:, c, NTOK:TOK], 1.0, bufA[:, c, NTOK:TOK], ALU.add))

                    for m in (0, 2, 1, 3):
                        for h in range(2):
                            u = ("conv", m, h)
                            wait_unit(dve, u)
                            src = R[:, bank(u), 0:HALF]
                            if m < 2:
                                evD.did(stt(bufA[:, m, tok(h)], src, 0.5, row[:, tok(h)]))
                            else:
                                evD.did(dve.tensor_tensor(bufB[:, m - 2, tok(h)], src, row[:, tok(h)], ALU.mult))
                        if m == 1:
                            conv_in(0)
                    conv_in(1)

                    def kq_sum(n):
                        w, i = divmod(n, NT)
                        r = ROWS_P[i]
                        wait_evac(dve, (("k", "q")[w], i, 0))
                        if n >= 2:
                            dve.wait_ge(krn_s.sem, n - 1)
                        kss_s.did(dve.reduce_sum(kss[0:r, n % 2, :], ksq[0:r, n % 2, :].rearrange("p (h d) -> p h d", h=HEADS), AX.X))
                        dve.wait_ge(kss_s.sem, n + 1)
                        kq_mid.did(dve.tensor_scalar(kss[0:r, n % 2, :], kss[0:r, n % 2, :], 1.0 / HD, EPS, ALU.mult, ALU.add))

                    dve.wait_ge(cv_s.sem, 4)
                    for j in range(CONV_W):
                        for c in range(2):
                            w = prm[:, 16 + CONV_W * c + j:17 + CONV_W * c + j]
                            if j == 0:
                                conv_s.did(dve.tensor_scalar(cc[:, c, 0:NTOK], uext[:, c, 0:NTOK], w, prm[:, 10 + c:11 + c], ALU.mult, ALU.add))
                            else:
                                dve.wait_ge(conv_s.sem, 2 * j + c - 1)
                                conv_s.did(stt(cc[:, c, 0:NTOK], uext[:, c, j:j + NTOK], w, cc[:, c, 0:NTOK], ALU.mult, ALU.add))
                        if j >= 6 and (j - 6) % 6 == 0:
                            kq_sum((j - 6) // 6)
                    for c in range(2):
                        taps = prm[:, 16 + CONV_W * c:16 + CONV_W * (c + 1)].unsqueeze(1).broadcast_to([128, N_SAMPLE, CONV_W])
                        tmp = gt[:, c, 0:N_SAMPLE * CONV_W].rearrange("p (b j) -> p b j", b=N_SAMPLE)
                        conv_s.did(dve.tensor_tensor(tmp, uxs[:, c, :, :], taps, ALU.mult))
                    for c in range(2):
                        tmp = gt[:, c, 0:N_SAMPLE * CONV_W].rearrange("p (b j) -> p b j", b=N_SAMPLE)
                        dve.wait_ge(conv_s.sem, 2 * CONV_W + 1 + c)
                        conv_s.did(dve.reduce_sum(wsum[:, c, :], tmp, AX.X))
                    for c in range(2):
                        dve.wait_ge(conv_s.sem, 2 * CONV_W + 3 + c)
                        conv_s.did(dve.tensor_scalar(cc[:, c, NTOK:TOK], wsum[:, c, :], prm[:, 10 + c:11 + c], None, ALU.add))

                    def area(i, lo=0, hi=None):
                        hi = SENT + WIDTH[i] if hi is None else hi
                        return bias[0:ROWS[i], i - 1, lo:hi]

                    last = {}

                    def gather(p):
                        i, h, lo, hi = PIECES[p]
                        dve.wait_ge(rel_s.sem, p + 1)
                        dst = area(i, SENT + lo, SENT + hi)
                        w = zi[0:ROWS[i], i, 384 + h:385 + h]
                        src = rel[0:ROWS[i], p % 2, 0:hi - lo]
                        if h == 0:
                            acc_s.did(dve.tensor_scalar(dst, src, w, None, ALU.mult))
                        else:
                            dve.wait_ge(acc_s.sem, last[i, lo])
                            acc_s.did(stt(dst, src, w, dst, ALU.mult, ALU.add))
                        last[i, lo] = acc_s.n

                    def causal(i, s):
                        d = area(i, SENT + START[i], SENT + WIDTH[i])
                        s.did(dve.tensor_tensor(d, d, tri[0:ROWS[i], 0:ROWS[i]], ALU.add))

                    def topk_round(pair):
                        for x, i in enumerate(pair):
                            dve.wait_ge(tk_s.sem, tk_s.n - 1) if tk_s.n > 1 else None
                            tk_s.did(dve.max(m8[0:ROWS[i], x, :], area(i)))
                        for x, i in enumerate(pair):
                            dve.wait_ge(tk_s.sem, tk_s.n - 1)
                            tk_s.did(dve.match_replace(area(i), m8[0:ROWS[i], x, :], area(i), GONE))

                    def to_bias(pair):
                        for i in pair:
                            dve.wait_ge(tk_s.sem, tk_s.n)
                            tk_s.did(dve.tensor_scalar(area(i), area(i), CUT, NEG, ALU.is_gt, ALU.mult))
                        for i in pair:
                            dve.wait_ge(tk_s.sem, tk_s.n)
                            causal(i, tk_s)

                    n1 = sum(1 for q in PIECES if q[0] <= 2)
                    for p in range(n1):
                        gather(p)
                    dve.wait_ge(acc_s.sem, acc_s.n)
                    for i in (1, 2):
                        causal(i, acc_s)
                    dve.wait_ge(acc_s.sem, acc_s.n)
                    done = 0
                    for p in range(n1, len(PIECES)):
                        gather(p)
                        if done < ROUNDS and (p - n1) % 4 != 3:
                            topk_round((1, 2))
                            done += 1
                        if (p - n1) % 5 == 4:
                            kq_sum(NT + (p - n1) // 5)
                    kq_sum(2 * NT - 1)
                    while done < ROUNDS:
                        topk_round((1, 2))
                        done += 1
                    to_bias((1, 2))
                    dve.wait_ge(acc_s.sem, acc_s.n)
                    for i in (3, 4):
                        causal(i, acc_s)
                    dve.wait_ge(acc_s.sem, acc_s.n)

                    rounds = [0]

                    def more_topk():
                        if rounds[0] < ROUNDS:
                            topk_round((3, 4))
                            rounds[0] += 1

                    def gate(g):
                        u = GATES[g]
                        dve.wait_ge(gt_s.sem, g + 1)
                        dst = yT[:, u[1], tok(u[0][2])]
                        gate_s.did(stt(dst, gt[:, g % 2, :], 1.0, dst, ALU.add))

                    def gate_in(u, ch):
                        wait_unit(dve, u)
                        evD.did(dve.tensor_tensor(yT[:, ch, tok(u[2])], R[:, bank(u), 0:HALF], row[:, tok(u[2])], ALU.mult))

                    g = 0
                    for m in range(4):
                        for h in range(2):
                            u = ("ub", m, h)
                            if m >= 2:
                                gate_in(u, 4 + m - 2)
                                if g:
                                    gate(g - 1)
                                g += 1
                            else:
                                wait_unit(dve, u)
                                src = R[:, bank(u), 0:HALF]
                                if h == 0:
                                    evD.did(dve.tensor_tensor(ubx[:, m, POOL_STATE:POOL_STATE + HALF], src, row[:, tok(0)], ALU.mult))
                                else:
                                    n = NTOK - HALF
                                    dve.tensor_tensor(ubx[:, m, POOL_STATE + HALF:POOL_STATE + NTOK], src[:, 0:n], row[:, HALF:NTOK], ALU.mult)
                                    evD.did(dve.tensor_tensor(ubs[:, m, :, POOL_STATE], src[:, n:HALF], row[:, NTOK:TOK], ALU.mult))
                            more_topk()
                    for m in range(2):
                        for h in range(2):
                            gate_in(("gc", m, h), 6 + m)
                            gate(g - 1)
                            g += 1
                            more_topk()
                    for h in range(2):
                        u = ("mean", 0, h)
                        wait_unit(dve, u)
                        dve.wait_ge(conv_s.sem, conv_s.n)
                        evD.did(stt(cc[:, :, tok(h)], R[:, bank(u), 0:HALF].unsqueeze(1).broadcast_to([128, 2, HALF]), -1.0 / D_C,
                                    cc[:, :, tok(h)], ALU.mult, ALU.add))
                    dve.wait_ge(ps_s.sem, 4)
                    first = slice(POOL_STATE, 2 * POOL_STATE)
                    rest = slice(2 * POOL_STATE, POOL_STATE + NTOK)
                    for half, src in ((slice(0, 64), bufA), (slice(64, 128), bufB)):
                        cnt = cst[half, K_CNT:K_CNT + 32].rearrange("p (c t) -> p c t", c=2)[:, :, 0:POOL_STATE]
                        pd_s.did(dve.tensor_tensor(bufA[half, :, first], src[half, :, first], cnt, ALU.mult))
                        for c in range(2):
                            pd_s.did(stt(bufA[half, c, rest], src[half, c, rest], cst[half, K_WIN + c:K_WIN + c + 1],
                                         ubx[half, c, rest], ALU.mult, ALU.subtract))
                        dve.wait_ge(pd_s.sem, pd_s.n - 2)
                        pd_s.did(dve.tensor_tensor(bufA[half, :, first], bufA[half, :, first], ubx[half, :, first], ALU.subtract))
                    for c in range(2):
                        for k in range(2):
                            rows = slice(64 * k, 64 * k + 64)
                            win = WINDOWS[2 * c + k]
                            pd_s.did(dve.reduce_sum(wsum[rows, c, :], ubs[rows, c, :, 16 - win:16], AX.X))
                    dve.wait_ge(pd_s.sem, pd_s.n)
                    for c in range(2):
                        pd_s.did(stt(bufA[:, c, POOL_STATE + NTOK:POOL_STATE + TOK], wsum[:, c, :], cst[:, K_WIN + c:K_WIN + c + 1],
                                     ubs[:, c, :, POOL_STATE], ALU.mult, ALU.subtract))
                    assert pd_s.n == PD_END

                    def page_scores(n):
                        dve.wait_ge(kp_s.sem, n + 1)
                        b, pg = divmod(n, 2)
                        kr_s.did(dve.reduce_sum(ssm[:, pg, 8 * b:8 * b + 8], KV[:, n % 4, :].rearrange("p (h d) -> p h d", h=HEADS), AX.X))

                    dve.wait_ge(kic_s, 256)
                    for b in range(8):
                        gate_in(("ga", b // 2, b % 2), b // 2)
                        gate(g - 1)
                        g += 1
                        dve.wait_ge(ib_k.sem, b + 1)
                        if b:
                            dve.wait_ge(ixr_s.sem, b)
                        prod = ixp[:, :].rearrange("p (g h d) -> p g h d", g=2, h=IH)
                        ixp_s.did(dve.tensor_tensor(prod, kic[:, b, :, :].unsqueeze(2).broadcast_to([128, 2, IH, ID]),
                                                    A[:, 0, 0:256].rearrange("p (h d) -> p h d", h=IH).unsqueeze(1).broadcast_to([128, 2, IH, ID]),
                                                    ALU.mult))
                        dve.wait_ge(ixp_s.sem, b + 1)
                        ixr_s.did(dve.reduce_sum(ds[:, :, b, :], prod, AX.X))
                        if b:
                            page_scores(2 * b - 2)
                            page_scores(2 * b - 1)
                        more_topk()
                        if b == 2:
                            dve.wait_ge(lnst_s.sem, 1)
                            ln_s.did(dve.tensor_scalar(lnv[0:SR, 0:NT], A[0:SR, 3, 0:NT], 1.0 / D_C, EPS, ALU.mult, ALU.add))
                        if b == 4:
                            dve.wait_ge(lnp_s.sem, 1)
                            for i in range(NT):
                                r = ROWS_P[i]
                                lnd_s.did(dve.tensor_scalar(diag[0:r, i, 0:r], ident[0:r, 0:r], lnr[0:r, i:i + 1], None, ALU.mult))
                    gate(g - 1)
                    page_scores(14)
                    page_scores(15)
                    while rounds[0] < ROUNDS:
                        more_topk()
                    to_bias((3, 4))
                    dve.wait_ge(lnk_s.sem, 2)
                    ln_s.did(dve.tensor_tensor(cc[:, :, :], cc[:, :, :], lnrow.unsqueeze(1).broadcast_to([128, 2, TOK]), ALU.mult))
                    for m in range(2):
                        for h in range(2):
                            u = ("pool", m, h)
                            wait_unit(dve, u)
                            dst = yT[:, 4 + m, tok(h)]
                            evD.did(stt(dst, R[:, bank(u), 0:HALF], prm_h[:, m:m + 1], dst))
                    for c in range(2):
                        dve.wait_ge(lth_s.sem, c + 1)
                        ln_s.did(dve.tensor_scalar(cc[:, c, :], cc[:, c, :], prm[:, 12 + c:13 + c], prm[:, 14 + c:15 + c], ALU.mult, ALU.add))
                        dve.wait_ge(ln_s.sem, ln_s.n)
                        ln_s.did(stt(qkT[:, c, :], qkT[:, c, :], 1.0, cc[:, c, :], ALU.add))
                        dve.wait_ge(ln_s.sem, ln_s.n)
                        ln_s.did(stt(yT[:, 6 + c, :], qkT[:, c, :], 0.25, yT[:, 6 + c, :]))
                    assert ln_s.n == LN_END

                    def sd(ins, name=None):
                        sd_s.did(ins)
                        dve.wait_ge(sd_s.sem, sd_s.n)
                        if name:
                            assert SD[name] == sd_s.n, (name, sd_s.n)

                    dve.wait_ge(ixr_s.sem, 8)
                    flat = smp[:, 0:128].rearrange("p (g x) -> p g x", g=2)
                    sd(stt(flat, flat, 0.0, wbc.unsqueeze(1).broadcast_to([128, 2, 64]), ALU.max))
                    sd(dve.reduce_sum(isc.rearrange("p (g b) -> p g b", g=2), ds[:, :, :, :], AX.X))
                    sd(dve.tensor_scalar(isc, isc, 1.0 / 16, None, ALU.mult), "isc")
                    t8 = ixp[0:8, :].rearrange("p (h d) -> p h d", h=8)
                    dve.wait_ge(row_z, 16)
                    sd(dve.tensor_tensor(t8[:, :, 0:ID], zis[:, 0:256].rearrange("p (h d) -> p h d", h=IH),
                                         zis[:, 256:288].unsqueeze(1).broadcast_to([8, IH, ID]), ALU.mult))
                    sd(dve.reduce_sum(d8, t8[:, :, 0:ID], AX.X))
                    sd(stt(e8, d8, 0.0, zis[:, 384:392], ALU.max))
                    sd(dve.reduce_sum(sc8[:, 256:257], e8, AX.X))
                    sd(dve.tensor_scalar(sc8[:, 256:257], sc8[:, 256:257], 1.0 / 16, None, ALU.mult))
                    dve.wait_ge(row_q, 16)
                    dve.wait_ge(row_k, 16)
                    sd(dve.tensor_tensor(t8, rows8[:, 0:512].rearrange("p (h d) -> p h d", h=8),
                                         rows8[:, 512:1024].rearrange("p (h d) -> p h d", h=8), ALU.mult))
                    sd(dve.reduce_sum(snw, t8, AX.X))
                    sd(dve.tensor_tensor(sn.rearrange("p (b h) -> p b h", b=8), E8.rearrange("p (b h) -> p b h", b=8),
                                         snw.unsqueeze(1).broadcast_to([8, 8, 8]), ALU.mult))
                    dve.wait_ge(sit_s.sem, 1)
                    sd(dve.tensor_copy(sc8[:, 0:256], A[0:8, 2, 0:256]))
                    for _ in range(TOPK_S // 8):
                        sd(dve.max(m8s, sc8[:, 0:PAST + 1]))
                        sd(dve.match_replace(sc8[:, 0:PAST + 1], m8s, sc8[:, 0:PAST + 1], GONE))
                    sd(dve.tensor_scalar(sc8[:, 0:PAST + 1], sc8[:, 0:PAST + 1], CUT, NEG, ALU.is_gt, ALU.mult), "logit_in")

                    Rf = R[:, :, :].rearrange("p k n -> p (k n)")
                    for n in range(len(ITEMS) + 6):
                        if n < len(ITEMS):
                            i, h = ITEMS[n]
                            r, w = ROWS[i], WIDTH[i]
                            dve.wait_ge(S_s.sem, n + 1)
                            if n >= 2:
                                dve.wait_ge(P_s.sem, n - 1)
                            b = tri[0:r, 0:r] if i == 0 else bias[0:r, i - 1, SENT:SENT + w]
                            ttr_s.did(dve.tensor_tensor_reduce(out=bufA[0:r, n % 2, 0:w], in0=Rf[0:r, 1024 * (n % 2):1024 * (n % 2) + w], in1=b,
                                                               scale=-0.125, scalar=BIG, op0=ALU.add, op1=ALU.min,
                                                               accum_out=mn[0:r, n % 2:n % 2 + 1]))
                        if 2 <= n < len(ITEMS) + 2:
                            m = n - 2
                            i, h = ITEMS[m]
                            dve.wait_ge(T_s.sem, m + 1)
                            if m >= 2:
                                dve.wait_ge(PV_s.sem, m - 1)
                            dst = bufB[0:MAXR, m % 2, 0:NT * MAXR].rearrange("p (j t) -> p j t", j=NT)[:, 0:i + 1, 0:ROWS[i]]
                            PTk_s.did(dve.tensor_copy(dst, A[0:MAXR, m % 2, 0:(i + 1) * ROWS[i]].rearrange("p (j t) -> p j t", j=i + 1)))
                        if n >= 11 and (n - 11) % 8 == 0:
                            i = (n - 11) // 8
                            r = ROWS[i]
                            dve.wait_ge(PV_s.sem, 8 * i + 8)
                            rec_s.did(dve.reciprocal(rrec[0:r, :], rsum[0:r, i % 2, :]))
                            dve.wait_ge(rec_s.sem, i + 1)
                            if i:
                                dve.wait_ge(oT_s.sem, i)
                            on_s.did(dve.tensor_tensor(ksq[0:r, 0, :].rearrange("p (h d) -> p h d", h=HEADS),
                                                       A[0:r, 2, :].rearrange("p (h d) -> p h d", h=HEADS),
                                                       rrec[0:r, :].unsqueeze(2).broadcast_to([r, HEADS, HD]), ALU.mult))
                        if n >= 13 and (n - 13) % 8 == 0:
                            i = (n - 13) // 8
                            dve.wait_ge(oT_s.sem, i + 1)
                            dst = yT[:, 0:4, START[i]:START[i] + ROWS[i]]
                            src = A[:, 3, 0:4 * MAXR].rearrange("p (c t) -> p c t", c=4)[:, :, 0:ROWS[i]]
                            y_s.did(stt(dst, src, 0.5, dst))
                        if n == SX["max"]:
                            dve.wait_ge(slog_s.sem, 1)
                            sd(dve.reduce_max(smx, R[0:64, 1, 0:257], AX.X))
                            sd(dve.tensor_scalar(snm, smx, -0.125, None, ALU.mult), "negmax")
                        if n == SX["norm"]:
                            dve.wait_ge(sexp_s.sem, 1)
                            sd(dve.reciprocal(srr, srs))
                            sd(dve.tensor_scalar(pn[:, 0:257], pn[:, 0:257], srr, None, ALU.mult))
                            sd(dve.tensor_scalar(etp, ET8, pn[:, 256:257], None, ALU.mult), "etp")
                        if n == SX["gate"]:
                            dve.wait_ge(spv_s.sem, 16)
                            for k in range(2):
                                rows = slice(64 * k, 64 * k + 64)
                                dst = yT[rows, 0:4, NTOK:TOK]
                                src = R[rows, 1, 0:64].rearrange("p (c b k) -> p c b k", c=4, b=8)[:, :, :, k]
                                ys_s.did(stt(dst, src, 0.5, dst))
                    for m in range(KC):
                        for h in range(2):
                            u = ("out", m, h)
                            wait_unit(dve, u)
                            evD.did(dve.tensor_tensor(xT[:, m, tok(h)], R[:, bank(u), 0:HALF], xT[:, m, tok(h)], ALU.add))

            for s in layer_sems:
                nc.gpsimd.sem_clear(s)
            nc.all_engine_barrier()

        with nc.Block() as block:
            spans = [(N_META + 128 * i, 128) for i in range(4)] + [(NTOK, N_SAMPLE)]

            @block.tensor
            def _(pe):
                n = 0
                for i, (c0, r) in enumerate(spans):
                    for g in range(2):
                        if n >= 4:
                            pe.wait_ge(pre["post_act"] if n % 2 else pre["post_dve"], (n - 4) // 2 + 1)
                        for j in range(4):
                            m = pe.transpose(R[0:r, n % 4, 128 * j:128 * j + 128], xT[:, 4 * g + j, c0:c0 + r], ident)
                        m.then_inc(pre["post_turned"], 1)
                        n += 1

            @block.vector
            def _(dve):
                for i, (c0, r) in enumerate(spans):
                    dve.wait_ge(pre["post_turned"], 2 * i + 1)
                    dve.tensor_copy(yout[0:r, i, 0:512], R[0:r, (2 * i) % 4, :]).then_inc(pre["post_dve"], 1)

            @block.scalar
            def _(act):
                for i, (c0, r) in enumerate(spans):
                    act.wait_ge(pre["post_turned"], 2 * i + 2)
                    act.activation(yout[0:r, i, 512:1024], R[0:r, (2 * i + 1) % 4, :], ACT.Copy).then_inc(pre["post_act"], 1)

            @block.sync
            def _(sp):
                for i, (c0, r) in enumerate(spans):
                    sp.wait_ge(pre["post_dve"], i + 1)
                    sp.wait_ge(pre["post_act"], i + 1)
                    dst = (o["y_prompt"].rearrange("b t d -> (b t) d")[128 * i:128 * i + 128] if i < 4
                           else o["y_sample"].rearrange("b t d -> (b t) d"))
                    sp.dma_start(dst, yout[0:r, i, :]).then_inc(pre["post_out"], 16)
                sp.wait_ge(pre["post_out"], 16 * len(spans))


_INS = ["x_prompt", "x_sample", "cache_k", "cache_v", "cache_kidx", "state_pool", "state_conv", "page_table",
        "meta_tokens", "norm_g", "w_in", "q_norm_g", "k_norm_g", "pool_w", "pool_scale", "conv_w", "conv_b",
        "conv_norm_g", "conv_norm_b", "w_out"]
_OUTS = [("y_prompt", (1, SEQ, D_MODEL)), ("y_sample", (N_SAMPLE, 1, D_MODEL)),
         ("new_k_prompt", (DEPTH, 1, NTOK, HEADS, HD)), ("new_v_prompt", (DEPTH, 1, NTOK, HEADS, HD)),
         ("new_kidx_prompt", (DEPTH, 1, NTOK, ID)), ("new_pool_prompt", (DEPTH, 1, POOL_STATE, D_B)),
         ("new_conv_prompt", (DEPTH, 1, CONV_STATE, D_C)), ("new_k_sample", (DEPTH, N_SAMPLE, 1, HEADS, HD)),
         ("new_v_sample", (DEPTH, N_SAMPLE, 1, HEADS, HD)), ("new_kidx_sample", (DEPTH, N_SAMPLE, 1, ID)),
         ("new_pool_sample", (DEPTH, N_SAMPLE, POOL_STATE, D_B)), ("new_conv_sample", (DEPTH, N_SAMPLE, CONV_STATE, D_C))]


def kernel(**inputs):
    import concourse.bacc as bacc
    from concourse.bass_utils import run_bass_kernel_spmd

    nc = bacc.Bacc("TRN2", target_bir_lowering=False, num_devices=1)
    arrays, a, o = {}, {}, {}
    given = {name: np.ascontiguousarray(inputs[name]) for name in _INS}
    given["consts"] = constants()
    for name, x in given.items():
        arrays[f"in_{name}"] = x
        a[name] = nc.dram_tensor(f"in_{name}", x.shape, mybir.dt.from_np(x.dtype), kind="ExternalInput").ap()
    for name, shape in _OUTS:
        o[name] = nc.dram_tensor(f"out_{name}", shape, F32, kind="ExternalOutput").ap()
    program(nc, a, o)
    r = run_bass_kernel_spmd(nc, [arrays], core_ids=[0])
    return tuple(r.results[0][f"out_{name}"] for name, _ in _OUTS)
```

```python
from contextlib import ExitStack

import numpy as np

import concourse.bass as bass
from concourse import mybir

F32 = mybir.dt.float32
I32 = mybir.dt.int32
ALU = mybir.AluOpType
ACT = mybir.ActivationFunctionType
AX = mybir.AxisListType

D_MODEL, SEQ, N_META, DEPTH = 1024, 512, 16, 2
N_SAMPLE, PAST, PAGE = 8, 256, 128
N_PAGES = PAST // PAGE
HEADS, HD = 8, 64
IH, ID = 8, 32
TOPK_P, TOPK_S = 132, 64
THETA = 500000.0
EPS = 1e-6
WINDOWS = (2, 4, 8, 16)
POOL_STATE, CONV_STATE, CONV_W = 15, 30, 31
D_B = D_C = 256

NTOK = SEQ + N_META
TOK = NTOK + N_SAMPLE
HALF = TOK // 2
KC = D_MODEL // 128
START = [0, 107, 214, 320, 426]
ROWS = [107, 107, 106, 106, 102]
NT = len(START)
ROWS_P = ROWS[:4] + [ROWS[4] + N_SAMPLE]
S0 = ROWS[4]
MAXR = 107
SR = 110
WIDTH = [START[i] + ROWS[i] for i in range(NT)]
SENT = (-TOPK_P) % 8
ROUNDS = (TOPK_P + SENT) // 8
NEG, GONE, CUT, BIG = -1e30, -3e38, -2e38, 3e38

C_Q, C_K, C_V, C_GA, C_I, C_UB, C_GB, C_CV, C_GC = 0, 512, 1024, 1536, 2048, 2344, 2600, 2856, 3368
GROUPS = [("in", C_I, 296), ("in", C_CV, 512), ("in", C_K, 512), ("in", C_Q, 512), ("in", C_V, 512),
          ("in", C_UB, 512), ("in", C_GC, 256), ("in", C_GA, 512), ("out", 0, 512), ("out", 512, 512)]
W_SLOTS = 5

PIPE = 5


def plan():
    fill = [("ub", m, h) for m in (0, 1) for h in range(2)] + [("mean", 0, 0), ("mean", 0, 1), ("ub", 2, 0), ("ub", 2, 1),
            ("lnsum", 0, 0), ("ub", 3, 0), ("ub", 3, 1), ("gc", 0, 0), ("lnrow", 0, 0), ("lnrow", 0, 1), ("gc", 0, 1),
            ("gc", 1, 0), ("gc", 1, 1)] + [("ga", m, h) for m in range(4) for h in range(2)]
    steps = [[] for _ in range(NT * HEADS + PIPE)]
    free = [n for n in range(30) if n < 8 or n % 4 != 3]
    for n, u in zip(free, fill):
        steps[n].append(u)
    assert len(free) >= len(fill)
    steps[30] += [("pool", m, h) for m in range(2) for h in range(2)]
    for m in range(KC):
        steps[32 + m].append(("out", m, 0))
    for i in range(NT):
        steps[8 * i + 12].append(("turn", i, 0))
    return steps


PLAN = plan()
EARLY = ([("idx", i, 0) for i in range(NT)]
         + [("conv", m, h) for m in (0, 2, 1, 3) for h in range(2)]
         + [(n, i, 0) for n in ("k", "q", "v") for i in range(NT)])
UNITS = EARLY + [u for step in PLAN for u in step] + [("out", m, 1) for m in range(KC)]
NUM = {u: n for n, u in enumerate(UNITS)}
ON_ACT = ("idx", "k", "v", "q", "lnrow", "turn")
LAST_UNIT = [("idx", 4, 0), ("conv", 3, 1), ("k", 4, 0), ("q", 4, 0), ("v", 4, 0), ("ub", 3, 1),
             ("gc", 1, 1), ("ga", 3, 1)]

PIECES = [(i, h, a, b) for pair in ((1, 2), (3, 4)) for h in range(IH) for i in pair
          for a, b in ([(0, WIDTH[i])] if WIDTH[i] <= 512 else [(0, WIDTH[i] // 2), (WIDTH[i] // 2, WIDTH[i])])]
ITEMS = [(i, h) for i in range(NT) for h in range(HEADS)]

K_ID, K_ROT, K_CNT, K_WIN, K_E, K_ET, K_TRI = 0, 128, 128 + 48 * NT, 160 + 48 * NT, 162 + 48 * NT, 226 + 48 * NT, 234 + 48 * NT
K_END = K_TRI + MAXR
ACC_END = len(PIECES) + 4


GATES = [(u, {"ub": 2, "gc": 6, "ga": 0}[u[0]] + u[1]) for step in PLAN for u in step
         if u[0] in ("gc", "ga") or u[0] == "ub" and u[1] >= 2]
GATE_OF = {u: g for g, (u, _) in enumerate(GATES)}
IX_CONV, IX_K, IX_Q = 2, 4, [2, 2, 2, 2, 0]
CONV_END, PD_END, LN_END = 2 * CONV_W + 6, 14, 7
SD = {"isc": 3, "logit_in": 29, "negmax": 31, "etp": 34}
SX = {"pool_diff": 10, "ln_diag": 11, "ln_mul": 15, "ln_tanh": 16, "pages": 16, "swish": 20, "index": 24, "index_turn": 25,
      "topk": 26, "logits": 30, "exp": 31, "norm": 32, "turn": 33, "keep": 34, "pv": 35, "gate": 44}


def constants():
    c = np.zeros((128, K_END), np.float32)
    c[:, :128] = np.eye(128)
    for i in range(NT):
        pos = np.full(128, float(PAST), np.float32)
        pos[:ROWS[i]] = START[i] + np.arange(ROWS[i])
        o = K_ROT + 48 * i
        for half, off in ((8, 0), (4, 32)):
            inv = np.float32(THETA) ** (-(np.arange(half, dtype=np.float32) / np.float32(half)))
            ang = pos[:, None] * inv[None, :].astype(np.float32)
            cos, sin = np.cos(ang), np.sin(ang)
            c[:, o + off:o + off + 4 * half] = np.concatenate([cos, cos, -sin, sin], 1)
    for m in range(2):
        for g in range(2):
            win = WINDOWS[2 * m + g]
            rows = slice(64 * g, 64 * g + 64)
            c[rows, K_CNT + 16 * m:K_CNT + 16 * m + 16] = 1.0 / np.minimum(np.arange(16) + 1, win)
            c[rows, K_WIN + m] = 1.0 / win
    for b in range(8):
        c[b, K_E + 8 * b:K_E + 8 * b + 8] = 1
        c[8 * b:8 * b + 8, K_ET + b] = 1
    t = np.arange(MAXR)
    c[:MAXR, K_TRI:K_TRI + MAXR] = np.where(t[None, :] <= t[:, None], 0, NEG)
    return c


class Stage:

    def __init__(self, sem):
        self.sem, self.n = sem, 0

    def did(self, ins):
        ins.then_inc(self.sem, 1)
        self.n += 1
        return ins


def program(nc, a, o):
    ctx = ExitStack()
    with ctx:
        def sb(name, *shape, dt=F32):
            return ctx.enter_context(nc.sbuf_tensor(name, list(shape), dt))

        def ps(name, *shape):
            return ctx.enter_context(nc.psum_tensor(name, list(shape), F32))

        layer_sems, loads = [], []

        def sem(name):
            s = ctx.enter_context(nc.semaphore(name))
            layer_sems.append(s)
            return s

        def stage(name):
            return Stage(sem(name))

        cst = sb("cst", 128, K_END)
        ident = cst[:, 0:128]
        E8 = cst[0:8, K_E:K_E + 64]
        ET8 = cst[0:64, K_ET:K_ET + 8]
        tri = cst[:, K_TRI:K_TRI + MAXR]
        ones = sb("ones", 128, 128)
        pow_e = sb("pow_e", 128, 8)
        table = sb("table", 1, N_SAMPLE * N_PAGES, dt=I32)
        params = sb("params", 128, DEPTH, 78)
        prm = sb("prm", 128, 78)
        prm_h = sb("prm_h", 128, 8)
        xT = sb("xT", 128, KC, TOK)
        xg = sb("xg", 128, KC, TOK)
        yT = sb("yT", 128, KC, TOK)
        W = sb("W", 128, W_SLOTS, 4, 512)
        kT = sb("kT", 128, 4, TOK)
        qT = sb("qT", 128, 4, TOK)
        V = sb("V", 128, NT, 512)
        bias = sb("bias", 128, NT - 1, SENT + NTOK)
        zi = sb("zi", 128, NT, 392)
        qkT = sb("qkT", 128, 3, TOK)
        kz = sb("kz", 128, 3, 512)
        ksq = sb("ksq", 128, 2, 512)
        gam = sb("gam", 128, 2, 64)
        uext = sb("uext", 128, 2, CONV_STATE + NTOK)
        uxs = sb("uxs", 128, 2, N_SAMPLE, CONV_W)
        bufA = sb("bufA", 128, 2, 552)
        bufB = sb("bufB", 128, 2, 552)
        cc = sb("cc", 128, 2, TOK)
        ubx = sb("ubx", 128, 2, POOL_STATE + NTOK)
        ubs = sb("ubs", 128, 2, N_SAMPLE, 16)
        pwb = sb("pwb", 128, 2, 128)
        row = sb("row", 128, TOK)
        rel = sb("rel", 128, 2, 552)
        gt = sb("gt", 128, 2, HALF)
        small = sb("small", 128, 192)
        kic = sb("kic", 128, N_SAMPLE, N_PAGES, ID)
        KV = sb("KV", 128, 4, 512)
        rows8 = sb("rows8", 8, 3 * 512)
        zis = sb("zis", 8, 392)
        sc8 = sb("sc8", 8, 272)
        zi_flat = zi[:, :, :].rearrange("p a b -> p (a b)")
        sb_scores = zi_flat[:, 0:1104].rearrange("p (a b) -> p a b", a=2)
        ibb = zi_flat[:, 1104:1104 + 784].rearrange("p (a b) -> p a b", a=2)
        pT = uext[:, :, :].rearrange("p a b -> p (a b)")[:, 0:2 * NT * MAXR].rearrange("p (a b) -> p a b", a=2)
        ixp = bufB[:, 1, 0:512]
        smp = kz[:, 0, :]
        pn = ksq[0:64, 1, 0:260]
        p64 = ksq[0:8, 1, 260:452]
        rot_tmp = sb("rot_tmp", 128, 256)
        ds = smp[:, 0:128].rearrange("p (g b h) -> p g b h", g=2, b=8)
        ssm = smp[:, 128:256].rearrange("p (g x) -> p g x", g=2)
        wbc = smp[:, 256:320]
        pts = smp[:, 320:448].rearrange("p (g x) -> p g x", g=2)
        sn = p64[:, 0:64]
        pd = p64[:, 64:128]
        qb = ubx[:, :, :].rearrange("p a b -> p (a b)")[:, 0:1024].rearrange("p (a b) -> p a b", a=2)
        lnrow = qkT[:, 2, :]
        ln_dg = bufB[:, 0, 0:NT * SR].rearrange("p (a b) -> p a b", a=NT)
        conv_new = kz[:, 1, :]
        pool_new = kz[:, 2, :]
        st_in = bufA[:, :, 0:256]
        stp_in = bufB[:, 0, 0:256]
        ssum = small[:, 0:8]
        rinv = small[:, 8:16]
        mn = small[:, 16:18]
        rsum = small[:, 18:34].rearrange("p (a b) -> p a b", a=2)
        rrec = small[:, 34:42]
        kss = small[:, 42:58].rearrange("p (a b) -> p a b", a=2)
        krn = small[:, 58:74].rearrange("p (a b) -> p a b", a=2)
        m8 = small[:, 74:90].rearrange("p (a b) -> p a b", a=2)
        lnv = small[:, 90:98]
        lnr = small[:, 98:106]
        wsum = small[:, 106:122].rearrange("p (a b) -> p a b", a=2)
        smx = small[0:64, 122:123]
        snm = small[0:64, 123:124]
        srs = small[0:64, 124:125]
        srr = small[0:64, 125:126]
        d8 = small[0:8, 126:134]
        e8 = small[0:8, 134:142]
        etp = small[0:64, 142:150]
        snw = small[0:8, 150:158]
        m8s = small[0:8, 158:166]
        isc = small[:, 166:182]
        diag = ksq[:, :, :].rearrange("p a b -> p (a b)")[:, 0:NT * SR].rearrange("p (a b) -> p a b", a=NT)

        R = ps("R", 128, 4, 512)
        A = ps("A", 128, 4, 512)

        xin = W[:, :, :, :].rearrange("p s k n -> p (s k n)")[:, 0:NT * D_MODEL].rearrange("p (i n) -> p i n", i=NT)
        yout = xin

        pre = {n: ctx.enter_context(nc.semaphore(n)) for n in
               ("pre_const", "pre_table", "pre_x", "pre_params", "pre_ones", "pre_turned", "pre_kept", "pre_par_t",
                "pre_par_k", "post_turned", "post_act", "post_dve", "post_out")}
        pin = kz[:, 0, 0:DEPTH * 128].rearrange("p (l n) -> p l n", l=DEPTH)
        pcw = kz[:, 1, 0:DEPTH * 256].rearrange("p (l n) -> p l n", l=DEPTH)
        with nc.Block() as block:
            @block.sync
            def _(sp):
                sp.dma_start(cst[:], a["consts"]).then_inc(pre["pre_const"], 16)
                x = a["x_prompt"][0]
                sp.dma_start(xin[0:N_META, 0, :], a["meta_tokens"]).then_inc(pre["pre_x"], 16)
                for i in range(NT):
                    lo = max(START[i] - N_META, 0)
                    n = START[i] + ROWS[i] - N_META - lo
                    off = ROWS[i] - n
                    sp.dma_start(xin[off:ROWS[i], i, :], x[lo:lo + n, :]).then_inc(pre["pre_x"], 16)
                sp.dma_start(xin[S0:S0 + N_SAMPLE, 4, :], a["x_sample"].rearrange("b t d -> (b t) d")).then_inc(pre["pre_x"], 16)
                for l in range(DEPTH):
                    for name, r0, n in (("norm_g", 0, 8), ("pool_scale", 8, 2), ("conv_b", 10, 2),
                                        ("conv_norm_g", 12, 2), ("conv_norm_b", 14, 2)):
                        sp.dma_start(pin[r0:r0 + n, l, :], a[name][l].rearrange("(c p) -> c p", p=128)).then_inc(pre["pre_params"], 16)
                    sp.dma_start(pcw[0:CONV_W, l, :], a["conv_w"][l]).then_inc(pre["pre_params"], 16)
                sp.dma_start(table[:, :], a["page_table"].rearrange("b n -> (b n)").unsqueeze(0)).then_inc(pre["pre_table"], 16)
                sp.wait_ge(pre["pre_table"], 16)

            @block.gpsimd
            def _(pool):
                pool.memset(ones[:], 1.0).then_inc(pre["pre_ones"], 1)
                pool.memset(pow_e[:], -0.5).then_inc(pre["pre_ones"], 1)
                pool.wait_ge(pre["pre_ones"], 2)

            @block.tensor
            def _(pe):
                pe.wait_ge(pre["pre_const"], 16)
                pe.wait_ge(pre["pre_x"], 16 * (NT + 2))
                n = 0
                for i in range(NT):
                    for g in range(2):
                        if n >= 4:
                            pe.wait_ge(pre["pre_kept"], n - 3)
                        for j in range(4):
                            m = pe.transpose(R[:, n % 4, SR * j:SR * j + ROWS_P[i]],
                                             xin[0:ROWS_P[i], i, 128 * (4 * g + j):128 * (4 * g + j) + 128],
                                             ident[0:ROWS_P[i], 0:ROWS_P[i]])
                        m.then_inc(pre["pre_turned"], 1)
                        n += 1
                pe.wait_ge(pre["pre_params"], 16 * 6 * DEPTH)
                for l in range(DEPTH):
                    pe.transpose(A[:, l, 0:16], pin[0:16, l, :], ident[0:16, 0:16])
                    for m in range(2):
                        t = pe.transpose(A[:, l, 16 + 31 * m:47 + 31 * m], pcw[0:CONV_W, l, 128 * m:128 * m + 128],
                                         ident[0:CONV_W, 0:CONV_W])
                t.then_inc(pre["pre_par_t"], 1)

            @block.vector
            def _(dve):
                n = 0
                for i in range(NT):
                    for g in range(2):
                        dve.wait_ge(pre["pre_turned"], n + 1)
                        src = R[:, n % 4, 0:4 * SR].rearrange("p (j t) -> p j t", j=4)[:, :, 0:ROWS_P[i]]
                        dve.tensor_copy(xT[:, 4 * g:4 * g + 4, START[i]:START[i] + ROWS_P[i]], src).then_inc(pre["pre_kept"], 1)
                        n += 1
                dve.wait_ge(pre["pre_par_t"], 1)
                for l in range(DEPTH):
                    dve.tensor_copy(params[:, l, :], A[:, l, 0:78]).then_inc(pre["pre_par_k"], 1)
                dve.wait_ge(pre["pre_par_k"], DEPTH)

        w_in_s = [sem(f"w_loaded{s}") for s in range(W_SLOTS)]
        gam_s, pw_s, kic_s, state_s = sem("gamma_loaded"), sem("pool_w_loaded"), sem("kidx_loaded"), sem("states_loaded")
        zero_s = stage("pool_w_zeroed")
        misc0 = stage("constants_set")
        kv_s = [sem(f"kv_loaded{s}") for s in range(4)]
        unit_s, evA, evD = stage("unit_done"), stage("evac_act"), stage("evac_dve")
        sq_s, xg_s, prm_s = stage("squares"), stage("x_scaled"), stage("params_set")
        stats_s, var_s, rinv_s, diag_s, row_t, row_s = (stage(n) for n in (
            "sumsq_done", "var_done", "rinv_done", "diag_done", "row_turned", "row_kept"))
        rope_s, idxz_s, idxt_s, idxk_s = stage("idx_rope"), stage("idx_ready"), stage("idx_turned"), stage("idx_kept")
        ix_s, rel_s, acc_s, tk_s = stage("idx_dots"), stage("idx_relu"), stage("idx_acc"), stage("topk_step")
        kss_s, krn_s, kzg_s, kz_s, kqt_s, kqk_s = (stage(n) for n in (
            "kq_sumsq", "kq_rinv", "kq_step", "kq_ready", "kq_turned", "kq_kept"))
        kq_mid = stage("kq_var")
        tanh_s, cv_s, conv_s = stage("tanh_done"), stage("conv_in_ready"), stage("conv_tap")
        gate_s = stage("gate_ready")
        st_t, st_k = stage("state_turned"), stage("state_kept")
        ps_s, pd_s = stage("pool_sum"), stage("pool_diff")
        ln_s, lnp_s, lnsq_s, lnst_s, lnt_s = (stage(n) for n in ("ln_step", "ln_rinv", "ln_square", "ln_sums", "ln_tanh"))
        nst_t, nst_k = stage("newstate_turned"), stage("newstate_kept")
        kp_s, kr_s = stage("page_product"), stage("page_scores")
        sd_s = stage("sample_step")
        zq_s, ibb_s, qbl_s, wbc_s = sem("rows_in_dram"), [sem(f"idx_row{x}_spread") for x in range(2)], [sem(f"q_row{x}_spread") for x in range(2)], sem("idx_w_spread")
        kx_s = sem("kidx_stored")
        sit_s, slog_s, sexp_s, spt_s, spk_s, spv_s = (stage(n) for n in (
            "s_idx_turned", "s_logits", "s_exp", "s_probs_turned", "s_probs_kept", "s_pv_done"))
        S_s, ttr_s, P_s, T_s, PTk_s, PV_s, on_s, y_s, rec_s = (stage(n) for n in (
            "scores", "scores_biased", "probs", "probs_turned", "probs_kept", "pv_done", "o_normed", "att_gated", "rowsum_inv"))
        out_s = [sem(f"kz_stored{s}") for s in range(3)]
        store_s, row_q, row_k, row_v, row_z = sem("stored"), sem("q_rows"), sem("k_rows"), sem("v_rows"), sem("z_rows")
        gt_s, ixp_s, ixr_s, ys_s = stage("gate_tanh"), stage("idxb_product"), stage("idxb_dots"), stage("sample_gated")
        lnd_s, lth_s = stage("ln_diag"), stage("swish_tanh")
        tb_bias = {}

        ev_of = {u: (evA, n + 1) for n, u in enumerate(u for u in UNITS if u[0] in ON_ACT)}
        ev_of.update({u: (evD, n + 1) for n, u in enumerate(u for u in UNITS if u[0] not in ON_ACT)})

        def wait_evac(eng, u):
            s, n = ev_of[u]
            eng.wait_ge(s.sem, n)

        def bank(u):
            return NUM[u] % (4 if NUM[u] < len(EARLY) else 2)

        def wait_unit(eng, u):
            eng.wait_ge(unit_s.sem, NUM[u] + 1)

        with nc.Fori(0, DEPTH) as layer:
            L = bass.ds(layer, 1)

            def dr(name):
                t = a[name] if name in a else o[name]
                return t[L]

            with nc.Block(no_gpsimd_drain=True) as block:
                @block.sync
                def _(sp):
                    stores = 0
                    z_dram, q_dram = a["z_rows"], a["q_rows"]

                    def w_load(m):
                        g, kh = divmod(m, 2)
                        kind, c0, n = GROUPS[g]
                        if m >= W_SLOTS:
                            wait_unit(sp, LAST_UNIT[(m - W_SLOTS) // 2])
                        src = dr("w_in" if kind == "in" else "w_out").rearrange("a (k p) n -> p (a k) n", p=128)
                        sp.dma_start(W[:, m % W_SLOTS, :, 0:n], src[:, 4 * kh:4 * kh + 4, c0:c0 + n]).then_inc(w_in_s[m % W_SLOTS], 16)

                    def kv_load(n):
                        name = "cache_k" if n < 16 else "cache_v"
                        if 4 <= n < 20:
                            sp.wait_ge(kr_s.sem, n - 3)
                        elif n >= 20:
                            sp.wait_ge(spv_s.sem, n - 19)
                        src = a[name][L, bass.ds(pages[n % 16], 1)].rearrange("a b p h d -> (a b p) (h d)")
                        sp.dma_start(KV[:, n % 4, :], src).then_inc(kv_s[n % 4], 16)

                    def store(dst, src):
                        nonlocal stores
                        sp.dma_start(dst, src).then_inc(store_s, 16)
                        stores += 1

                    for m in range(4):
                        w_load(m)
                    sp.dma_start(gam[:, 0, :], dr("k_norm_g").broadcast_to([128, HD])).then_inc(gam_s, 16)
                    sp.dma_start(gam[:, 1, :], dr("q_norm_g").broadcast_to([128, HD])).then_inc(gam_s, 16)
                    w_load(4)
                    sc = dr("state_conv").rearrange("a (g b) j c -> (a g) (b j) c", g=2)
                    for g in range(2):
                        sp.dma_start(st_in[0:120, g, :], sc[g]).then_inc(state_s, 16)
                    sp.dma_start(stp_in[0:120, :], dr("state_pool").rearrange("a b j c -> (a b j) c")).then_inc(state_s, 16)
                    store(dr("new_conv_sample")[:, :, 0:CONV_STATE - 1, :], dr("state_conv")[:, :, 1:CONV_STATE, :])
                    store(dr("new_pool_sample")[:, :, 0:POOL_STATE - 1, :], dr("state_pool")[:, :, 1:POOL_STATE, :])
                    sp.wait_ge(zero_s.sem, 1)
                    for g in range(4):
                        lo = 64 * (g % 2)
                        sp.dma_start(pwb[lo:lo + 64, g // 2, lo:lo + 64], dr("pool_w")[:, g].rearrange("a i o -> (a i) o")).then_inc(pw_s, 16)
                    w_load(5)
                    w_load(6)
                    pages = [sp.value_load(table[0:1, n:n + 1], min_val=0, max_val=a["cache_k"].shape[1] - 1)
                             for n in range(N_SAMPLE * N_PAGES)]
                    for n in range(N_SAMPLE * N_PAGES):
                        sp.dma_start(kic[:, n // N_PAGES, n % N_PAGES, :],
                                     a["cache_kidx"][L, bass.ds(pages[n], 1)].rearrange("a b p d -> (a b p) d")).then_inc(kic_s, 16)
                    for n in range(4):
                        kv_load(n)
                    for i in range(NT):
                        sp.wait_ge(idxz_s.sem, i + 1)
                        sp.dma_start(dr("new_kidx_prompt").rearrange("a b t d -> (a b t) d")[START[i]:START[i] + ROWS[i]],
                                     zi[0:ROWS[i], i, 256:288]).then_inc(kx_s, 16)
                    sp.dma_start(dr("new_kidx_sample").rearrange("a b t d -> (a b t) d"), zi[S0:S0 + 8, 4, 256:288]).then_inc(kx_s, 16)
                    sp.dma_start(zis[:, :], zi[S0:S0 + 8, 4, :]).then_inc(row_z, 16)
                    sp.dma_start(z_dram, zi[S0:S0 + 8, 4, :]).then_inc(zq_s, 16)
                    w_load(7)
                    w_load(8)

                    def k_store(i):
                        sp.wait_ge(kz_s.sem, i + 1)
                        sp.dma_start(dr("new_k_prompt").rearrange("a b t h d -> (a b t) (h d)")[START[i]:START[i] + ROWS[i]],
                                     kz[0:ROWS[i], i % 3, :]).then_inc(out_s[i % 3], 16)

                    for i in range(3):
                        k_store(i)
                    w_load(9)
                    w_load(10)
                    for i in range(3, NT):
                        k_store(i)
                    sp.dma_start(dr("new_k_sample").rearrange("a b t h d -> (a b t) (h d)"), kz[S0:S0 + 8, 1, :]).then_inc(out_s[1], 16)
                    sp.dma_start(rows8[:, 512:1024], kz[S0:S0 + 8, 1, :]).then_inc(row_k, 16)
                    w_load(11)
                    w_load(12)
                    sp.wait_ge(kz_s.sem, 2 * NT)
                    sp.dma_start(rows8[:, 0:512], kz[S0:S0 + 8, 9 % 3, :]).then_inc(row_q, 16)
                    sp.dma_start(q_dram, kz[S0:S0 + 8, 9 % 3, :]).then_inc(zq_s, 16)
                    w_load(13)
                    w_load(14)
                    for i in range(NT):
                        wait_evac(sp, ("v", i, 0))
                        store(dr("new_v_prompt").rearrange("a b t h d -> (a b t) (h d)")[START[i]:START[i] + ROWS[i]], V[0:ROWS[i], i, :])
                    store(dr("new_v_sample").rearrange("a b t h d -> (a b t) (h d)"), V[S0:S0 + 8, 4, :])
                    sp.dma_start(rows8[:, 1024:1536], V[S0:S0 + 8, 4, :]).then_inc(row_v, 16)
                    sp.wait_ge(nst_k.sem, 4)
                    new_cp = dr("new_conv_prompt").rearrange("a b j c -> (a b j) c")
                    new_pp = dr("new_pool_prompt").rearrange("a b j c -> (a b j) c")
                    store(new_cp, conv_new[0:CONV_STATE, 0:256])
                    store(dr("new_conv_sample")[:, :, CONV_STATE - 1, :].rearrange("a b c -> (a b) c"), conv_new[0:8, 256:512])
                    store(new_pp, pool_new[0:POOL_STATE, 0:256])
                    store(dr("new_pool_sample")[:, :, POOL_STATE - 1, :].rearrange("a b c -> (a b) c"), pool_new[0:8, 256:512])
                    w_load(15)
                    w_load(16)
                    sp.wait_ge(zq_s, 32)
                    sp.wait_ge(row_q, 16)
                    sp.wait_ge(row_z, 16)
                    sp.wait_ge(kx_s, 96)
                    sp.wait_ge(acc_s.sem, ACC_END)
                    sp.wait_ge(kqt_s.sem, 2 * NT)
                    sp.dma_start(wbc.rearrange("p (b h) -> p b h", b=8), z_dram[:, 384:392].unsqueeze(0).broadcast_to([128, 8, 8])).then_inc(wbc_s, 16)
                    sp.wait_ge(pd_s.sem, PD_END)

                    def spread(b):
                        if b >= 2:
                            sp.wait_ge(ixp_s.sem, b - 1)
                        sp.dma_start(ibb[:, b % 2, :], z_dram[b:b + 1, :].broadcast_to([128, 392])).then_inc(ibb_s[b % 2], 16)
                        if b >= 2:
                            sp.wait_ge(kp_s.sem, 2 * b - 2)
                        sp.dma_start(qb[:, b % 2, :], q_dram[b:b + 1, :].broadcast_to([128, 512])).then_inc(qbl_s[b % 2], 16)

                    spread(0)
                    spread(1)
                    for b in range(6):
                        spread(b + 2)
                        kv_load(2 * b + 4)
                        kv_load(2 * b + 5)
                        if b == 2:
                            w_load(17)
                            w_load(18)
                    w_load(19)
                    for n in range(16, 32):
                        kv_load(n)
                    sp.wait_ge(store_s, 16 * stores)
                    for s in range(3):
                        sp.wait_ge(out_s[s], 16 * ([2, 3, 1][s]))

                @block.gpsimd
                def _(pool):
                    zero_s.did(pool.memset(pwb[:], 0.0))
                    misc0.did(pool.memset(bias[:, :, 0:SENT], BIG))
                    misc0.did(pool.memset(rel[:], 0.0))
                    misc0.did(pool.memset(uext[:, :, 0:CONV_STATE], 0.0))
                    misc0.did(pool.memset(ubx[:, :, 0:POOL_STATE], 0.0))
                    pool.wait_ge(var_s.sem, 1)
                    rinv_s.did(pool.tensor_tensor(rinv[0:SR, 0:NT], ssum[0:SR, 0:NT], pow_e[0:SR, 0:NT], ALU.pow))

                    def rotate(z, heads, hd, half, i, n, tab, tmp, s):
                        r = ROWS_P[i]
                        cos = cst[0:r, K_ROT + 48 * i + tab:K_ROT + 48 * i + tab + 2 * half].unsqueeze(1)
                        sin = cst[0:r, K_ROT + 48 * i + tab + 2 * half:K_ROT + 48 * i + tab + 4 * half].unsqueeze(1)
                        w = heads * 2 * half
                        ta = tmp[0:r, 0:w].rearrange("p (h x) -> p h x", h=heads)
                        tb = tmp[0:r, w:2 * w].rearrange("p (h x) -> p h x", h=heads)
                        s.did(pool.tensor_tensor(ta, z[:, :, 0:2 * half], cos.broadcast_to([r, heads, 2 * half]), ALU.mult))
                        s.did(pool.tensor_tensor(tb[:, :, 0:half], z[:, :, half:2 * half], sin[:, :, 0:half].broadcast_to([r, heads, half]), ALU.mult))
                        s.did(pool.tensor_tensor(tb[:, :, half:2 * half], z[:, :, 0:half], sin[:, :, half:2 * half].broadcast_to([r, heads, half]), ALU.mult))
                        pool.wait_ge(s.sem, s.n)
                        return ta, tb

                    for i in range(NT):
                        r = ROWS_P[i]
                        wait_evac(pool, ("idx", i, 0))
                        z = zi[0:r, i, 0:288].rearrange("p (h d) -> p h d", h=9)
                        if i:
                            pool.wait_ge(idxz_s.sem, i)
                        ta, tb = rotate(z, 9, ID, 4, i, 0, 32, rot_tmp, rope_s)
                        rope_s.did(pool.tensor_tensor(z[:, :, 0:8], ta, tb, ALU.add))
                        pool.wait_ge(rope_s.sem, rope_s.n)
                        idxz_s.did(pool.tensor_copy(zi[0:r, i, 288:384].rearrange("p (h d) -> p h d", h=3),
                                                    zi[0:r, i, 256:288].unsqueeze(1).broadcast_to([r, 3, ID])))

                    def kq_tile(n):
                        w, i = divmod(n, NT)
                        r = ROWS_P[i]
                        z = kz[0:r, n % 3, :].rearrange("p (h d) -> p h d", h=HEADS)
                        pool.wait_ge(kq_mid.sem, n + 1)
                        krn_s.did(pool.tensor_tensor(krn[0:r, n % 2, :], kss[0:r, n % 2, :], pow_e[0:r, :], ALU.pow))
                        pool.wait_ge(krn_s.sem, n + 1)
                        kzg_s.did(pool.tensor_tensor(z, z, krn[0:r, n % 2, :].unsqueeze(2).broadcast_to([r, HEADS, HD]), ALU.mult))
                        pool.wait_ge(kzg_s.sem, kzg_s.n)
                        kzg_s.did(pool.tensor_tensor(z, z, gam[0:r, w, :].unsqueeze(1).broadcast_to([r, HEADS, HD]), ALU.mult))
                        pool.wait_ge(kzg_s.sem, kzg_s.n)
                        ta, tb = rotate(z, HEADS, HD, 8, i, n, 0, rot_tmp, kzg_s)
                        kz_s.did(pool.tensor_tensor(z[:, :, 0:16], ta, tb, ALU.add))
                        pool.wait_ge(kz_s.sem, n + 1)

                    pool.wait_ge(gam_s, 32)
                    for n in range(2 * NT):
                        kq_tile(n)

                    pool.wait_ge(st_k.sem, 2)
                    pool.wait_ge(cv_s.sem, 4)
                    wait_evac(pool, ("ub", 1, 1))
                    n = POOL_STATE + NTOK
                    ps_s.did(pool.tensor_tensor(bufA[:, :, 1:n], ubx[:, :, 1:n], ubx[:, :, 0:n - 1], ALU.add))
                    pool.wait_ge(ps_s.sem, 1)
                    ps_s.did(pool.tensor_tensor(bufB[:, :, 3:n], bufA[:, :, 3:n], bufA[:, :, 1:n - 2], ALU.add))
                    pool.wait_ge(ps_s.sem, 2)
                    ps_s.did(pool.tensor_tensor(bufA[:, 1, 7:n], bufB[:, 1, 7:n], bufB[:, 1, 3:n - 4], ALU.add))
                    pool.wait_ge(ps_s.sem, 3)
                    ps_s.did(pool.tensor_tensor(bufB[64:128, 1, 15:n], bufA[64:128, 1, 15:n], bufA[64:128, 1, 7:n - 8], ALU.add))
                    pool.wait_ge(ps_s.sem, 4)

                    wait_evac(pool, ("lnsum", 0, 0))
                    lnp_s.did(pool.tensor_tensor(lnr[0:SR, 0:NT], lnv[0:SR, 0:NT], pow_e[0:SR, 0:NT], ALU.pow))

                    pool.wait_ge(kic_s, 256)
                    pool.wait_ge(pd_s.sem, PD_END)
                    prod = ixp.rearrange("p (g h d) -> p g h d", g=2, h=IH)
                    for b in range(8):
                        pool.wait_ge(ibb_s[b % 2], 16 * (b // 2 + 1))
                        if b:
                            pool.wait_ge(ixr_s.sem, b)
                        ixp_s.did(pool.tensor_tensor(prod, kic[:, b, :, :].unsqueeze(2).broadcast_to([128, 2, IH, ID]),
                                                     ibb[:, b % 2, 0:256].rearrange("p (h d) -> p h d", h=IH).unsqueeze(1).broadcast_to([128, 2, IH, ID]),
                                                     ALU.mult))
                        pool.wait_ge(qbl_s[b % 2], 16 * (b // 2 + 1))
                        for n in (2 * b, 2 * b + 1):
                            pool.wait_ge(kv_s[n % 4], 16 * (n // 4 + 1))
                            kp_s.did(pool.tensor_tensor(KV[:, n % 4, :], KV[:, n % 4, :], qb[:, b % 2, :], ALU.mult))

                @block.scalar
                def _(act):
                    def copy(out, in_, scale=1.0):
                        return act.activation(out, in_, ACT.Copy, scale=scale)

                    for kc in range(KC):
                        sq_s.did(act.activation(yT[:, kc, :], xT[:, kc, :], ACT.Square))
                    act.wait_ge(rinv_s.sem, 1)

                    def idx_evac(i):
                        r, k = ROWS_P[i], bank(("idx", i, 0))
                        wait_unit(act, ("idx", i, 0))
                        copy(zi[0:r, i, 0:256], R[0:r, k, 0:256], rinv[0:r, i:i + 1])
                        copy(zi[0:r, i, 256:288], R[0:r, k, 264:296], rinv[0:r, i:i + 1])
                        evA.did(copy(zi[0:r, i, 384:392], R[0:r, k, 256:264], rinv[0:r, i:i + 1]))

                    for i in range(NT):
                        idx_evac(i)
                        if i == 2:
                            act.wait_ge(row_t.sem, 1)
                            row_s.did(copy(row[:, 0:START[4]], A[:, 2, 0:START[4]]))
                            row_s.did(copy(row[:, START[4]:TOK], A[:, 3, 16:16 + SR]))

                    act.wait_ge(st_t.sem, 1)
                    st_k.did(copy(uxs[:, :, :, 0:CONV_STATE], A[:, 0, 0:480].rearrange("p (c b j) -> p c b j", c=2, b=8)))
                    act.wait_ge(st_t.sem, 2)
                    st_k.did(copy(ubs[:, :, :, 0:POOL_STATE], A[:, 1, 0:240].rearrange("p (c b j) -> p c b j", c=2, b=8)))

                    def half_tanh(c):
                        wait_evac(act, ("conv", 2 + c, 1))
                        tanh_s.did(act.activation(bufB[:, c, 0:TOK], bufB[:, c, 0:TOK], ACT.Tanh, scale=0.5))

                    for i in range(NT):
                        act.wait_ge(idxt_s.sem, i + 1)
                        idxk_s.did(copy(qkT[:, :, START[i]:START[i] + ROWS_P[i]],
                                        A[:, i % 2, 0:336].rearrange("p (c t) -> p c t", c=3)[:, :, 0:ROWS_P[i]]))

                    def kq_evac(n):
                        w, i = divmod(n, NT)
                        u, r = (("k", "q")[w], i, 0), ROWS_P[i]
                        wait_unit(act, u)
                        if n >= 3:
                            act.wait_ge(kqt_s.sem, n - 2)
                        if 3 <= n < 8:
                            act.wait_ge(out_s[n % 3], 16 * (n // 3) if n != 7 else 48)
                        if n == 7:
                            act.wait_ge(row_k, 16)
                        copy(kz[0:r, n % 3, :], R[0:r, bank(u), :], rinv[0:r, i:i + 1])
                        if n >= 2:
                            act.wait_ge(kss_s.sem, n - 1)
                        evA.did(act.activation(ksq[0:r, n % 2, :], R[0:r, bank(u), :], ACT.Square, scale=rinv[0:r, i:i + 1]))

                    def kq_keep(n):
                        i, dst = n % NT, (kT, qT)[n // NT]
                        act.wait_ge(kqt_s.sem, n + 1)
                        kqk_s.did(copy(dst[:, :, START[i]:START[i] + ROWS_P[i]],
                                       A[:, 2 + n % 2, 0:448].rearrange("p (c t) -> p c t", c=4)[:, :, 0:ROWS_P[i]]))

                    def relu(p):
                        i, h, lo, hi = PIECES[p]
                        act.wait_ge(ix_s.sem, p + 1)
                        if p >= 2:
                            act.wait_ge(acc_s.sem, p - 1 if p - 1 <= 16 else p + 1)
                        rel_s.did(act.activation(rel[0:ROWS[i], p % 2, 0:hi - lo], A[0:ROWS[i], p % 2, 0:hi - lo], ACT.Relu,
                                                 scale=1.0 / 16))

                    act.wait_ge(misc0.sem, 2)
                    for p in range(6 * IX_CONV):
                        relu(p)
                        if p == 2 * IX_CONV - 1:
                            half_tanh(0)
                    half_tanh(1)
                    p += 1
                    for i in range(NT):
                        kq_evac(i)
                        if i >= 2:
                            kq_keep(i - 2)
                        for _ in range(IX_K):
                            relu(p)
                            p += 1
                    for i in range(NT):
                        kq_evac(NT + i)
                        kq_keep(3 + i)
                        for _ in range(IX_Q[i]):
                            relu(p)
                            p += 1
                    for i in range(NT):
                        wait_unit(act, ("v", i, 0))
                        evA.did(copy(V[0:ROWS_P[i], i, :], R[0:ROWS_P[i], bank(("v", i, 0)), :], rinv[0:ROWS_P[i], i:i + 1]))
                        if i < 2:
                            kq_keep(8 + i)

                    def gate_tanh(g):
                        u = GATES[g]
                        wait_evac(act, u[0])
                        if g >= 2:
                            act.wait_ge(gate_s.sem, g - 1)
                        gt_s.did(act.activation(gt[:, g % 2, :], yT[:, u[1], HALF * u[0][2]:HALF * u[0][2] + HALF], ACT.Tanh, scale=0.5))

                    def new_state(dst, rows, n):
                        act.wait_ge(nst_t.sem, n)
                        nst_k.did(copy(dst[0:rows, 0:256], A[0:rows, 3, 0:256]))
                        nst_k.did(copy(dst[0:8, 256:512], A[0:8, 3, 256:512]))

                    new_state(conv_new, CONV_STATE, 1)
                    for n in range(len(ITEMS) + PIPE):
                        if n < len(ITEMS):
                            i, h = ITEMS[n]
                            r, w = ROWS[i], WIDTH[i]
                            act.wait_ge(ttr_s.sem, n + 1)
                            if n >= 2:
                                act.wait_ge(T_s.sem, n - 1)
                            if i >= 2 and h == 0:
                                act.wait_ge(rec_s.sem, i - 1)
                            P_s.did(act.activation(rel[0:r, n % 2, 0:w], sb_scores[0:r, n % 2, 0:w], ACT.Exp,
                                                   bias=mn[0:r, n % 2:n % 2 + 1], scale=-1.0, accum_out=rsum[0:r, i % 2, h:h + 1]))
                        if 2 <= n < len(ITEMS) + 2:
                            m = n - 2
                            i, h = ITEMS[m]
                            act.wait_ge(T_s.sem, m + 1)
                            if m >= 2:
                                act.wait_ge(PV_s.sem, m - 1)
                            dst = pT[0:MAXR, m % 2, :].rearrange("p (j t) -> p j t", j=NT)[:, 0:i + 1, 0:ROWS[i]]
                            PTk_s.did(copy(dst, A[0:MAXR, m % 2, 0:(i + 1) * ROWS[i]].rearrange("p (j t) -> p j t", j=i + 1)))
                        if n == 5:
                            new_state(pool_new, POOL_STATE, 2)
                        if n == SX["ln_tanh"]:
                            act.wait_ge(ln_s.sem, 1)
                            for c in range(2):
                                lth_s.did(act.activation(qkT[:, c, :], cc[:, c, :], ACT.Tanh, scale=prm_h[:, 4 + c:5 + c], bias=prm_h[:, 6 + c:7 + c]))
                        if n == SX["exp"]:
                            act.wait_ge(sd_s.sem, SD["negmax"])
                            sexp_s.did(act.activation(pn[:, 0:257], A[0:64, 3, 0:257], ACT.Exp, bias=snm, scale=0.125, accum_out=srs))
                        if n == SX["keep"]:
                            act.wait_ge(spt_s.sem, 1)
                            spk_s.did(copy(pts[:, :, :], A[:, 3, 0:128].rearrange("p (g x) -> p g x", g=2)))
                            spk_s.did(copy(pd[:, :], A[0:8, 3, 128:192]))
                        for u in PLAN[n]:
                            if u in GATE_OF:
                                gate_tanh(GATE_OF[u])
                            if u == ("mean", 0, 1):
                                wait_evac(act, u)
                                lnsq_s.did(act.activation(qkT[:, 0:2, :], cc[:, :, :], ACT.Square))
                            if u[0] == "lnrow":
                                wait_unit(act, u)
                                lo, hi = ((0, START[4]), (START[4], TOK))[u[2]]
                                evA.did(copy(lnrow[:, lo:hi], R[:, bank(u), 0:hi - lo]))
                            if u[0] == "turn":
                                i = u[1]
                                wait_unit(act, u)
                                evA.did(copy(qT[:, :, START[i]:START[i] + ROWS[i]],
                                             R[:, bank(u), 0:4 * MAXR].rearrange("p (c t) -> p c t", c=4)[:, :, 0:ROWS[i]]))

                @block.tensor
                def _(pe):
                    def turn(out, in_, k):
                        return pe.transpose(out, in_, ident[0:k, 0:k])

                    def open_unit(u):
                        old = [v for v in UNITS[:NUM[u]] if bank(v) == bank(u)]
                        if old:
                            wait_evac(pe, old[-1])
                        return bank(u)

                    def w_wait(g, kh):
                        m = 2 * g + kh
                        pe.wait_ge(w_in_s[m % W_SLOTS], 16 * (m // W_SLOTS + 1))
                        return m % W_SLOTS

                    def unit_tm(u, g, n, first=False):
                        i, k = u[1], open_unit(u)
                        r = ROWS_P[i]
                        for kc in range(KC):
                            slot = w_wait(g, kc // 4)
                            if first:
                                pe.wait_ge(xg_s.sem, kc + 1)
                            m = pe.matmul(R[0:r, k, 0:n], xg[:, kc, START[i]:START[i] + r], W[:, slot, kc % 4, 0:n],
                                          start=(kc == 0), stop=(kc == KC - 1))
                        unit_s.did(m)

                    def unit_fm(u, g, col, src):
                        k = open_unit(u)
                        for kc in range(KC):
                            slot = w_wait(g, kc // 4)
                            m = pe.matmul(R[:, k, 0:HALF], W[:, slot, kc % 4, col:col + 128], src[:, kc, HALF * u[2]:HALF * u[2] + HALF],
                                          start=(kc == 0), stop=(kc == KC - 1))
                        unit_s.did(m)

                    unit_tm(("idx", 0, 0), 0, 296, first=True)
                    pe.wait_ge(sq_s.sem, KC)
                    for i in range(NT):
                        for kc in range(KC):
                            m = pe.matmul(A[0:SR, 3, i:i + 1], yT[:, kc, START[i]:START[i] + SR], ones[:, 0:1],
                                          start=(kc == 0), stop=(kc == KC - 1))
                    stats_s.did(m)
                    unit_tm(("idx", 1, 0), 0, 296)
                    unit_tm(("idx", 2, 0), 0, 296)

                    def spread(src, stage):
                        for i in range(NT):
                            r = ROWS_P[i] if i == 4 else ROWS[i]
                            out = A[:, 2, START[i]:START[i] + r] if i < 4 else A[:, 3, 16:16 + r]
                            m = pe.matmul(out, ones[0:r, :], diag[0:r, i, 0:r], start=True, stop=True)
                        stage.did(m)

                    pe.wait_ge(diag_s.sem, NT)
                    spread(diag, row_t)
                    unit_tm(("idx", 3, 0), 0, 296)
                    unit_tm(("idx", 4, 0), 0, 296)
                    pe.wait_ge(state_s, 48)
                    for c in range(2):
                        for g in range(2):
                            m = turn(A[:, 0, 240 * c + 120 * g:240 * c + 120 * g + 120], st_in[0:120, g, 128 * c:128 * c + 128], 120)
                    st_t.did(m)
                    for c in range(2):
                        m = turn(A[:, 1, 120 * c:120 * c + 120], stp_in[0:120, 128 * c:128 * c + 128], 120)
                    st_t.did(m)
                    for h in range(2):
                        unit_fm(("conv", 0, h), 1, 0, xg)
                    pe.wait_ge(st_k.sem, 2)
                    for i in range(NT):
                        pe.wait_ge(idxz_s.sem, i + 1)
                        if i >= 2:
                            pe.wait_ge(idxk_s.sem, i - 1)
                        for j in range(3):
                            m = turn(A[:, i % 2, 112 * j:112 * j + ROWS_P[i]], zi[0:ROWS_P[i], i, 128 * j:128 * j + 128], ROWS_P[i])
                        idxt_s.did(m)

                    def kq_turn(n):
                        i = n % NT
                        r = ROWS_P[i]
                        pe.wait_ge(kz_s.sem, n + 1)
                        if n < 2:
                            pe.wait_ge(row_s.sem, 2)
                        else:
                            pe.wait_ge(kqk_s.sem, n - 1)
                        for j in range(4):
                            m = turn(A[:, 2 + n % 2, 112 * j:112 * j + r], kz[0:r, n % 3, 128 * j:128 * j + 128], r)
                        kqt_s.did(m)

                    def dots(p):
                        i, h, lo, hi = PIECES[p]
                        if p == 0:
                            pe.wait_ge(idxk_s.sem, NT)
                        if p >= 2:
                            pe.wait_ge(rel_s.sem, p - 1)
                        b = 32 * (h % 4)
                        ix_s.did(pe.matmul(A[0:ROWS[i], p % 2, 0:hi - lo], qkT[b:b + 32, h // 4, START[i]:START[i] + ROWS[i]],
                                           qkT[b:b + 32, 2, lo:hi], start=True, stop=True))

                    p = 0
                    for m in (2, 1, 3):
                        for h in range(2):
                            unit_fm(("conv", m, h), 1, 128 * m, xg)
                            for _ in range(IX_CONV):
                                dots(p)
                                p += 1
                    for i in range(NT):
                        unit_tm(("k", i, 0), 2, 512)
                        if i >= 2:
                            kq_turn(i - 2)
                        for _ in range(IX_K):
                            dots(p)
                            p += 1
                    for i in range(NT):
                        unit_tm(("q", i, 0), 3, 512)
                        kq_turn(3 + i)
                        for _ in range(IX_Q[i]):
                            dots(p)
                            p += 1
                    for i in range(NT):
                        unit_tm(("v", i, 0), 4, 512)
                        if i < 2:
                            kq_turn(8 + i)

                    def new_state(ext, rows, s, last):
                        for c in range(2):
                            turn(A[0:rows, 3, 128 * c:128 * c + 128], ext[:, c, NTOK:NTOK + rows], 128)
                            m = turn(A[0:8, 3, 256 + 128 * c:384 + 128 * c], s[:, c, :, last], 128)
                        nst_t.did(m)

                    pe.wait_ge(kqk_s.sem, 2 * NT)
                    pe.wait_ge(cv_s.sem, 4)
                    new_state(uext, CONV_STATE, uxs, CONV_STATE)
                    pe.wait_ge(rel_s.sem, len(PIECES))
                    for u in UNITS[len(EARLY) - 2:len(EARLY)]:
                        wait_evac(pe, u)

                    def scores(n):
                        i, h = ITEMS[n]
                        r, w, b = ROWS[i], WIDTH[i], 64 * (h % 2)
                        if w > 512:
                            pe.wait_ge(ttr_s.sem, n)
                        elif n >= 2:
                            pe.wait_ge(ttr_s.sem, n - 1)
                        k = 2 if w > 512 else 2 + n % 2
                        lhs = qT[b:b + 64, h // 2, START[i]:START[i] + r]
                        m = pe.matmul(R[0:r, k, 0:min(w, 512)], lhs, kT[b:b + 64, h // 2, 0:min(w, 512)], start=True, stop=True)
                        if w > 512:
                            m = pe.matmul(R[0:r, k + 1, 0:w - 512], lhs, kT[b:b + 64, h // 2, 512:w], start=True, stop=True)
                        S_s.did(m)

                    def turn_probs(n):
                        i, h = ITEMS[n]
                        pe.wait_ge(P_s.sem, n + 1)
                        if n >= 2:
                            pe.wait_ge(PTk_s.sem, n - 1)
                        for j in range(i + 1):
                            m = turn(A[0:MAXR, n % 2, ROWS[i] * j:ROWS[i] * (j + 1)], rel[0:ROWS[i], n % 2, START[j]:START[j] + MAXR], ROWS[i])
                        T_s.did(m)

                    def weigh(n):
                        i, h = ITEMS[n]
                        pe.wait_ge(PTk_s.sem, n + 1)
                        if h == 0 and i:
                            pe.wait_ge(on_s.sem, i)
                        pt = pT[:, n % 2, :].rearrange("p (j t) -> p j t", j=NT)
                        for j in range(i + 1):
                            m = pe.matmul(A[0:ROWS[i], 2, HD * h:HD * h + HD], pt[0:ROWS[j], j, 0:ROWS[i]],
                                          V[0:ROWS[j], j, HD * h:HD * h + HD], start=(j == 0), stop=(j == i))
                        PV_s.did(m)

                    def unit(u):
                        kind, m, h = u
                        if kind == "ub":
                            unit_fm(u, 5, 128 * m, xg)
                        elif kind == "gc":
                            unit_fm(u, 6, 128 * m, xg)
                        elif kind == "ga":
                            unit_fm(u, 7, 128 * m, xg)
                        elif kind == "out":
                            unit_fm(u, 8 + m // 4, 128 * (m % 4), yT)
                        elif kind == "mean":
                            if h == 0:
                                pe.wait_ge(conv_s.sem, CONV_END)
                            k = open_unit(u)
                            for c in range(2):
                                x = pe.matmul(R[:, k, 0:HALF], ones[:], cc[:, c, HALF * h:HALF * h + HALF], start=(c == 0), stop=(c == 1))
                            unit_s.did(x)
                        elif kind == "lnsum":
                            k = open_unit(u)
                            pe.wait_ge(lnsq_s.sem, 1)
                            for i in range(NT):
                                for c in range(2):
                                    x = pe.matmul(R[0:SR, k, i:i + 1], qkT[:, c, START[i]:START[i] + SR], ones[:, 0:1],
                                                  start=(c == 0), stop=(c == 1))
                            unit_s.did(x)
                        elif kind == "lnrow":
                            k = open_unit(u)
                            pe.wait_ge(lnd_s.sem, NT)
                            for i in (range(4), range(4, NT))[h]:
                                r = ROWS[i] if i < 4 else ROWS_P[i]
                                lo = START[i] if i < 4 else 0
                                x = pe.matmul(R[:, k, lo:lo + r], ones[0:r, :], ln_dg[0:r, i, 0:r], start=True, stop=True)
                            unit_s.did(x)
                        elif kind == "pool":
                            k = open_unit(u)
                            pe.wait_ge(pw_s, 64)
                            lo = POOL_STATE + HALF * h
                            unit_s.did(pe.matmul(R[:, k, 0:HALF], pwb[:, m, :], bufA[:, m, lo:lo + HALF], start=True, stop=True))
                        elif kind == "turn":
                            k = open_unit(u)
                            pe.wait_ge(on_s.sem, m + 1)
                            for c in range(4):
                                x = turn(R[:, k, MAXR * c:MAXR * c + ROWS[m]], ksq[0:ROWS[m], 0, 128 * c:128 * c + 128], ROWS[m])
                            unit_s.did(x)

                    for n in range(len(ITEMS) + PIPE):
                        if n < len(ITEMS):
                            scores(n)
                        if n == SX["index_turn"]:
                            pe.wait_ge(sd_s.sem, SD["isc"])
                            for g in range(2):
                                m = turn(A[0:8, 3, 128 * g:128 * g + 128], isc[:, 8 * g:8 * g + 8], 128)
                            sit_s.did(m)
                        if n == SX["logits"]:
                            pe.wait_ge(sd_s.sem, SD["logit_in"])
                            pe.wait_ge(kr_s.sem, 16)
                            out = A[0:64, 3, :]
                            pe.matmul(out[:, 0:257], E8, sc8[:, 0:257], start=True, stop=False)
                            for g in range(2):
                                pe.matmul(out[:, 128 * g:128 * g + 128], ssm[:, g, :], ident, start=False, stop=False)
                            slog_s.did(pe.matmul(out[:, 256:257], sn, ones[0:8, 0:1], start=False, stop=True))
                        if n == SX["turn"]:
                            pe.wait_ge(sd_s.sem, SD["etp"])
                            for g in range(2):
                                turn(A[:, 3, 64 * g:64 * g + 64], pn[:, 128 * g:128 * g + 128], 64)
                            spt_s.did(pe.matmul(A[0:8, 3, 128:192], etp, ident[0:64, 0:64], start=True, stop=True))
                        if n == 5:
                            pe.wait_ge(nst_k.sem, 2)
                            wait_evac(pe, ("ub", 1, 1))
                            new_state(ubx, POOL_STATE, ubs, POOL_STATE)
                        if n == 32:
                            pe.wait_ge(y_s.sem, 1)
                            pe.wait_ge(ln_s.sem, LN_END)
                            wait_evac(pe, ("pool", 1, 1))
                        for u in PLAN[n]:
                            if u[0] != "turn":
                                unit(u)
                        if 2 <= n < len(ITEMS) + 2:
                            turn_probs(n - 2)
                        if 3 <= n < len(ITEMS) + 3:
                            weigh(n - 3)
                        for u in PLAN[n]:
                            if u[0] == "turn":
                                unit(u)
                        if SX["pv"] <= n < SX["pv"] + 8:
                            acc = A[:, 3, 0:64]
                            if n == SX["pv"]:
                                pe.wait_ge(spk_s.sem, 2)
                                pe.wait_ge(row_v, 16)
                                for c in range(4):
                                    new = pd[:, :].rearrange("p (b h) -> p b h", b=8)[:, :, 2 * c:2 * c + 2]
                                    pe.matmul(acc[:, 16 * c:16 * c + 16], rows8[:, 1024 + 128 * c:1152 + 128 * c], new,
                                              start=(c == 0), stop=False, skip_group_check=True)
                            b = n - SX["pv"]
                            for g in range(2):
                                page = 16 + 2 * b + g
                                pe.wait_ge(kv_s[page % 4], 16 * (page // 4 + 1))
                                for c in range(4):
                                    m = pe.matmul(acc[:, 16 * c + 2 * b:16 * c + 2 * b + 2], KV[:, page % 4, 128 * c:128 * c + 128],
                                                  pts[:, g, 8 * b + 2 * c:8 * b + 2 * c + 2], start=False,
                                                  stop=(page == 31 and c == 3), skip_group_check=True)
                                spv_s.did(m)
                    pe.wait_ge(y_s.sem, 3)
                    pe.wait_ge(ys_s.sem, 2)
                    for m in range(KC):
                        unit(("out", m, 1))

                @block.vector
                def _(dve):
                    def stt(out, a0, s, a1, op0=ALU.mult, op1=ALU.mult):
                        return dve.scalar_tensor_tensor(out=out, in0=a0, scalar=s, in1=a1, op0=op0, op1=op1)

                    prm_s.did(dve.tensor_copy(prm[:, :], params[:, L, :].rearrange("p a n -> p (a n)")))
                    dve.wait_ge(prm_s.sem, 1)
                    for kc in range(KC):
                        xg_s.did(dve.tensor_scalar(xg[:, kc, :], xT[:, kc, :], prm[:, kc:kc + 1], None, ALU.mult))
                    prm_s.did(dve.tensor_scalar(prm_h[:, :], prm[:, 8:16], 0.5, None, ALU.mult))
                    dve.wait_ge(stats_s.sem, 1)
                    var_s.did(dve.tensor_scalar(ssum[0:SR, 0:NT], A[0:SR, 3, 0:NT], 1.0 / D_MODEL, EPS, ALU.mult, ALU.add))
                    dve.wait_ge(rinv_s.sem, 1)
                    for i in range(NT):
                        r = ROWS_P[i]
                        diag_s.did(dve.tensor_scalar(diag[0:r, i, 0:r], ident[0:r, 0:r], rinv[0:r, i:i + 1], None, ALU.mult))
                    dve.wait_ge(row_s.sem, 2)
                    dve.wait_ge(st_t.sem, 2)
                    dve.wait_ge(misc0.sem, 4)
                    dve.wait_ge(st_k.sem, 2)

                    def tok(h):
                        return slice(HALF * h, HALF * h + HALF)

                    def conv_in(c):
                        dve.wait_ge(tanh_s.sem, c + 1)
                        cv_s.did(stt(uext[:, c, CONV_STATE:CONV_STATE + NTOK], bufB[:, c, 0:NTOK], 1.0, bufA[:, c, 0:NTOK], ALU.add))
                        cv_s.did(stt(uxs[:, c, :, CONV_STATE], bufB[:, c, NTOK:TOK], 1.0, bufA[:, c, NTOK:TOK], ALU.add))

                    def kq_sum(n):
                        w, i = divmod(n, NT)
                        r = ROWS_P[i]
                        wait_evac(dve, (("k", "q")[w], i, 0))
                        if n >= 2:
                            dve.wait_ge(krn_s.sem, n - 1)
                        kss_s.did(dve.reduce_sum(kss[0:r, n % 2, :], ksq[0:r, n % 2, :].rearrange("p (h d) -> p h d", h=HEADS), AX.X))
                        dve.wait_ge(kss_s.sem, n + 1)
                        kq_mid.did(dve.tensor_scalar(kss[0:r, n % 2, :], kss[0:r, n % 2, :], 1.0 / HD, EPS, ALU.mult, ALU.add))

                    def area(i, lo=0, hi=None):
                        hi = SENT + WIDTH[i] if hi is None else hi
                        return bias[0:ROWS[i], i - 1, lo:hi]

                    last = {}

                    def gather(p):
                        i, h, lo, hi = PIECES[p]
                        dve.wait_ge(rel_s.sem, p + 1)
                        dst = area(i, SENT + lo, SENT + hi)
                        w = zi[0:ROWS[i], i, 384 + h:385 + h]
                        src = rel[0:ROWS[i], p % 2, 0:hi - lo]
                        if h == 0:
                            acc_s.did(dve.tensor_scalar(dst, src, w, None, ALU.mult))
                        else:
                            dve.wait_ge(acc_s.sem, last[i, lo])
                            acc_s.did(stt(dst, src, w, dst, ALU.mult, ALU.add))
                        last[i, lo] = acc_s.n

                    def causal(i, s):
                        d = area(i, SENT + START[i], SENT + WIDTH[i])
                        s.did(dve.tensor_tensor(d, d, tri[0:ROWS[i], 0:ROWS[i]], ALU.add))

                    def topk_round(pair):
                        for x, i in enumerate(pair):
                            dve.wait_ge(tk_s.sem, tk_s.n - 1) if tk_s.n > 1 else None
                            tk_s.did(dve.max(m8[0:ROWS[i], x, :], area(i)))
                        for x, i in enumerate(pair):
                            dve.wait_ge(tk_s.sem, tk_s.n - 1)
                            tk_s.did(dve.match_replace(area(i), m8[0:ROWS[i], x, :], area(i), GONE))

                    def to_bias(pair):
                        for i in pair:
                            dve.wait_ge(tk_s.sem, tk_s.n)
                            tk_s.did(dve.tensor_scalar(area(i), area(i), CUT, NEG, ALU.is_gt, ALU.mult))
                        for i in pair:
                            dve.wait_ge(tk_s.sem, tk_s.n)
                            causal(i, tk_s)

                    n1 = sum(1 for q in PIECES if q[0] <= 2)

                    def piece(p):
                        gather(p)
                        if p in (n1 - 1, len(PIECES) - 1):
                            dve.wait_ge(acc_s.sem, acc_s.n)
                            for i in (1, 2) if p == n1 - 1 else (3, 4):
                                causal(i, acc_s)

                    def tap(j):
                        for c in range(2):
                            w = prm[:, 16 + CONV_W * c + j:17 + CONV_W * c + j]
                            if j == 0:
                                dve.wait_ge(cv_s.sem, 2 * c + 2)
                                conv_s.did(dve.tensor_scalar(cc[:, c, 0:NTOK], uext[:, c, 0:NTOK], w, prm[:, 10 + c:11 + c], ALU.mult, ALU.add))
                            else:
                                dve.wait_ge(conv_s.sem, 2 * j + c - 1)
                                conv_s.did(stt(cc[:, c, 0:NTOK], uext[:, c, j:j + NTOK], w, cc[:, c, 0:NTOK], ALU.mult, ALU.add))

                    p = 0
                    for m in (0, 2, 1, 3):
                        for h in range(2):
                            u = ("conv", m, h)
                            wait_unit(dve, u)
                            src = R[:, bank(u), 0:HALF]
                            if m < 2:
                                evD.did(stt(bufA[:, m, tok(h)], src, 0.5, row[:, tok(h)]))
                            else:
                                evD.did(dve.tensor_tensor(bufB[:, m - 2, tok(h)], src, row[:, tok(h)], ALU.mult))
                            if m:
                                for _ in range(IX_CONV):
                                    piece(p)
                                    p += 1
                        if m == 1:
                            conv_in(0)
                    conv_in(1)
                    j = 0
                    for i in range(NT):
                        kq_sum(i)
                        for _ in range(IX_K):
                            piece(p)
                            tap(j)
                            p, j = p + 1, j + 1
                    for i in range(NT):
                        kq_sum(NT + i)
                        for _ in range(IX_Q[i]):
                            piece(p)
                            tap(j)
                            p, j = p + 1, j + 1
                        if j < CONV_W:
                            tap(j)
                            j += 1
                        topk_round((1, 2))
                    assert j == CONV_W and p == len(PIECES) and acc_s.n == ACC_END
                    for c in range(2):
                        taps = prm[:, 16 + CONV_W * c:16 + CONV_W * (c + 1)].unsqueeze(1).broadcast_to([128, N_SAMPLE, CONV_W])
                        tmp = gt[:, c, 0:N_SAMPLE * CONV_W].rearrange("p (b j) -> p b j", b=N_SAMPLE)
                        conv_s.did(dve.tensor_tensor(tmp, uxs[:, c, :, :], taps, ALU.mult))
                    topk_round((1, 2))
                    for c in range(2):
                        tmp = gt[:, c, 0:N_SAMPLE * CONV_W].rearrange("p (b j) -> p b j", b=N_SAMPLE)
                        dve.wait_ge(conv_s.sem, 2 * CONV_W + 1 + c)
                        conv_s.did(dve.reduce_sum(wsum[:, c, :], tmp, AX.X))
                    topk_round((1, 2))
                    for c in range(2):
                        dve.wait_ge(conv_s.sem, 2 * CONV_W + 3 + c)
                        conv_s.did(dve.tensor_scalar(cc[:, c, NTOK:TOK], wsum[:, c, :], prm[:, 10 + c:11 + c], None, ALU.add))
                    for _ in range(NT + 2, ROUNDS):
                        topk_round((1, 2))
                    to_bias((1, 2))
                    tb12 = tk_s.n

                    rounds = [0]

                    def more_topk():
                        if rounds[0] < ROUNDS:
                            topk_round((3, 4))
                            rounds[0] += 1

                    def gate(g):
                        u = GATES[g]
                        dve.wait_ge(gt_s.sem, g + 1)
                        dst = yT[:, u[1], tok(u[0][2])]
                        gate_s.did(stt(dst, gt[:, g % 2, :], 1.0, dst, ALU.add))

                    def gate_in(u, ch):
                        wait_unit(dve, u)
                        evD.did(dve.tensor_tensor(yT[:, ch, tok(u[2])], R[:, bank(u), 0:HALF], row[:, tok(u[2])], ALU.mult))

                    def take(u):
                        kind, m, h = u
                        src = R[:, bank(u), 0:HALF]
                        if u in GATE_OF:
                            gate_in(u, GATES[GATE_OF[u]][1])
                        elif kind == "ub":
                            wait_unit(dve, u)
                            if h == 0:
                                evD.did(dve.tensor_tensor(ubx[:, m, POOL_STATE:POOL_STATE + HALF], src, row[:, tok(0)], ALU.mult))
                            else:
                                k = NTOK - HALF
                                dve.tensor_tensor(ubx[:, m, POOL_STATE + HALF:POOL_STATE + NTOK], src[:, 0:k], row[:, HALF:NTOK], ALU.mult)
                                evD.did(dve.tensor_tensor(ubs[:, m, :, POOL_STATE], src[:, k:HALF], row[:, NTOK:TOK], ALU.mult))
                        elif kind == "mean":
                            wait_unit(dve, u)
                            dve.wait_ge(conv_s.sem, conv_s.n)
                            evD.did(stt(cc[:, :, tok(h)], src.unsqueeze(1).broadcast_to([128, 2, HALF]), -1.0 / D_C,
                                        cc[:, :, tok(h)], ALU.mult, ALU.add))
                        elif kind == "lnsum":
                            wait_unit(dve, u)
                            evD.did(dve.tensor_scalar(lnv[0:SR, 0:NT], R[0:SR, bank(u), 0:NT], 1.0 / D_C, EPS, ALU.mult, ALU.add))
                        elif kind == "pool":
                            wait_unit(dve, u)
                            dst = yT[:, 4 + m, tok(h)]
                            evD.did(stt(dst, src, prm_h[:, m:m + 1], dst))
                        elif kind == "out":
                            wait_unit(dve, u)
                            evD.did(dve.tensor_tensor(xT[:, m, tok(h)], src, xT[:, m, tok(h)], ALU.add))

                    def pool_differences():
                        dve.wait_ge(ps_s.sem, 4)
                        first = slice(POOL_STATE, 2 * POOL_STATE)
                        rest = slice(2 * POOL_STATE, POOL_STATE + NTOK)
                        for half, src in ((slice(0, 64), bufA), (slice(64, 128), bufB)):
                            cnt = cst[half, K_CNT:K_CNT + 32].rearrange("p (c t) -> p c t", c=2)[:, :, 0:POOL_STATE]
                            pd_s.did(dve.tensor_tensor(bufA[half, :, first], src[half, :, first], cnt, ALU.mult))
                            for c in range(2):
                                pd_s.did(stt(bufA[half, c, rest], src[half, c, rest], cst[half, K_WIN + c:K_WIN + c + 1],
                                             ubx[half, c, rest], ALU.mult, ALU.subtract))
                            dve.wait_ge(pd_s.sem, pd_s.n - 2)
                            pd_s.did(dve.tensor_tensor(bufA[half, :, first], bufA[half, :, first], ubx[half, :, first], ALU.subtract))
                        for c in range(2):
                            for k in range(2):
                                rows = slice(64 * k, 64 * k + 64)
                                win = WINDOWS[2 * c + k]
                                pd_s.did(dve.reduce_sum(wsum[rows, c, :], ubs[rows, c, :, 16 - win:16], AX.X))
                        dve.wait_ge(pd_s.sem, pd_s.n)
                        for c in range(2):
                            pd_s.did(stt(bufA[:, c, POOL_STATE + NTOK:POOL_STATE + TOK], wsum[:, c, :], cst[:, K_WIN + c:K_WIN + c + 1],
                                         ubs[:, c, :, POOL_STATE], ALU.mult, ALU.subtract))
                        assert pd_s.n == PD_END

                    def page_scores(n):
                        dve.wait_ge(kp_s.sem, n + 1)
                        b, pg = divmod(n, 2)
                        kr_s.did(dve.reduce_sum(ssm[:, pg, 8 * b:8 * b + 8], KV[:, n % 4, :].rearrange("p (h d) -> p h d", h=HEADS), AX.X))

                    def swish():
                        dve.wait_ge(gate_s.sem, gate_s.n)
                        for c in range(2):
                            dve.wait_ge(lth_s.sem, c + 1)
                            ln_s.did(dve.tensor_scalar(cc[:, c, :], cc[:, c, :], prm[:, 12 + c:13 + c], prm[:, 14 + c:15 + c], ALU.mult, ALU.add))
                        for c in range(2):
                            dve.wait_ge(ln_s.sem, 2 + c)
                            ln_s.did(stt(qkT[:, c, :], qkT[:, c, :], 1.0, cc[:, c, :], ALU.add))
                        for c in range(2):
                            dve.wait_ge(ln_s.sem, 4 + c)
                            ln_s.did(stt(yT[:, 6 + c, :], qkT[:, c, :], 0.25, yT[:, 6 + c, :]))
                        assert ln_s.n == LN_END

                    def sd(make, name=None):
                        if sd_s.n:
                            dve.wait_ge(sd_s.sem, sd_s.n)
                        sd_s.did(make())
                        if name:
                            assert SD[name] == sd_s.n, (name, sd_s.n)

                    flat = smp[:, 0:128].rearrange("p (g x) -> p g x", g=2)
                    t8 = bufB[0:8, 1, 0:512].rearrange("p (h d) -> p h d", h=8)
                    chosen = sc8[:, 0:PAST + 1]
                    logits = A[0:64, 3, 0:PAST + 1]

                    Rf = R[:, :, :].rearrange("p k n -> p (k n)")
                    dve.wait_ge(kx_s, 96)
                    dve.wait_ge(row_z, 16)
                    dve.wait_ge(zq_s, 32)
                    dve.wait_ge(acc_s.sem, ACC_END)
                    for n in range(len(ITEMS) + PIPE + 1):
                        if n < len(ITEMS):
                            i, h = ITEMS[n]
                            r, w = ROWS[i], WIDTH[i]
                            if n in (HEADS, 3 * HEADS):
                                dve.wait_ge(tk_s.sem, tb12 if n == HEADS else tb34)
                            dve.wait_ge(S_s.sem, n + 1)
                            if n >= 2:
                                dve.wait_ge(P_s.sem, n - 1)
                            b = tri[0:r, 0:r] if i == 0 else bias[0:r, i - 1, SENT:SENT + w]
                            lo = 1024 + (512 * (n % 2) if w <= 512 else 0)
                            ttr_s.did(dve.tensor_tensor_reduce(out=sb_scores[0:r, n % 2, 0:w], in0=Rf[0:r, lo:lo + w], in1=b,
                                                               scale=-0.125, scalar=BIG, op0=ALU.add, op1=ALU.min,
                                                               accum_out=mn[0:r, n % 2:n % 2 + 1]))
                        if n >= 11 and (n - 11) % 8 == 0:
                            i = (n - 11) // 8
                            r = ROWS[i]
                            dve.wait_ge(PV_s.sem, 8 * i + 8)
                            rec_s.did(dve.reciprocal(rrec[0:r, :], rsum[0:r, i % 2, :]))
                            dve.wait_ge(rec_s.sem, i + 1)
                            if i:
                                wait_unit(dve, ("turn", i - 1, 0))
                            on_s.did(dve.tensor_tensor(ksq[0:r, 0, :].rearrange("p (h d) -> p h d", h=HEADS),
                                                       A[0:r, 2, :].rearrange("p (h d) -> p h d", h=HEADS),
                                                       rrec[0:r, :].unsqueeze(2).broadcast_to([r, HEADS, HD]), ALU.mult))
                        if n and PLAN[n - 1] and PLAN[n - 1][0] in GATE_OF:
                            gate(GATE_OF[PLAN[n - 1][0]])
                        more_topk()
                        if n == ROUNDS:
                            to_bias((3, 4))
                            tb34 = tk_s.n
                        if n == SX["pool_diff"]:
                            pool_differences()
                        if n == SX["ln_diag"]:
                            dve.wait_ge(lnp_s.sem, 1)
                            dve.wait_ge(pd_s.sem, PD_END)
                            for i in range(NT):
                                r = ROWS_P[i]
                                lnd_s.did(dve.tensor_scalar(ln_dg[0:r, i, 0:r], ident[0:r, 0:r], lnr[0:r, i:i + 1], None, ALU.mult))
                        if n == SX["ln_mul"]:
                            wait_evac(dve, ("lnrow", 0, 1))
                            ln_s.did(dve.tensor_tensor(cc[:, :, :], cc[:, :, :], lnrow.unsqueeze(1).broadcast_to([128, 2, TOK]), ALU.mult))
                        if n == SX["swish"]:
                            swish()
                        b = n - SX["pages"]
                        if 0 <= b < 8:
                            dve.wait_ge(ixp_s.sem, b + 1)
                            ixr_s.did(dve.reduce_sum(ds[:, :, b, :], ixp.rearrange("p (g h d) -> p g h d", g=2, h=IH), AX.X))
                            page_scores(2 * b)
                            page_scores(2 * b + 1)
                        if n == SX["index"]:
                            dve.wait_ge(wbc_s, 16)
                            dve.wait_ge(ixr_s.sem, 8)
                            sd(lambda: stt(flat, flat, 0.0, wbc.unsqueeze(1).broadcast_to([128, 2, 64]), ALU.max))
                            sd(lambda: dve.reduce_sum(isc.rearrange("p (g b) -> p g b", g=2), ds[:, :, :, :], AX.X))
                            sd(lambda: dve.tensor_scalar(isc, isc, 1.0 / 16, None, ALU.mult), "isc")
                            sd(lambda: dve.tensor_tensor(t8[:, :, 0:ID], zis[:, 0:256].rearrange("p (h d) -> p h d", h=IH),
                                                         zis[:, 256:288].unsqueeze(1).broadcast_to([8, IH, ID]), ALU.mult))
                            sd(lambda: dve.reduce_sum(d8, t8[:, :, 0:ID], AX.X))
                            sd(lambda: stt(e8, d8, 0.0, zis[:, 384:392], ALU.max))
                            sd(lambda: dve.reduce_sum(sc8[:, 256:257], e8, AX.X))
                            sd(lambda: dve.tensor_scalar(sc8[:, 256:257], sc8[:, 256:257], 1.0 / 16, None, ALU.mult))
                        if n == SX["index_turn"]:
                            dve.wait_ge(row_q, 16)
                            dve.wait_ge(row_k, 16)
                            sd(lambda: dve.tensor_tensor(t8, rows8[:, 0:512].rearrange("p (h d) -> p h d", h=8),
                                                         rows8[:, 512:1024].rearrange("p (h d) -> p h d", h=8), ALU.mult))
                            sd(lambda: dve.reduce_sum(snw, t8, AX.X))
                            sd(lambda: dve.tensor_tensor(sn.rearrange("p (b h) -> p b h", b=8), E8.rearrange("p (b h) -> p b h", b=8),
                                                         snw.unsqueeze(1).broadcast_to([8, 8, 8]), ALU.mult))
                            dve.wait_ge(sit_s.sem, 1)
                            sd(lambda: dve.tensor_copy(sc8[:, 0:256], A[0:8, 3, 0:256]))
                        if 0 <= n - SX["topk"] < 4:
                            for _ in range(TOPK_S // 32):
                                sd(lambda: dve.max(m8s, chosen))
                                sd(lambda: dve.match_replace(chosen, m8s, chosen, GONE))
                        if n == SX["topk"] + 3:
                            sd(lambda: dve.tensor_scalar(chosen, chosen, CUT, NEG, ALU.is_gt, ALU.mult), "logit_in")
                        if n == SX["logits"]:
                            dve.wait_ge(slog_s.sem, 1)
                            sd(lambda: dve.reduce_max(smx, logits, AX.X))
                            sd(lambda: dve.tensor_scalar(snm, smx, -0.125, None, ALU.mult), "negmax")
                        if n == SX["norm"]:
                            dve.wait_ge(sexp_s.sem, 1)
                            sd(lambda: dve.reciprocal(srr, srs))
                            sd(lambda: dve.tensor_scalar(pn[:, 0:257], pn[:, 0:257], srr, None, ALU.mult))
                            sd(lambda: dve.tensor_scalar(etp, ET8, pn[:, 256:257], None, ALU.mult), "etp")
                        if n == SX["gate"]:
                            dve.wait_ge(spv_s.sem, 16)
                            for k in range(2):
                                rows = slice(64 * k, 64 * k + 64)
                                dst = yT[rows, 0:4, NTOK:TOK]
                                src = A[rows, 3, 0:64].rearrange("p (c b k) -> p c b k", c=4, b=8)[:, :, :, k]
                                ys_s.did(stt(dst, src, 0.5, dst))
                        if n < len(PLAN):
                            for u in PLAN[n]:
                                if u[0] not in ON_ACT:
                                    take(u)
                        for at, tile, lo, hi in ((31, 2, 0, HALF), (37, 3, HALF, START[4]), (45, 4, START[4], NTOK)):
                            if n == at:
                                wait_evac(dve, ("turn", tile, 0))
                                dve.wait_ge(gate_s.sem, len(GATES))
                                y_s.did(stt(yT[:, 0:4, lo:hi], qT[:, :, lo:hi], 0.5, yT[:, 0:4, lo:hi]))
                    for m in range(KC):
                        take(("out", m, 1))

            for s in layer_sems:
                nc.gpsimd.sem_clear(s)
            nc.all_engine_barrier()

        with nc.Block() as block:
            spans = [(N_META + 128 * i, 128) for i in range(4)] + [(NTOK, N_SAMPLE)]

            @block.tensor
            def _(pe):
                n = 0
                for i, (c0, r) in enumerate(spans):
                    for g in range(2):
                        if n >= 4:
                            pe.wait_ge(pre["post_act"] if n % 2 else pre["post_dve"], (n - 4) // 2 + 1)
                        for j in range(4):
                            m = pe.transpose(R[0:r, n % 4, 128 * j:128 * j + 128], xT[:, 4 * g + j, c0:c0 + r], ident)
                        m.then_inc(pre["post_turned"], 1)
                        n += 1

            @block.vector
            def _(dve):
                for i, (c0, r) in enumerate(spans):
                    dve.wait_ge(pre["post_turned"], 2 * i + 1)
                    dve.tensor_copy(yout[0:r, i, 0:512], R[0:r, (2 * i) % 4, :]).then_inc(pre["post_dve"], 1)

            @block.scalar
            def _(act):
                for i, (c0, r) in enumerate(spans):
                    act.wait_ge(pre["post_turned"], 2 * i + 2)
                    act.activation(yout[0:r, i, 512:1024], R[0:r, (2 * i + 1) % 4, :], ACT.Copy).then_inc(pre["post_act"], 1)

            @block.sync
            def _(sp):
                for i, (c0, r) in enumerate(spans):
                    sp.wait_ge(pre["post_dve"], i + 1)
                    sp.wait_ge(pre["post_act"], i + 1)
                    dst = (o["y_prompt"].rearrange("b t d -> (b t) d")[128 * i:128 * i + 128] if i < 4
                           else o["y_sample"].rearrange("b t d -> (b t) d"))
                    sp.dma_start(dst, yout[0:r, i, :]).then_inc(pre["post_out"], 16)
                sp.wait_ge(pre["post_out"], 16 * len(spans))


_INS = ["x_prompt", "x_sample", "cache_k", "cache_v", "cache_kidx", "state_pool", "state_conv", "page_table",
        "meta_tokens", "norm_g", "w_in", "q_norm_g", "k_norm_g", "pool_w", "pool_scale", "conv_w", "conv_b",
        "conv_norm_g", "conv_norm_b", "w_out"]
_OUTS = [("y_prompt", (1, SEQ, D_MODEL)), ("y_sample", (N_SAMPLE, 1, D_MODEL)),
         ("new_k_prompt", (DEPTH, 1, NTOK, HEADS, HD)), ("new_v_prompt", (DEPTH, 1, NTOK, HEADS, HD)),
         ("new_kidx_prompt", (DEPTH, 1, NTOK, ID)), ("new_pool_prompt", (DEPTH, 1, POOL_STATE, D_B)),
         ("new_conv_prompt", (DEPTH, 1, CONV_STATE, D_C)), ("new_k_sample", (DEPTH, N_SAMPLE, 1, HEADS, HD)),
         ("new_v_sample", (DEPTH, N_SAMPLE, 1, HEADS, HD)), ("new_kidx_sample", (DEPTH, N_SAMPLE, 1, ID)),
         ("new_pool_sample", (DEPTH, N_SAMPLE, POOL_STATE, D_B)), ("new_conv_sample", (DEPTH, N_SAMPLE, CONV_STATE, D_C))]


def kernel(**inputs):
    import concourse.bacc as bacc
    from concourse.bass_utils import run_bass_kernel_spmd

    nc = bacc.Bacc("TRN2", target_bir_lowering=False, num_devices=1)
    arrays, a, o = {}, {}, {}
    given = {name: np.ascontiguousarray(inputs[name]) for name in _INS}
    given["consts"] = constants()
    for name, x in given.items():
        arrays[f"in_{name}"] = x
        a[name] = nc.dram_tensor(f"in_{name}", x.shape, mybir.dt.from_np(x.dtype), kind="ExternalInput").ap()
    for name, shape in _OUTS:
        o[name] = nc.dram_tensor(f"out_{name}", shape, F32, kind="ExternalOutput").ap()
    a["z_rows"] = nc.dram_tensor("z_rows", (N_SAMPLE, 392), F32, kind="Internal").ap()
    a["q_rows"] = nc.dram_tensor("q_rows", (N_SAMPLE, HEADS * HD), F32, kind="Internal").ap()
    program(nc, a, o)
    r = run_bass_kernel_spmd(nc, [arrays], core_ids=[0])
    return tuple(r.results[0][f"out_{name}"] for name, _ in _OUTS)
```

```python
from contextlib import ExitStack

import numpy as np

import concourse.bass as bass
from concourse import mybir

F32 = mybir.dt.float32
F32R = mybir.dt.float32r
I32 = mybir.dt.int32
ALU = mybir.AluOpType
ACT = mybir.ActivationFunctionType
AX = mybir.AxisListType

D_MODEL, SEQ, N_META, DEPTH = 1024, 512, 16, 2
N_SAMPLE, PAST, PAGE = 8, 256, 128
N_PAGES = PAST // PAGE
HEADS, HD = 8, 64
IH, ID = 8, 32
TOPK_P, TOPK_S = 132, 64
THETA = 500000.0
EPS = 1e-6
WINDOWS = (2, 4, 8, 16)
POOL_STATE, CONV_STATE, CONV_W = 15, 30, 31
D_B = D_C = 256

NTOK = SEQ + N_META
TOK = NTOK + N_SAMPLE
HALF = TOK // 2
KC = D_MODEL // 128
START = [0, 107, 214, 320, 426]
ROWS = [107, 107, 106, 106, 102]
NT = len(START)
ROWS_P = ROWS[:4] + [ROWS[4] + N_SAMPLE]
S0 = ROWS[4]
MAXR = 107
SR = 110
WIDTH = [START[i] + ROWS[i] for i in range(NT)]
SENT = (-TOPK_P) % 8
ROUNDS = (TOPK_P + SENT) // 8
NEG, GONE, CUT, BIG = -1e30, -3e38, -2e38, 3e38

C_Q, C_K, C_V, C_GA, C_I, C_UB, C_GB, C_CV, C_GC = 0, 512, 1024, 1536, 2048, 2344, 2600, 2856, 3368
GROUPS = [("cv", C_CV, 256, 4), ("cg", C_CV + 256, 256, 4), ("idx", C_I, 296, 2), ("k", C_K, 512, 2), ("q", C_Q, 512, 2),
          ("v", C_V, 512, 2), ("ub", C_UB, 256, 4), ("gb", C_GB, 256, 4), ("gc", C_GC, 256, 4), ("ga0", C_GA, 256, 4),
          ("ga1", C_GA + 256, 256, 4)]
G = {name: g for g, (name, _, _, _) in enumerate(GROUPS)}
SLOTS_OF = [KC // per for _, _, _, per in GROUPS]
FIRST = [sum(SLOTS_OF[:g]) for g in range(len(GROUPS) + 1)]
LOADS = [(g, q) for g in range(len(GROUPS)) for q in range(SLOTS_OF[g])] + [(len(GROUPS) + g, q) for g in range(2) for q in range(2)]
LOAD_OF = {x: m for m, x in enumerate(LOADS)}
W_SLOTS = 6
REST_ON_POOL = [FIRST[G["q"]], FIRST[G["q"]] + 1, FIRST[G["v"]], FIRST[G["v"]] + 1] + list(range(FIRST[G["ub"]], FIRST[-1]))

PIPE = 5


def plan():
    fill = [("ub", m, h) for m in (0, 1) for h in range(2)] + [("mean", 0, 0), ("mean", 0, 1), ("ub", 2, 0), ("ub", 2, 1),
            ("lnsum", 0, 0), ("ub", 3, 0), ("ub", 3, 1), ("gc", 0, 0), ("lnrow", 0, 0), ("lnrow", 0, 1), ("gc", 0, 1),
            ("gc", 1, 0), ("gc", 1, 1)] + [("ga", m, h) for m in range(4) for h in range(2)]
    steps = [[] for _ in range(NT * HEADS + PIPE)]
    free = [n for n in range(30) if n < 8 or n % 4 != 3]
    for n, u in zip(free, fill):
        steps[n].append(u)
    assert len(free) >= len(fill)
    steps[30] += [("pool", m, h) for m in range(2) for h in range(2)]
    for n, m in zip((31, 32, 33, 34, 35, 36, 37, 38), range(KC)):
        steps[n].append(("out", m, 0))
    for n, m in zip((39, 40, 41, 42, 43, 43, 44, 44), range(KC)):
        steps[n].append(("out", m, 1))
    for i in range(NT):
        steps[8 * i + 12].append(("turn", i, 0))
    return steps


PLAN = plan()
OUT_PART = [(0, HALF), (HALF, START[4]), (START[4], TOK)]
EARLY = ([("conv", m, h) for m in range(4) for h in range(2)]
         + [("idx", i, 0) for i in range(NT)]
         + [(n, i, 0) for n in ("k", "q", "v") for i in range(NT)])
UNITS = EARLY + [u for step in PLAN for u in step] + [("out", m, 2) for m in range(KC)]
NUM = {u: n for n, u in enumerate(UNITS)}
ON_ACT = ("idx", "k", "v", "q", "lnrow", "turn")
LAST_UNIT = [("conv", 1, 1), ("conv", 3, 1), ("idx", 4, 0), ("k", 4, 0), ("q", 4, 0), ("v", 4, 0), ("ub", 1, 1), ("ub", 3, 1),
             ("gc", 1, 1), ("ga", 1, 1), ("ga", 3, 1)]

PIECES = [(i, h, a, b) for pair in ((1, 2), (3, 4)) for h in range(IH) for i in pair
          for a, b in ([(0, WIDTH[i])] if WIDTH[i] <= 512 else [(0, WIDTH[i] // 2), (WIDTH[i] // 2, WIDTH[i])])]
ITEMS = [(i, h) for i in range(NT) for h in range(HEADS)]

K_ID, K_ROT, K_CNT, K_WIN, K_E, K_ET, K_TRI = 0, 128, 128 + 48 * NT, 160 + 48 * NT, 162 + 48 * NT, 226 + 48 * NT, 234 + 48 * NT
K_END = K_TRI + MAXR
ACC_END = len(PIECES) + 4


GATES = [(u, {"ub": 2, "gc": 6, "ga": 0}[u[0]] + u[1]) for step in PLAN for u in step
         if u[0] in ("gc", "ga") or u[0] == "ub" and u[1] >= 2]
GATE_OF = {u: g for g, (u, _) in enumerate(GATES)}
IX_K, IX_Q = 4, 4
HIGH_AT = {1: 22, 2: 23, 3: 24, 4: 25, 7: 26, 8: 27, 13: 28, 14: 29}
TAPS_IDX, TAPS_K, TAPS_Q, ROUNDS_V = 11, (2, 2, 3, 2, 3), (2, 2, 2, 1, 1), (3, 3, 2, 2, 2)
NO_ROUND = (9, 10, 11, 12, 15)
CONV_END, PD_END, LN_END = 2 * CONV_W + 6, 14, 7
SD = {"isc": 3, "logit_in": 29, "negmax": 31, "etp": 34}
SX = {"pool_diff": 9, "pool_diff2": 10, "ln_diag": 12, "ln_mul": 15, "ln_tanh": 16, "pages": 18, "swish": 20, "index": 26,
      "index_turn": 27, "topk": 28, "logits": 32, "exp": 33, "norm": 34, "turn": 35, "keep": 36, "pv": 37, "gate": 45}



def constants():
    c = np.zeros((128, K_END), np.float32)
    c[:, :128] = np.eye(128)
    for i in range(NT):
        pos = np.full(128, float(PAST), np.float32)
        pos[:ROWS[i]] = START[i] + np.arange(ROWS[i])
        o = K_ROT + 48 * i
        for half, off in ((8, 0), (4, 32)):
            inv = np.float32(THETA) ** (-(np.arange(half, dtype=np.float32) / np.float32(half)))
            ang = pos[:, None] * inv[None, :].astype(np.float32)
            cos, sin = np.cos(ang), np.sin(ang)
            c[:, o + off:o + off + 4 * half] = np.concatenate([cos, cos, -sin, sin], 1)
    for m in range(2):
        for g in range(2):
            win = WINDOWS[2 * m + g]
            rows = slice(64 * g, 64 * g + 64)
            c[rows, K_CNT + 16 * m:K_CNT + 16 * m + 16] = 1.0 / np.minimum(np.arange(16) + 1, win)
            c[rows, K_WIN + m] = 1.0 / win
    for b in range(8):
        c[b, K_E + 8 * b:K_E + 8 * b + 8] = 1
        c[8 * b:8 * b + 8, K_ET + b] = 1
    t = np.arange(MAXR)
    c[:MAXR, K_TRI:K_TRI + MAXR] = np.where(t[None, :] <= t[:, None], 0, NEG)
    return c


class Stage:

    def __init__(self, sem):
        self.sem, self.n = sem, 0

    def did(self, ins):
        ins.then_inc(self.sem, 1)
        self.n += 1
        return ins


def program(nc, a, o):
    ctx = ExitStack()
    with ctx:
        def sb(name, *shape, dt=F32):
            return ctx.enter_context(nc.sbuf_tensor(name, list(shape), dt))

        def ps(name, *shape):
            return ctx.enter_context(nc.psum_tensor(name, list(shape), F32))

        layer_sems, loads = [], []

        def sem(name):
            s = ctx.enter_context(nc.semaphore(name))
            layer_sems.append(s)
            return s

        def stage(name):
            return Stage(sem(name))

        cst = sb("cst", 128, K_END)
        ident = cst[:, 0:128]
        E8 = cst[0:8, K_E:K_E + 64]
        ET8 = cst[0:64, K_ET:K_ET + 8]
        tri = cst[:, K_TRI:K_TRI + MAXR]
        ones = sb("ones", 128, 128)
        pow_e = sb("pow_e", 128, 8)
        table = sb("table", 1, N_SAMPLE * N_PAGES, dt=I32)
        params = sb("params", 128, DEPTH, 78)
        prm = sb("prm", 128, 78)
        prm_h = sb("prm_h", 128, 8)
        x_hi = sb("x_hi", 128, KC, TOK, dt=F32R)
        x_lo = sb("x_lo", 128, KC, TOK, dt=F32R)
        yT = sb("yT", 128, KC, TOK)
        with nc.sbuf_tensor("W_r", [128, W_SLOTS, 4, 512], F32R) as W_r:
            pass
        W = sb("W", 128, W_SLOTS, 4, 512)
        kT = sb("kT", 128, 4, TOK)
        qT = sb("qT", 128, 4, TOK)
        V = sb("V", 128, NT, 512)
        bias = sb("bias", 128, NT - 1, SENT + NTOK)
        zi = sb("zi", 128, NT, 392)
        qkT = sb("qkT", 128, 3, TOK)
        kz = sb("kz", 128, 3, 512)
        ksq = sb("ksq", 128, 2, 512)
        gam = sb("gam", 128, 2, 64)
        uext = sb("uext", 128, 2, CONV_STATE + NTOK)
        uxs = sb("uxs", 128, 2, N_SAMPLE, CONV_W)
        bufA = sb("bufA", 128, 2, 552)
        bufB = sb("bufB", 128, 2, 552)
        cc = sb("cc", 128, 2, TOK)
        ubx = sb("ubx", 128, 2, POOL_STATE + NTOK)
        ubs = sb("ubs", 128, 2, N_SAMPLE, 16)
        pwb = sb("pwb", 128, 2, 128)
        row = sb("row", 128, TOK)
        rel = sb("rel", 128, 2, 552)
        gt = sb("gt", 128, 2, HALF)
        small = sb("small", 128, 192)
        kic = sb("kic", 128, N_SAMPLE, N_PAGES, ID)
        KV = sb("KV", 128, 4, 512)
        rows8 = qkT[0:8, :, :].rearrange("p a b -> p (a b)")[:, 0:3 * 512]
        cc_rows = cc[0:8, :, :].rearrange("p a b -> p (a b)")
        zis = cc_rows[:, 0:392]
        sc8 = cc_rows[:, 512:784]
        zi_flat = zi[:, :, :].rearrange("p a b -> p (a b)")
        sb_scores = zi_flat[:, 0:1104].rearrange("p (a b) -> p a b", a=2)
        ibb = zi_flat[:, 1104:1104 + 784].rearrange("p (a b) -> p a b", a=2)
        pT = uext[:, :, :].rearrange("p a b -> p (a b)")[:, 0:2 * NT * MAXR].rearrange("p (a b) -> p a b", a=2)
        ixp = bufB[:, 1, 0:512]
        smp = kz[:, 0, :]
        pn = ksq[0:64, 1, 0:260]
        p64 = ksq[0:8, 1, 260:452]
        rot_tmp = sb("rot_tmp", 128, 256)
        ds = smp[:, 0:128].rearrange("p (g b h) -> p g b h", g=2, b=8)
        ssm = smp[:, 128:256].rearrange("p (g x) -> p g x", g=2)
        wbc = smp[:, 256:320]
        pts = smp[:, 320:448].rearrange("p (g x) -> p g x", g=2)
        sn = p64[:, 0:64]
        pd = p64[:, 64:128]
        qb = ubx[:, :, :].rearrange("p a b -> p (a b)")[:, 0:1024].rearrange("p (a b) -> p a b", a=2)
        lnrow = qkT[:, 2, :]
        ln_dg = bufB[:, 0, 0:NT * SR].rearrange("p (a b) -> p a b", a=NT)
        conv_new = kz[:, 1, :]
        pool_new = kz[:, 2, :]
        st_in = bufA[:, :, 0:256]
        stp_in = bufB[:, 0, 0:256]
        ssum = small[:, 0:8]
        rinv = small[:, 8:16]
        mn = small[:, 16:18]
        rsum = small[:, 18:34].rearrange("p (a b) -> p a b", a=2)
        rrec = small[:, 34:42]
        kss = small[:, 42:58].rearrange("p (a b) -> p a b", a=2)
        krn = small[:, 58:74].rearrange("p (a b) -> p a b", a=2)
        m8 = small[:, 74:90].rearrange("p (a b) -> p a b", a=2)
        lnv = small[:, 90:98]
        lnr = small[:, 98:106]
        wsum = small[:, 106:122].rearrange("p (a b) -> p a b", a=2)
        smx = small[0:64, 122:123]
        snm = small[0:64, 123:124]
        srs = small[0:64, 124:125]
        srr = small[0:64, 125:126]
        d8 = small[0:8, 126:134]
        e8 = small[0:8, 134:142]
        etp = small[0:64, 142:150]
        snw = small[0:8, 150:158]
        m8s = small[0:8, 158:166]
        isc = small[:, 166:182]
        diag = ksq[:, :, :].rearrange("p a b -> p (a b)")[:, 0:NT * SR].rearrange("p (a b) -> p a b", a=NT)

        R = ps("R", 128, 4, 512)
        A = ps("A", 128, 4, 512)

        xin = W[:, :, :, :].rearrange("p s k n -> p (s k n)")[:, 0:NT * D_MODEL].rearrange("p (i n) -> p i n", i=NT)
        yout = xin

        pre = {n: ctx.enter_context(nc.semaphore(n)) for n in
               ("pre_const", "pre_table", "pre_x", "pre_params", "pre_ones", "pre_turned", "pre_hi", "pre_kept", "pre_par_t",
                "pre_par_k", "post_turned", "post_act", "post_dve", "post_out", "post_sum_dve", "post_sum_pool")}
        pin = kz[:, 0, 0:DEPTH * 128].rearrange("p (l n) -> p l n", l=DEPTH)
        pcw = kz[:, 1, 0:DEPTH * 256].rearrange("p (l n) -> p l n", l=DEPTH)
        with nc.Block() as block:
            @block.sync
            def _(sp):
                sp.dma_start(cst[:], a["consts"]).then_inc(pre["pre_const"], 16)
                x = a["x_prompt"][0]
                sp.dma_start(xin[0:N_META, 0, :], a["meta_tokens"]).then_inc(pre["pre_x"], 16)
                for i in range(NT):
                    lo = max(START[i] - N_META, 0)
                    n = START[i] + ROWS[i] - N_META - lo
                    off = ROWS[i] - n
                    sp.dma_start(xin[off:ROWS[i], i, :], x[lo:lo + n, :]).then_inc(pre["pre_x"], 16)
                sp.dma_start(xin[S0:S0 + N_SAMPLE, 4, :], a["x_sample"].rearrange("b t d -> (b t) d")).then_inc(pre["pre_x"], 16)
                for l in range(DEPTH):
                    for name, r0, n in (("norm_g", 0, 8), ("pool_scale", 8, 2), ("conv_b", 10, 2),
                                        ("conv_norm_g", 12, 2), ("conv_norm_b", 14, 2)):
                        sp.dma_start(pin[r0:r0 + n, l, :], a[name][l].rearrange("(c p) -> c p", p=128)).then_inc(pre["pre_params"], 16)
                    sp.dma_start(pcw[0:CONV_W, l, :], a["conv_w"][l]).then_inc(pre["pre_params"], 16)
                sp.dma_start(table[:, :], a["page_table"].rearrange("b n -> (b n)").unsqueeze(0)).then_inc(pre["pre_table"], 16)
                sp.wait_ge(pre["pre_table"], 16)

            @block.gpsimd
            def _(pool):
                pool.memset(ones[:], 1.0).then_inc(pre["pre_ones"], 1)
                pool.memset(pow_e[:], -0.5).then_inc(pre["pre_ones"], 1)
                pool.wait_ge(pre["pre_ones"], 2)

            @block.tensor
            def _(pe):
                pe.wait_ge(pre["pre_const"], 16)
                pe.wait_ge(pre["pre_x"], 16 * (NT + 2))
                n = 0
                for i in range(NT):
                    for g in range(2):
                        if n >= 4:
                            pe.wait_ge(pre["pre_kept"], n - 3)
                        for j in range(4):
                            m = pe.transpose(R[:, n % 4, SR * j:SR * j + ROWS_P[i]],
                                             xin[0:ROWS_P[i], i, 128 * (4 * g + j):128 * (4 * g + j) + 128],
                                             ident[0:ROWS_P[i], 0:ROWS_P[i]])
                        m.then_inc(pre["pre_turned"], 1)
                        n += 1
                pe.wait_ge(pre["pre_params"], 16 * 6 * DEPTH)
                for l in range(DEPTH):
                    pe.transpose(A[:, l, 0:16], pin[0:16, l, :], ident[0:16, 0:16])
                    for m in range(2):
                        t = pe.transpose(A[:, l, 16 + 31 * m:47 + 31 * m], pcw[0:CONV_W, l, 128 * m:128 * m + 128],
                                         ident[0:CONV_W, 0:CONV_W])
                t.then_inc(pre["pre_par_t"], 1)

            @block.vector
            def _(dve):
                n = 0
                for i in range(NT):
                    for g in range(2):
                        dve.wait_ge(pre["pre_turned"], n + 1)
                        src = R[:, n % 4, 0:4 * SR].rearrange("p (j t) -> p j t", j=4)[:, :, 0:ROWS_P[i]]
                        part = (slice(None), slice(4 * g, 4 * g + 4), slice(START[i], START[i] + ROWS_P[i]))
                        dve.tensor_copy(x_hi[part], src).then_inc(pre["pre_hi"], 1)
                        dve.wait_ge(pre["pre_hi"], n + 1)
                        dve.tensor_tensor(x_lo[part], src, x_hi[part].bitcast(F32), ALU.subtract).then_inc(pre["pre_kept"], 1)
                        n += 1
                dve.wait_ge(pre["pre_par_t"], 1)
                for l in range(DEPTH):
                    dve.tensor_copy(params[:, l, :], A[:, l, 0:78]).then_inc(pre["pre_par_k"], 1)
                dve.wait_ge(pre["pre_par_k"], DEPTH)

        w_in_s = [sem(f"w_loaded{s}") for s in range(W_SLOTS)]
        gam_s, pw_s, kic_s, state_s = sem("gamma_loaded"), sem("pool_w_loaded"), sem("kidx_loaded"), sem("states_loaded")
        zero_s = stage("pool_w_zeroed")
        misc0 = stage("constants_set")
        kv_s = [sem(f"kv_loaded{s}") for s in range(4)]
        unit_s, evA, evD = stage("unit_done"), stage("evac_act"), stage("evac_dve")
        sq_s, xs_s, xs2_s, prm_s = stage("squares"), stage("x_joined_dve"), stage("x_joined_pool"), stage("params_set")
        free_s, hi_s, lo_s, lo2_s, wg_s = stage("w_slot_free"), stage("w_high"), stage("w_rest_dve"), stage("w_rest_pool"), stage("w_scaled")
        res_s, ssq_s = stage("residual_step"), stage("squares_joined")
        stats_s, var_s, rinv_s, diag_s, row_t, row_s = (stage(n) for n in (
            "sumsq_done", "var_done", "rinv_done", "diag_done", "row_turned", "row_kept"))
        rope_s, idxz_s, idxt_s, idxk_s = stage("idx_rope"), stage("idx_ready"), stage("idx_turned"), stage("idx_kept")
        ix_s, rel_s, acc_s, tk_s = stage("idx_dots"), stage("idx_relu"), stage("idx_acc"), stage("topk_step")
        kss_s, krn_s, kzg_s, kz_s, kqt_s, kqk_s = (stage(n) for n in (
            "kq_sumsq", "kq_rinv", "kq_step", "kq_ready", "kq_turned", "kq_kept"))
        kq_mid = stage("kq_var")
        tanh_s, cv_s, conv_s = stage("tanh_done"), stage("conv_in_ready"), stage("conv_tap")
        gate_s = stage("gate_ready")
        st_t, st_k = stage("state_turned"), stage("state_kept")
        ps_s, pd_s = stage("pool_sum"), stage("pool_diff")
        ln_s, lnp_s, lnsq_s, lnst_s, lnt_s = (stage(n) for n in ("ln_step", "ln_rinv", "ln_square", "ln_sums", "ln_tanh"))
        nst_t, nst_k = stage("newstate_turned"), stage("newstate_kept")
        kp_s, kr_s = stage("page_product"), stage("page_scores")
        sd_s = stage("sample_step")
        ibb_s, qbl_s, wbc_s = [sem(f"idx_row{x}_spread") for x in range(2)], [sem(f"q_row{x}_spread") for x in range(2)], sem("idx_w_spread")
        kx_s = sem("kidx_stored")
        sit_s, slog_s, sexp_s, spt_s, spk_s, spv_s = (stage(n) for n in (
            "s_idx_turned", "s_logits", "s_exp", "s_probs_turned", "s_probs_kept", "s_pv_done"))
        S_s, ttr_s, P_s, T_s, PTk_s, PV_s, on_s, y_s, rec_s = (stage(n) for n in (
            "scores", "scores_biased", "probs", "probs_turned", "probs_kept", "pv_done", "o_normed", "att_gated", "rowsum_inv"))
        out_s = [sem(f"kz_stored{s}") for s in range(3)]
        store_s, row_q, row_k, row_v, row_z = sem("stored"), sem("q_row_kept"), sem("k_row_kept"), sem("v_row_kept"), sem("z_row_kept")
        rows_s = sem("sample_rows")
        gt_s, ixp_s, ixr_s, ys_s = stage("gate_tanh"), stage("idxb_product"), stage("idxb_dots"), stage("sample_gated")
        lnd_s, lth_s = stage("ln_diag"), stage("swish_tanh")
        tb_bias = {}

        ev_of = {u: (evA, n + 1) for n, u in enumerate(u for u in UNITS if u[0] in ON_ACT)}
        ev_of.update({u: (evD, n + 1) for n, u in enumerate(u for u in UNITS if u[0] not in ON_ACT)})

        def wait_evac(eng, u):
            s, n = ev_of[u]
            eng.wait_ge(s.sem, n)

        def w_raw(m, ring=W):
            g, _ = LOADS[m]
            _, _, n, per = GROUPS[g]
            if per == 2:
                return ring[:, m % W_SLOTS, 2:4, 0:n]
            return ring[:, m % W_SLOTS, 2:4, :].rearrange("p a (b n) -> p (a b) n", b=2)

        def w_high(m, ring=W):
            g, _ = LOADS[m]
            _, _, n, per = GROUPS[g]
            if per == 2:
                return ring[:, m % W_SLOTS, 0:2, 0:n]
            return ring[:, m % W_SLOTS, 0:2, :].rearrange("p a (b n) -> p (a b) n", b=2)

        def wait_loaded(eng, m):
            eng.wait_ge(w_in_s[m % W_SLOTS], 16 * (m // W_SLOTS + 1))

        def wait_split(eng, m):
            on_pool = sum(1 for x in REST_ON_POOL if x <= m)
            if m in REST_ON_POOL:
                eng.wait_ge(lo2_s.sem, on_pool)
            else:
                eng.wait_ge(lo_s.sem, m + 1 - on_pool)

        def bank(u):
            return NUM[u] % (4 if NUM[u] < len(EARLY) else 2)

        def wait_unit(eng, u):
            eng.wait_ge(unit_s.sem, NUM[u] + 1)

        with nc.Fori(0, DEPTH) as layer:
            L = bass.ds(layer, 1)

            def dr(name):
                t = a[name] if name in a else o[name]
                return t[L]

            def w_source(m):
                g, q = LOADS[m]
                _, c0, n, per = GROUPS[g]
                return dr("w_in").rearrange("a (k p) n -> p (a k) n", p=128)[:, per * q:per * q + per, c0:c0 + n]

            for s in w_in_s:
                nc.sync.sem_clear(s)
            for m in range(4):
                nc.sync.dma_start(w_raw(m), w_source(m)).then_inc(w_in_s[m % W_SLOTS], 16)
            for n, s in enumerate(x for x in layer_sems if x not in w_in_s):
                (nc.gpsimd, nc.vector, nc.scalar, nc.tensor)[n % 4].sem_clear(s)
            nc.all_engine_barrier()

            with nc.Block(no_gpsimd_drain=True) as block:
                @block.sync
                def _(sp):
                    stores = 0
                    z_dram, qkv_dram = a["z_rows"], a["qkv_rows"]

                    def w_load(m):
                        g, q = LOADS[m]
                        if m >= W_SLOTS:
                            og, oq = LOADS[m - W_SLOTS]
                            if oq == SLOTS_OF[og] - 1:
                                wait_unit(sp, LAST_UNIT[og])
                            else:
                                sp.wait_ge(free_s.sem, sum(1 for x in LOADS[:m - W_SLOTS + 1] if x[0] < len(GROUPS) and x[1] < SLOTS_OF[x[0]] - 1))
                        if g < len(GROUPS):
                            src, dst = w_source(m), w_raw(m)
                        else:
                            src = dr("w_out").rearrange("a (k p) n -> p (a k) n", p=128)[:, 4 * q:4 * q + 4, 512 * (g - len(GROUPS)):][:, :, 0:512]
                            dst = W[:, m % W_SLOTS, :, :]
                        sp.dma_start(dst, src).then_inc(w_in_s[m % W_SLOTS], 16)

                    def kv_load(n):
                        name = "cache_k" if n < 16 else "cache_v"
                        if 4 <= n < 20:
                            sp.wait_ge(kr_s.sem, n - 3)
                        elif n >= 20:
                            sp.wait_ge(spv_s.sem, n - 19)
                        src = a[name][L, bass.ds(pages[n % 16], 1)].rearrange("a b p h d -> (a b p) (h d)")
                        sp.dma_start(KV[:, n % 4, :], src).then_inc(kv_s[n % 4], 16)

                    def store(dst, src):
                        nonlocal stores
                        sp.dma_start(dst, src).then_inc(store_s, 16)
                        stores += 1

                    sp.dma_start(gam[:, 0, :], dr("k_norm_g").broadcast_to([128, HD])).then_inc(gam_s, 16)
                    sp.dma_start(gam[:, 1, :], dr("q_norm_g").broadcast_to([128, HD])).then_inc(gam_s, 16)
                    sc = dr("state_conv").rearrange("a (g b) j c -> (a g) (b j) c", g=2)
                    for g in range(2):
                        sp.dma_start(st_in[0:120, g, :], sc[g]).then_inc(state_s, 16)
                    sp.dma_start(stp_in[0:120, :], dr("state_pool").rearrange("a b j c -> (a b j) c")).then_inc(state_s, 16)
                    w_load(4)
                    w_load(5)
                    store(dr("new_conv_sample")[:, :, 0:CONV_STATE - 1, :], dr("state_conv")[:, :, 1:CONV_STATE, :])
                    store(dr("new_pool_sample")[:, :, 0:POOL_STATE - 1, :], dr("state_pool")[:, :, 1:POOL_STATE, :])
                    sp.wait_ge(zero_s.sem, 1)
                    for g in range(4):
                        lo = 64 * (g % 2)
                        sp.dma_start(pwb[lo:lo + 64, g // 2, lo:lo + 64], dr("pool_w")[:, g].rearrange("a i o -> (a i) o")).then_inc(pw_s, 16)
                    pages = [sp.value_load(table[0:1, n:n + 1], min_val=0, max_val=a["cache_k"].shape[1] - 1)
                             for n in range(N_SAMPLE * N_PAGES)]
                    for n in range(N_SAMPLE * N_PAGES):
                        sp.dma_start(kic[:, n // N_PAGES, n % N_PAGES, :],
                                     a["cache_kidx"][L, bass.ds(pages[n], 1)].rearrange("a b p d -> (a b p) d")).then_inc(kic_s, 16)
                    for n in range(4):
                        kv_load(n)
                    for m in range(6, 14):
                        w_load(m)
                    for i in range(NT):
                        sp.wait_ge(idxz_s.sem, i + 1)
                        sp.dma_start(dr("new_kidx_prompt").rearrange("a b t d -> (a b t) d")[START[i]:START[i] + ROWS[i]],
                                     zi[0:ROWS[i], i, 256:288]).then_inc(kx_s, 16)
                    sp.dma_start(dr("new_kidx_sample").rearrange("a b t d -> (a b t) d"), zi[S0:S0 + 8, 4, 256:288]).then_inc(kx_s, 16)
                    sp.dma_start(z_dram, zi[S0:S0 + 8, 4, :]).then_inc(row_z, 16)
                    def k_store(i):
                        sp.wait_ge(kz_s.sem, i + 1)
                        sp.dma_start(dr("new_k_prompt").rearrange("a b t h d -> (a b t) (h d)")[START[i]:START[i] + ROWS[i]],
                                     kz[0:ROWS[i], i % 3, :]).then_inc(out_s[i % 3], 16)

                    for i in range(2):
                        k_store(i)
                    for m in range(14, 18):
                        w_load(m)
                    for i in range(2, NT):
                        k_store(i)
                    sp.dma_start(dr("new_k_sample").rearrange("a b t h d -> (a b t) (h d)"), kz[S0:S0 + 8, 1, :]).then_inc(out_s[1], 16)
                    sp.dma_start(qkv_dram[1], kz[S0:S0 + 8, 1, :]).then_inc(row_k, 16)
                    for m in range(18, 22):
                        w_load(m)
                    sp.wait_ge(kz_s.sem, 2 * NT)
                    sp.dma_start(qkv_dram[0], kz[S0:S0 + 8, 9 % 3, :]).then_inc(row_q, 16)

                    def v_store(i):
                        wait_evac(sp, ("v", i, 0))
                        store(dr("new_v_prompt").rearrange("a b t h d -> (a b t) (h d)")[START[i]:START[i] + ROWS[i]], V[0:ROWS[i], i, :])

                    for i in range(4):
                        v_store(i)
                    for m in range(22, 26):
                        w_load(m)
                    v_store(4)
                    store(dr("new_v_sample").rearrange("a b t h d -> (a b t) (h d)"), V[S0:S0 + 8, 4, :])
                    sp.dma_start(qkv_dram[2], V[S0:S0 + 8, 4, :]).then_inc(row_v, 16)
                    w_load(26)
                    w_load(27)
                    sp.wait_ge(nst_k.sem, 4)
                    new_cp = dr("new_conv_prompt").rearrange("a b j c -> (a b j) c")
                    new_pp = dr("new_pool_prompt").rearrange("a b j c -> (a b j) c")
                    store(new_cp, conv_new[0:CONV_STATE, 0:256])
                    store(dr("new_conv_sample")[:, :, CONV_STATE - 1, :].rearrange("a b c -> (a b) c"), conv_new[0:8, 256:512])
                    store(new_pp, pool_new[0:POOL_STATE, 0:256])
                    store(dr("new_pool_sample")[:, :, POOL_STATE - 1, :].rearrange("a b c -> (a b) c"), pool_new[0:8, 256:512])
                    w_load(28)
                    w_load(29)
                    sp.wait_ge(row_q, 16)
                    sp.wait_ge(row_z, 16)
                    sp.wait_ge(kx_s, 96)
                    sp.wait_ge(acc_s.sem, ACC_END)
                    sp.wait_ge(kqt_s.sem, 2 * NT)
                    sp.dma_start(wbc.rearrange("p (b h) -> p b h", b=8), z_dram[:, 384:392].unsqueeze(0).broadcast_to([128, 8, 8])).then_inc(wbc_s, 16)
                    sp.wait_ge(pd_s.sem, PD_END)

                    def spread(b):
                        if b >= 2:
                            sp.wait_ge(ixp_s.sem, b - 1)
                        sp.dma_start(ibb[:, b % 2, :], z_dram[b:b + 1, :].broadcast_to([128, 392])).then_inc(ibb_s[b % 2], 16)
                        if b >= 2:
                            sp.wait_ge(kp_s.sem, 2 * b - 2)
                        sp.dma_start(qb[:, b % 2, :], qkv_dram[0, b:b + 1, :].broadcast_to([128, 512])).then_inc(qbl_s[b % 2], 16)

                    spread(0)
                    spread(1)
                    for b in range(6):
                        if b == 5:
                            sp.wait_ge(ln_s.sem, LN_END)
                            sp.wait_ge(row_k, 16)
                            sp.wait_ge(row_v, 16)
                            sp.dma_start(rows8.rearrange("b (a n) -> b a n", a=3), qkv_dram.rearrange("a b n -> b a n")).then_inc(rows_s, 16)
                            sp.dma_start(zis, z_dram).then_inc(rows_s, 16)
                        spread(b + 2)
                        kv_load(2 * b + 4)
                        kv_load(2 * b + 5)
                        if b == 2:
                            w_load(30)
                            w_load(31)
                    w_load(32)
                    w_load(33)
                    for n in range(16, 32):
                        kv_load(n)
                    sp.wait_ge(store_s, 16 * stores)
                    for s in range(3):
                        sp.wait_ge(out_s[s], 16 * ([2, 3, 1][s]))

                @block.gpsimd
                def _(pool):
                    zero_s.did(pool.memset(pwb[:], 0.0))
                    misc0.did(pool.memset(bias[:, :, 0:SENT], BIG))
                    misc0.did(pool.memset(rel[:], 0.0))
                    misc0.did(pool.memset(uext[:, :, 0:CONV_STATE], 0.0))
                    misc0.did(pool.memset(ubx[:, :, 0:POOL_STATE], 0.0))
                    for kc in range(4, KC):
                        xs2_s.did(pool.tensor_tensor(yT[:, kc, :], x_hi[:, kc, :].bitcast(F32), x_lo[:, kc, :].bitcast(F32), ALU.add))

                    def rest(m):
                        pool.wait_ge(hi_s.sem, m + 1)
                        lo2_s.did(pool.tensor_tensor(w_raw(m, W_r), w_raw(m), w_high(m, W_r).bitcast(F32), ALU.subtract))

                    pool.wait_ge(var_s.sem, 1)
                    rinv_s.did(pool.tensor_tensor(rinv[0:SR, 0:NT], ssum[0:SR, 0:NT], pow_e[0:SR, 0:NT], ALU.pow))

                    def rotate(z, heads, hd, half, i, n, tab, tmp, s):
                        r = ROWS_P[i]
                        cos = cst[0:r, K_ROT + 48 * i + tab:K_ROT + 48 * i + tab + 2 * half].unsqueeze(1)
                        sin = cst[0:r, K_ROT + 48 * i + tab + 2 * half:K_ROT + 48 * i + tab + 4 * half].unsqueeze(1)
                        w = heads * 2 * half
                        ta = tmp[0:r, 0:w].rearrange("p (h x) -> p h x", h=heads)
                        tb = tmp[0:r, w:2 * w].rearrange("p (h x) -> p h x", h=heads)
                        s.did(pool.tensor_tensor(ta, z[:, :, 0:2 * half], cos.broadcast_to([r, heads, 2 * half]), ALU.mult))
                        s.did(pool.tensor_tensor(tb[:, :, 0:half], z[:, :, half:2 * half], sin[:, :, 0:half].broadcast_to([r, heads, half]), ALU.mult))
                        s.did(pool.tensor_tensor(tb[:, :, half:2 * half], z[:, :, 0:half], sin[:, :, half:2 * half].broadcast_to([r, heads, half]), ALU.mult))
                        pool.wait_ge(s.sem, s.n)
                        return ta, tb

                    for i in range(NT):
                        r = ROWS_P[i]
                        wait_evac(pool, ("idx", i, 0))
                        z = zi[0:r, i, 0:288].rearrange("p (h d) -> p h d", h=9)
                        if i:
                            pool.wait_ge(idxz_s.sem, i)
                        ta, tb = rotate(z, 9, ID, 4, i, 0, 32, rot_tmp, rope_s)
                        rope_s.did(pool.tensor_tensor(z[:, :, 0:8], ta, tb, ALU.add))
                        pool.wait_ge(rope_s.sem, rope_s.n)
                        idxz_s.did(pool.tensor_copy(zi[0:r, i, 288:384].rearrange("p (h d) -> p h d", h=3),
                                                    zi[0:r, i, 256:288].unsqueeze(1).broadcast_to([r, 3, ID])))

                    def kq_tile(n):
                        w, i = divmod(n, NT)
                        r = ROWS_P[i]
                        z = kz[0:r, n % 3, :].rearrange("p (h d) -> p h d", h=HEADS)
                        pool.wait_ge(kq_mid.sem, n + 1)
                        krn_s.did(pool.tensor_tensor(krn[0:r, n % 2, :], kss[0:r, n % 2, :], pow_e[0:r, :], ALU.pow))
                        pool.wait_ge(krn_s.sem, n + 1)
                        kzg_s.did(pool.tensor_tensor(z, z, krn[0:r, n % 2, :].unsqueeze(2).broadcast_to([r, HEADS, HD]), ALU.mult))
                        pool.wait_ge(kzg_s.sem, kzg_s.n)
                        kzg_s.did(pool.tensor_tensor(z, z, gam[0:r, w, :].unsqueeze(1).broadcast_to([r, HEADS, HD]), ALU.mult))
                        pool.wait_ge(kzg_s.sem, kzg_s.n)
                        ta, tb = rotate(z, HEADS, HD, 8, i, n, 0, rot_tmp, kzg_s)
                        kz_s.did(pool.tensor_tensor(z[:, :, 0:16], ta, tb, ALU.add))
                        pool.wait_ge(kz_s.sem, n + 1)

                    pool.wait_ge(gam_s, 32)
                    for n in range(2 * NT):
                        if n in (0, 6):
                            for m in (12, 13) if n == 0 else (16, 17):
                                rest(m)
                        kq_tile(n)

                    for m in range(20, 24):
                        rest(m)
                    pool.wait_ge(st_k.sem, 2)
                    pool.wait_ge(cv_s.sem, 4)
                    wait_evac(pool, ("ub", 1, 1))
                    n = POOL_STATE + NTOK
                    ps_s.did(pool.tensor_tensor(bufA[:, :, 1:n], ubx[:, :, 1:n], ubx[:, :, 0:n - 1], ALU.add))
                    pool.wait_ge(ps_s.sem, 1)
                    ps_s.did(pool.tensor_tensor(bufB[:, :, 3:n], bufA[:, :, 3:n], bufA[:, :, 1:n - 2], ALU.add))
                    pool.wait_ge(ps_s.sem, 2)
                    ps_s.did(pool.tensor_tensor(bufA[:, 1, 7:n], bufB[:, 1, 7:n], bufB[:, 1, 3:n - 4], ALU.add))
                    pool.wait_ge(ps_s.sem, 3)
                    ps_s.did(pool.tensor_tensor(bufB[64:128, 1, 15:n], bufA[64:128, 1, 15:n], bufA[64:128, 1, 7:n - 8], ALU.add))
                    pool.wait_ge(ps_s.sem, 4)

                    for m in (24, 25):
                        rest(m)
                    wait_evac(pool, ("lnsum", 0, 0))
                    lnp_s.did(pool.tensor_tensor(lnr[0:SR, 0:NT], lnv[0:SR, 0:NT], pow_e[0:SR, 0:NT], ALU.pow))

                    for m in (26, 27):
                        rest(m)
                    pool.wait_ge(kic_s, 256)
                    pool.wait_ge(pd_s.sem, PD_END)
                    prod = ixp.rearrange("p (g h d) -> p g h d", g=2, h=IH)
                    for b in range(8):
                        if b == 1:
                            for m in (28, 29):
                                rest(m)
                        pool.wait_ge(ibb_s[b % 2], 16 * (b // 2 + 1))
                        if b:
                            pool.wait_ge(ixr_s.sem, b)
                        ixp_s.did(pool.tensor_tensor(prod, kic[:, b, :, :].unsqueeze(2).broadcast_to([128, 2, IH, ID]),
                                                     ibb[:, b % 2, 0:256].rearrange("p (h d) -> p h d", h=IH).unsqueeze(1).broadcast_to([128, 2, IH, ID]),
                                                     ALU.mult))
                        pool.wait_ge(qbl_s[b % 2], 16 * (b // 2 + 1))
                        for n in (2 * b, 2 * b + 1):
                            pool.wait_ge(kv_s[n % 4], 16 * (n // 4 + 1))
                            kp_s.did(pool.tensor_tensor(KV[:, n % 4, :], KV[:, n % 4, :], qb[:, b % 2, :], ALU.mult))

                @block.scalar
                def _(act):
                    def copy(out, in_, scale=1.0):
                        return act.activation(out, in_, ACT.Copy, scale=scale)

                    def high(m):
                        g, q = LOADS[m]
                        per = GROUPS[g][3]
                        wait_loaded(act, m)
                        for j in range(per):
                            gain = prm[:, per * q + j:per * q + j + 1]
                            if m not in REST_ON_POOL:
                                x = copy(w_high(m, W_r)[:, j, :], w_raw(m)[:, j, :], gain)
                            else:
                                wg_s.did(copy(w_raw(m)[:, j, :], w_raw(m)[:, j, :], gain))
                        if m in REST_ON_POOL:
                            act.wait_ge(wg_s.sem, wg_s.n)
                            x = copy(w_high(m, W_r), w_raw(m))
                        hi_s.did(x)

                    act.wait_ge(prm_s.sem, 1)
                    high(0)
                    high(1)
                    for kc in range(KC):
                        act.wait_ge(*((xs_s.sem, kc + 1) if kc < 4 else (xs2_s.sem, kc - 3)))
                        sq_s.did(act.activation(yT[:, kc, :], yT[:, kc, :], ACT.Square))
                    for m in range(2, 6):
                        high(m)
                    act.wait_ge(rinv_s.sem, 1)

                    def idx_evac(i):
                        r, k = ROWS_P[i], bank(("idx", i, 0))
                        wait_unit(act, ("idx", i, 0))
                        copy(zi[0:r, i, 0:256], R[0:r, k, 0:256], rinv[0:r, i:i + 1])
                        copy(zi[0:r, i, 256:288], R[0:r, k, 264:296], rinv[0:r, i:i + 1])
                        evA.did(copy(zi[0:r, i, 384:392], R[0:r, k, 256:264], rinv[0:r, i:i + 1]))

                    act.wait_ge(row_t.sem, 1)
                    row_s.did(copy(row[:, 0:START[4]], A[:, 2, 0:START[4]]))
                    row_s.did(copy(row[:, START[4]:TOK], A[:, 3, 16:16 + SR]))
                    act.wait_ge(st_t.sem, 1)
                    st_k.did(copy(uxs[:, :, :, 0:CONV_STATE], A[:, 0, 0:480].rearrange("p (c b j) -> p c b j", c=2, b=8)))
                    act.wait_ge(st_t.sem, 2)
                    st_k.did(copy(ubs[:, :, :, 0:POOL_STATE], A[:, 1, 0:240].rearrange("p (c b j) -> p c b j", c=2, b=8)))

                    def half_tanh(c):
                        wait_evac(act, ("conv", 2 + c, 1))
                        tanh_s.did(act.activation(bufB[:, c, 0:TOK], bufB[:, c, 0:TOK], ACT.Tanh, scale=0.5))

                    high(6)
                    high(7)
                    half_tanh(0)
                    for i in range(NT):
                        idx_evac(i)
                        if i == 0:
                            half_tanh(1)
                        if i == 2:
                            high(8)
                            high(9)
                    high(10)
                    high(11)
                    for i in range(NT):
                        act.wait_ge(idxt_s.sem, i + 1)
                        idxk_s.did(copy(qkT[:, :, START[i]:START[i] + ROWS_P[i]],
                                        A[:, i % 2, 0:336].rearrange("p (c t) -> p c t", c=3)[:, :, 0:ROWS_P[i]]))

                    def kq_evac(n):
                        w, i = divmod(n, NT)
                        u, r = (("k", "q")[w], i, 0), ROWS_P[i]
                        wait_unit(act, u)
                        if n >= 3:
                            act.wait_ge(kqt_s.sem, n - 2)
                        if 3 <= n < 8:
                            act.wait_ge(out_s[n % 3], 16 * (n // 3) if n != 7 else 48)
                        if n == 7:
                            act.wait_ge(row_k, 16)
                        copy(kz[0:r, n % 3, :], R[0:r, bank(u), :], rinv[0:r, i:i + 1])
                        if n >= 2:
                            act.wait_ge(kss_s.sem, n - 1)
                        evA.did(act.activation(ksq[0:r, n % 2, :], R[0:r, bank(u), :], ACT.Square, scale=rinv[0:r, i:i + 1]))

                    def kq_keep(n):
                        i, dst = n % NT, (kT, qT)[n // NT]
                        act.wait_ge(kqt_s.sem, n + 1)
                        kqk_s.did(copy(dst[:, :, START[i]:START[i] + ROWS_P[i]],
                                       A[:, 2 + n % 2, 0:448].rearrange("p (c t) -> p c t", c=4)[:, :, 0:ROWS_P[i]]))

                    def relu(p):
                        i, h, lo, hi = PIECES[p]
                        act.wait_ge(ix_s.sem, p + 1)
                        if p >= 2:
                            act.wait_ge(acc_s.sem, p - 1 if p - 1 <= 16 else p + 1)
                        rel_s.did(act.activation(rel[0:ROWS[i], p % 2, 0:hi - lo], A[0:ROWS[i], p % 2, 0:hi - lo], ACT.Relu,
                                                 scale=1.0 / 16))

                    act.wait_ge(misc0.sem, 2)
                    high(12)
                    high(13)
                    p = 0
                    for i in range(NT):
                        for _ in range(IX_K):
                            relu(p)
                            p += 1
                        kq_evac(i)
                        if i == 4:
                            high(14)
                            high(15)
                        if i >= 2:
                            kq_keep(i - 2)
                    for i in range(NT):
                        for _ in range(IX_Q):
                            relu(p)
                            p += 1
                        kq_evac(NT + i)
                        if i == 1:
                            high(16)
                            high(17)
                        if i == 4:
                            high(18)
                            high(19)
                        kq_keep(3 + i)
                    for i in range(NT):
                        wait_unit(act, ("v", i, 0))
                        evA.did(copy(V[0:ROWS_P[i], i, :], R[0:ROWS_P[i], bank(("v", i, 0)), :], rinv[0:ROWS_P[i], i:i + 1]))
                        if i < 2:
                            kq_keep(8 + i)
                        if i in (2, 3):
                            high(18 + i)

                    def gate_tanh(g):
                        u = GATES[g]
                        wait_evac(act, u[0])
                        if g >= 2:
                            act.wait_ge(gate_s.sem, g - 1)
                        gt_s.did(act.activation(gt[:, g % 2, :], yT[:, u[1], HALF * u[0][2]:HALF * u[0][2] + HALF], ACT.Tanh, scale=0.5))

                    def new_state(dst, rows, n):
                        act.wait_ge(nst_t.sem, n)
                        nst_k.did(copy(dst[0:rows, 0:256], A[0:rows, 3, 0:256]))
                        nst_k.did(copy(dst[0:8, 256:512], A[0:8, 3, 256:512]))

                    new_state(conv_new, CONV_STATE, 1)
                    for n in range(len(ITEMS) + PIPE):
                        if n < len(ITEMS):
                            i, h = ITEMS[n]
                            r, w = ROWS[i], WIDTH[i]
                            act.wait_ge(ttr_s.sem, n + 1)
                            if n >= 2:
                                act.wait_ge(T_s.sem, n - 1)
                            if i >= 2 and h == 0:
                                act.wait_ge(rec_s.sem, i - 1)
                            P_s.did(act.activation(rel[0:r, n % 2, 0:w], sb_scores[0:r, n % 2, 0:w], ACT.Exp,
                                                   bias=mn[0:r, n % 2:n % 2 + 1], scale=-1.0, accum_out=rsum[0:r, i % 2, h:h + 1]))
                        if 2 <= n < len(ITEMS) + 2:
                            m = n - 2
                            i, h = ITEMS[m]
                            act.wait_ge(T_s.sem, m + 1)
                            if m >= 2:
                                act.wait_ge(PV_s.sem, m - 1)
                            dst = pT[0:MAXR, m % 2, :].rearrange("p (j t) -> p j t", j=NT)[:, 0:i + 1, 0:ROWS[i]]
                            PTk_s.did(copy(dst, A[0:MAXR, m % 2, 0:(i + 1) * ROWS[i]].rearrange("p (j t) -> p j t", j=i + 1)))
                        if n in HIGH_AT:
                            high(HIGH_AT[n])
                        if n == 5:
                            new_state(pool_new, POOL_STATE, 2)
                        if n == SX["ln_tanh"]:
                            act.wait_ge(ln_s.sem, 1)
                            for c in range(2):
                                lth_s.did(act.activation(qkT[:, c, :], cc[:, c, :], ACT.Tanh, scale=prm_h[:, 4 + c:5 + c], bias=prm_h[:, 6 + c:7 + c]))
                        if n == SX["exp"]:
                            act.wait_ge(sd_s.sem, SD["negmax"])
                            sexp_s.did(act.activation(pn[:, 0:257], A[0:64, 3, 0:257], ACT.Exp, bias=snm, scale=0.125, accum_out=srs))
                        if n == SX["keep"]:
                            act.wait_ge(spt_s.sem, 1)
                            spk_s.did(copy(pts[:, :, :], A[:, 3, 0:128].rearrange("p (g x) -> p g x", g=2)))
                            spk_s.did(copy(pd[:, :], A[0:8, 3, 128:192]))
                        for u in PLAN[n]:
                            if u in GATE_OF:
                                gate_tanh(GATE_OF[u])
                            if u == ("mean", 0, 1):
                                wait_evac(act, u)
                                lnsq_s.did(act.activation(qkT[:, 0:2, :], cc[:, :, :], ACT.Square))
                            if u[0] == "lnrow":
                                wait_unit(act, u)
                                lo, hi = ((0, START[4]), (START[4], TOK))[u[2]]
                                evA.did(copy(lnrow[:, lo:hi], R[:, bank(u), 0:hi - lo]))
                            if u[0] == "turn":
                                i = u[1]
                                wait_unit(act, u)
                                evA.did(copy(qT[:, :, START[i]:START[i] + ROWS[i]],
                                             R[:, bank(u), 0:4 * MAXR].rearrange("p (c t) -> p c t", c=4)[:, :, 0:ROWS[i]]))

                @block.tensor
                def _(pe):
                    def turn(out, in_, k):
                        return pe.transpose(out, in_, ident[0:k, 0:k])

                    def open_unit(u):
                        old = [v for v in UNITS[:NUM[u]] if bank(v) == bank(u)]
                        if old:
                            wait_evac(pe, old[-1])
                        return bank(u)

                    def chunks(g):
                        per = GROUPS[g][3]
                        for kc in range(KC):
                            m = LOAD_OF[g, kc // per]
                            if kc % per == 0:
                                wait_split(pe, m)
                            yield (kc, w_high(m, W_r)[:, kc % per, :], w_raw(m, W_r)[:, kc % per, :],
                                   kc % per == per - 1 and kc < KC - 1)

                    def unit_tm(u, name, first_dots=None):
                        i, k = u[1], open_unit(u)
                        g = G[name]
                        n = GROUPS[g][2]
                        rows = slice(START[i], START[i] + ROWS_P[i])
                        for kc, hi, lo, more in chunks(g):
                            out = R[0:ROWS_P[i], k, 0:n]
                            pe.matmul(out, x_hi[:, kc, rows], hi, start=(kc == 0), stop=False)
                            pe.matmul(out, x_hi[:, kc, rows], lo, start=False, stop=False)
                            m = pe.matmul(out, x_lo[:, kc, rows], hi, start=False, stop=(kc == KC - 1))
                            if more and u == LAST_UNIT[g]:
                                free_s.did(m)
                            if kc == KC - 1:
                                unit_s.did(m)
                            if first_dots is not None and kc % 2:
                                dots(first_dots + kc // 2)

                    def unit_fm(u, name, col):
                        k, g = open_unit(u), G[name]
                        toks = slice(HALF * u[2], HALF * u[2] + HALF)
                        for kc, hi, lo, more in chunks(g):
                            out, cols = R[:, k, 0:HALF], slice(col, col + 128)
                            pe.matmul(out, hi[:, cols], x_hi[:, kc, toks], start=(kc == 0), stop=False)
                            pe.matmul(out, hi[:, cols], x_lo[:, kc, toks], start=False, stop=False)
                            m = pe.matmul(out, lo[:, cols], x_hi[:, kc, toks], start=False, stop=(kc == KC - 1))
                            if more and u == LAST_UNIT[g]:
                                free_s.did(m)
                        unit_s.did(m)

                    def unit_out(u):
                        k = open_unit(u)
                        lo, hi = OUT_PART[u[2]]
                        for kc in range(KC):
                            x = LOAD_OF[len(GROUPS) + u[1] // 4, kc // 4]
                            wait_loaded(pe, x)
                            m = pe.matmul(R[:, k, 0:hi - lo], W[:, x % W_SLOTS, kc % 4, 128 * (u[1] % 4):128 * (u[1] % 4) + 128],
                                          yT[:, kc, lo:hi], start=(kc == 0), stop=(kc == KC - 1))
                        unit_s.did(m)

                    for h in range(2):
                        unit_fm(("conv", 0, h), "cv", 0)
                    pe.wait_ge(ssq_s.sem, KC - 1)
                    for i in range(NT):
                        m = pe.matmul(A[0:SR, 3, i:i + 1], yT[:, 0, START[i]:START[i] + SR], ones[:, 0:1], start=True, stop=True)
                    stats_s.did(m)
                    for h in range(2):
                        unit_fm(("conv", 1, h), "cv", 128)

                    def spread(src, stage):
                        for i in range(NT):
                            r = ROWS_P[i] if i == 4 else ROWS[i]
                            out = A[:, 2, START[i]:START[i] + r] if i < 4 else A[:, 3, 16:16 + r]
                            m = pe.matmul(out, ones[0:r, :], diag[0:r, i, 0:r], start=True, stop=True)
                        stage.did(m)

                    pe.wait_ge(diag_s.sem, NT)
                    spread(diag, row_t)
                    pe.wait_ge(state_s, 48)
                    for c in range(2):
                        for g in range(2):
                            m = turn(A[:, 0, 240 * c + 120 * g:240 * c + 120 * g + 120], st_in[0:120, g, 128 * c:128 * c + 128], 120)
                    st_t.did(m)
                    for c in range(2):
                        m = turn(A[:, 1, 120 * c:120 * c + 120], stp_in[0:120, 128 * c:128 * c + 128], 120)
                    st_t.did(m)
                    for m in (2, 3):
                        for h in range(2):
                            unit_fm(("conv", m, h), "cg", 128 * (m % 2))
                    for i in range(NT):
                        unit_tm(("idx", i, 0), "idx")
                    pe.wait_ge(st_k.sem, 2)
                    for i in range(NT):
                        pe.wait_ge(idxz_s.sem, i + 1)
                        if i >= 2:
                            pe.wait_ge(idxk_s.sem, i - 1)
                        for j in range(3):
                            m = turn(A[:, i % 2, 112 * j:112 * j + ROWS_P[i]], zi[0:ROWS_P[i], i, 128 * j:128 * j + 128], ROWS_P[i])
                        idxt_s.did(m)

                    def kq_turn(n):
                        i = n % NT
                        r = ROWS_P[i]
                        pe.wait_ge(kz_s.sem, n + 1)
                        if n < 2:
                            pe.wait_ge(row_s.sem, 2)
                        else:
                            pe.wait_ge(kqk_s.sem, n - 1)
                        for j in range(4):
                            m = turn(A[:, 2 + n % 2, 112 * j:112 * j + r], kz[0:r, n % 3, 128 * j:128 * j + 128], r)
                        kqt_s.did(m)

                    def dots(p):
                        i, h, lo, hi = PIECES[p]
                        if p == 0:
                            pe.wait_ge(idxk_s.sem, NT)
                        if p >= 2:
                            pe.wait_ge(rel_s.sem, p - 1)
                        b = 32 * (h % 4)
                        ix_s.did(pe.matmul(A[0:ROWS[i], p % 2, 0:hi - lo], qkT[b:b + 32, h // 4, START[i]:START[i] + ROWS[i]],
                                           qkT[b:b + 32, 2, lo:hi], start=True, stop=True))

                    p = 0
                    for i in range(NT):
                        unit_tm(("k", i, 0), "k", 4 * i)
                        if i >= 2:
                            kq_turn(i - 2)
                    for i in range(NT):
                        unit_tm(("q", i, 0), "q", 4 * NT + 4 * i)
                        kq_turn(3 + i)
                    for i in range(NT):
                        unit_tm(("v", i, 0), "v")
                        if i < 2:
                            kq_turn(8 + i)

                    def new_state(ext, rows, s, last):
                        for c in range(2):
                            turn(A[0:rows, 3, 128 * c:128 * c + 128], ext[:, c, NTOK:NTOK + rows], 128)
                            m = turn(A[0:8, 3, 256 + 128 * c:384 + 128 * c], s[:, c, :, last], 128)
                        nst_t.did(m)

                    pe.wait_ge(kqk_s.sem, 2 * NT)
                    pe.wait_ge(cv_s.sem, 4)
                    new_state(uext, CONV_STATE, uxs, CONV_STATE)
                    pe.wait_ge(rel_s.sem, len(PIECES))
                    for u in UNITS[len(EARLY) - 2:len(EARLY)]:
                        wait_evac(pe, u)

                    def scores(n):
                        i, h = ITEMS[n]
                        r, w, b = ROWS[i], WIDTH[i], 64 * (h % 2)
                        if w > 512:
                            pe.wait_ge(ttr_s.sem, n)
                        elif n >= 2:
                            pe.wait_ge(ttr_s.sem, n - 1)
                        k = 2 if w > 512 else 2 + n % 2
                        lhs = qT[b:b + 64, h // 2, START[i]:START[i] + r]
                        m = pe.matmul(R[0:r, k, 0:min(w, 512)], lhs, kT[b:b + 64, h // 2, 0:min(w, 512)], start=True, stop=True)
                        if w > 512:
                            m = pe.matmul(R[0:r, k + 1, 0:w - 512], lhs, kT[b:b + 64, h // 2, 512:w], start=True, stop=True)
                        S_s.did(m)

                    def turn_probs(n):
                        i, h = ITEMS[n]
                        pe.wait_ge(P_s.sem, n + 1)
                        if n >= 2:
                            pe.wait_ge(PTk_s.sem, n - 1)
                        for j in range(i + 1):
                            m = turn(A[0:MAXR, n % 2, ROWS[i] * j:ROWS[i] * (j + 1)], rel[0:ROWS[i], n % 2, START[j]:START[j] + MAXR], ROWS[i])
                        T_s.did(m)

                    def weigh(n):
                        i, h = ITEMS[n]
                        pe.wait_ge(PTk_s.sem, n + 1)
                        if h == 0 and i:
                            pe.wait_ge(on_s.sem, i)
                        pt = pT[:, n % 2, :].rearrange("p (j t) -> p j t", j=NT)
                        for j in range(i + 1):
                            m = pe.matmul(A[0:ROWS[i], 2, HD * h:HD * h + HD], pt[0:ROWS[j], j, 0:ROWS[i]],
                                          V[0:ROWS[j], j, HD * h:HD * h + HD], start=(j == 0), stop=(j == i))
                        PV_s.did(m)

                    def unit(u):
                        kind, m, h = u
                        if kind == "ub":
                            unit_fm(u, ("ub", "gb")[m // 2], 128 * (m % 2))
                        elif kind == "gc":
                            unit_fm(u, "gc", 128 * m)
                        elif kind == "ga":
                            unit_fm(u, ("ga0", "ga1")[m // 2], 128 * (m % 2))
                        elif kind == "out":
                            unit_out(u)
                        elif kind == "mean":
                            if h == 0:
                                pe.wait_ge(conv_s.sem, CONV_END)
                            k = open_unit(u)
                            for c in range(2):
                                x = pe.matmul(R[:, k, 0:HALF], ones[:], cc[:, c, HALF * h:HALF * h + HALF], start=(c == 0), stop=(c == 1))
                            unit_s.did(x)
                        elif kind == "lnsum":
                            k = open_unit(u)
                            pe.wait_ge(lnsq_s.sem, 1)
                            for i in range(NT):
                                for c in range(2):
                                    x = pe.matmul(R[0:SR, k, i:i + 1], qkT[:, c, START[i]:START[i] + SR], ones[:, 0:1],
                                                  start=(c == 0), stop=(c == 1))
                            unit_s.did(x)
                        elif kind == "lnrow":
                            k = open_unit(u)
                            pe.wait_ge(lnd_s.sem, NT)
                            for i in (range(4), range(4, NT))[h]:
                                r = ROWS[i] if i < 4 else ROWS_P[i]
                                lo = START[i] if i < 4 else 0
                                x = pe.matmul(R[:, k, lo:lo + r], ones[0:r, :], ln_dg[0:r, i, 0:r], start=True, stop=True)
                            unit_s.did(x)
                        elif kind == "pool":
                            k = open_unit(u)
                            pe.wait_ge(pw_s, 64)
                            lo = POOL_STATE + HALF * h
                            unit_s.did(pe.matmul(R[:, k, 0:HALF], pwb[:, m, :], bufA[:, m, lo:lo + HALF], start=True, stop=True))
                        elif kind == "turn":
                            k = open_unit(u)
                            pe.wait_ge(on_s.sem, m + 1)
                            for c in range(4):
                                x = turn(R[:, k, MAXR * c:MAXR * c + ROWS[m]], ksq[0:ROWS[m], 0, 128 * c:128 * c + 128], ROWS[m])
                            unit_s.did(x)

                    for n in range(len(ITEMS) + PIPE):
                        if n < len(ITEMS):
                            scores(n)
                        if n == SX["index_turn"]:
                            pe.wait_ge(sd_s.sem, SD["isc"])
                            for g in range(2):
                                m = turn(A[0:8, 3, 128 * g:128 * g + 128], isc[:, 8 * g:8 * g + 8], 128)
                            sit_s.did(m)
                        if n == SX["logits"]:
                            pe.wait_ge(sd_s.sem, SD["logit_in"])
                            pe.wait_ge(kr_s.sem, 16)
                            out = A[0:64, 3, :]
                            pe.matmul(out[:, 0:257], E8, sc8[:, 0:257], start=True, stop=False)
                            for g in range(2):
                                pe.matmul(out[:, 128 * g:128 * g + 128], ssm[:, g, :], ident, start=False, stop=False)
                            slog_s.did(pe.matmul(out[:, 256:257], sn, ones[0:8, 0:1], start=False, stop=True))
                        if n == SX["turn"]:
                            pe.wait_ge(sd_s.sem, SD["etp"])
                            for g in range(2):
                                turn(A[:, 3, 64 * g:64 * g + 64], pn[:, 128 * g:128 * g + 128], 64)
                            spt_s.did(pe.matmul(A[0:8, 3, 128:192], etp, ident[0:64, 0:64], start=True, stop=True))
                        if n == 5:
                            pe.wait_ge(nst_k.sem, 2)
                            wait_evac(pe, ("ub", 1, 1))
                            new_state(ubx, POOL_STATE, ubs, POOL_STATE)
                        if n == 39:
                            pe.wait_ge(y_s.sem, 2)
                        if n == 31:
                            pe.wait_ge(y_s.sem, 1)
                            pe.wait_ge(ln_s.sem, LN_END)
                            wait_evac(pe, ("pool", 1, 1))
                        for u in PLAN[n]:
                            if u[0] != "turn":
                                unit(u)
                        if 2 <= n < len(ITEMS) + 2:
                            turn_probs(n - 2)
                        if 3 <= n < len(ITEMS) + 3:
                            weigh(n - 3)
                        for u in PLAN[n]:
                            if u[0] == "turn":
                                unit(u)
                        if SX["pv"] <= n < SX["pv"] + 8:
                            acc = A[:, 3, 0:64]
                            if n == SX["pv"]:
                                pe.wait_ge(spk_s.sem, 2)
                                pe.wait_ge(rows_s, 32)
                                for c in range(4):
                                    new = pd[:, :].rearrange("p (b h) -> p b h", b=8)[:, :, 2 * c:2 * c + 2]
                                    pe.matmul(acc[:, 16 * c:16 * c + 16], rows8[:, 1024 + 128 * c:1152 + 128 * c], new,
                                              start=(c == 0), stop=False, skip_group_check=True)
                            b = n - SX["pv"]
                            for g in range(2):
                                page = 16 + 2 * b + g
                                pe.wait_ge(kv_s[page % 4], 16 * (page // 4 + 1))
                                for c in range(4):
                                    m = pe.matmul(acc[:, 16 * c + 2 * b:16 * c + 2 * b + 2], KV[:, page % 4, 128 * c:128 * c + 128],
                                                  pts[:, g, 8 * b + 2 * c:8 * b + 2 * c + 2], start=False,
                                                  stop=(page == 31 and c == 3), skip_group_check=True)
                                spv_s.did(m)
                    pe.wait_ge(y_s.sem, 3)
                    pe.wait_ge(ys_s.sem, 2)
                    for m in range(KC):
                        unit(("out", m, 2))

                @block.vector
                def _(dve):
                    def stt(out, a0, s, a1, op0=ALU.mult, op1=ALU.mult):
                        return dve.scalar_tensor_tensor(out=out, in0=a0, scalar=s, in1=a1, op0=op0, op1=op1)

                    prm_s.did(dve.tensor_copy(prm[:, :], params[:, L, :].rearrange("p a n -> p (a n)")))
                    dve.wait_ge(prm_s.sem, 1)
                    for kc in range(4):
                        xs_s.did(dve.tensor_tensor(yT[:, kc, :], x_hi[:, kc, :].bitcast(F32), x_lo[:, kc, :].bitcast(F32), ALU.add))

                    def rest(m):
                        g, q = LOADS[m]
                        per = GROUPS[g][3]
                        dve.wait_ge(hi_s.sem, m + 1)
                        for j in range(per):
                            x = stt(w_raw(m, W_r)[:, j, :], w_raw(m)[:, j, :], prm[:, per * q + j:per * q + j + 1],
                                    w_high(m, W_r)[:, j, :].bitcast(F32), ALU.mult, ALU.subtract)
                        lo_s.did(x)

                    rest(0)
                    rest(1)
                    for kc in range(1, KC):
                        dve.wait_ge(sq_s.sem, kc + 1)
                        if kc > 1:
                            dve.wait_ge(ssq_s.sem, kc - 1)
                        ssq_s.did(dve.tensor_tensor(yT[:, 0, :], yT[:, 0, :], yT[:, kc, :], ALU.add))
                    prm_s.did(dve.tensor_scalar(prm_h[:, :], prm[:, 8:16], 0.5, None, ALU.mult))
                    dve.wait_ge(stats_s.sem, 1)
                    var_s.did(dve.tensor_scalar(ssum[0:SR, 0:NT], A[0:SR, 3, 0:NT], 1.0 / D_MODEL, EPS, ALU.mult, ALU.add))
                    dve.wait_ge(rinv_s.sem, 1)
                    for i in range(NT):
                        r = ROWS_P[i]
                        diag_s.did(dve.tensor_scalar(diag[0:r, i, 0:r], ident[0:r, 0:r], rinv[0:r, i:i + 1], None, ALU.mult))
                    for m in range(2, 6):
                        rest(m)
                    dve.wait_ge(row_s.sem, 2)
                    dve.wait_ge(st_t.sem, 2)
                    dve.wait_ge(misc0.sem, 4)
                    dve.wait_ge(st_k.sem, 2)

                    def tok(h):
                        return slice(HALF * h, HALF * h + HALF)

                    def conv_in(c):
                        dve.wait_ge(tanh_s.sem, c + 1)
                        cv_s.did(stt(uext[:, c, CONV_STATE:CONV_STATE + NTOK], bufB[:, c, 0:NTOK], 1.0, bufA[:, c, 0:NTOK], ALU.add))
                        cv_s.did(stt(uxs[:, c, :, CONV_STATE], bufB[:, c, NTOK:TOK], 1.0, bufA[:, c, NTOK:TOK], ALU.add))

                    def kq_sum(n):
                        w, i = divmod(n, NT)
                        r = ROWS_P[i]
                        wait_evac(dve, (("k", "q")[w], i, 0))
                        if n >= 2:
                            dve.wait_ge(krn_s.sem, n - 1)
                        kss_s.did(dve.reduce_sum(kss[0:r, n % 2, :], ksq[0:r, n % 2, :].rearrange("p (h d) -> p h d", h=HEADS), AX.X))
                        dve.wait_ge(kss_s.sem, n + 1)
                        kq_mid.did(dve.tensor_scalar(kss[0:r, n % 2, :], kss[0:r, n % 2, :], 1.0 / HD, EPS, ALU.mult, ALU.add))

                    def area(i, lo=0, hi=None):
                        hi = SENT + WIDTH[i] if hi is None else hi
                        return bias[0:ROWS[i], i - 1, lo:hi]

                    last = {}

                    def gather(p):
                        i, h, lo, hi = PIECES[p]
                        dve.wait_ge(rel_s.sem, p + 1)
                        dst = area(i, SENT + lo, SENT + hi)
                        w = zi[0:ROWS[i], i, 384 + h:385 + h]
                        src = rel[0:ROWS[i], p % 2, 0:hi - lo]
                        if h == 0:
                            acc_s.did(dve.tensor_scalar(dst, src, w, None, ALU.mult))
                        else:
                            dve.wait_ge(acc_s.sem, last[i, lo])
                            acc_s.did(stt(dst, src, w, dst, ALU.mult, ALU.add))
                        last[i, lo] = acc_s.n

                    def causal(i, s):
                        d = area(i, SENT + START[i], SENT + WIDTH[i])
                        s.did(dve.tensor_tensor(d, d, tri[0:ROWS[i], 0:ROWS[i]], ALU.add))

                    def topk_round(pair):
                        for x, i in enumerate(pair):
                            dve.wait_ge(tk_s.sem, tk_s.n - 1) if tk_s.n > 1 else None
                            tk_s.did(dve.max(m8[0:ROWS[i], x, :], area(i)))
                        for x, i in enumerate(pair):
                            dve.wait_ge(tk_s.sem, tk_s.n - 1)
                            tk_s.did(dve.match_replace(area(i), m8[0:ROWS[i], x, :], area(i), GONE))

                    def to_bias(pair):
                        for i in pair:
                            dve.wait_ge(tk_s.sem, tk_s.n)
                            tk_s.did(dve.tensor_scalar(area(i), area(i), CUT, NEG, ALU.is_gt, ALU.mult))
                        for i in pair:
                            dve.wait_ge(tk_s.sem, tk_s.n)
                            causal(i, tk_s)

                    n1 = sum(1 for q in PIECES if q[0] <= 2)

                    def piece(p):
                        gather(p)
                        if p in (n1 - 1, len(PIECES) - 1):
                            dve.wait_ge(acc_s.sem, acc_s.n)
                            for i in (1, 2) if p == n1 - 1 else (3, 4):
                                causal(i, acc_s)

                    def tap(j):
                        for c in range(2):
                            w = prm[:, 16 + CONV_W * c + j:17 + CONV_W * c + j]
                            if j == 0:
                                dve.wait_ge(cv_s.sem, 2 * c + 2)
                                conv_s.did(dve.tensor_scalar(cc[:, c, 0:NTOK], uext[:, c, 0:NTOK], w, prm[:, 10 + c:11 + c], ALU.mult, ALU.add))
                            else:
                                dve.wait_ge(conv_s.sem, 2 * j + c - 1)
                                conv_s.did(stt(cc[:, c, 0:NTOK], uext[:, c, j:j + NTOK], w, cc[:, c, 0:NTOK], ALU.mult, ALU.add))

                    p = 0
                    for m in range(4):
                        for h in range(2):
                            u = ("conv", m, h)
                            wait_unit(dve, u)
                            src = R[:, bank(u), 0:HALF]
                            if m < 2:
                                evD.did(stt(bufA[:, m, tok(h)], src, 0.5, row[:, tok(h)]))
                            else:
                                evD.did(dve.tensor_tensor(bufB[:, m - 2, tok(h)], src, row[:, tok(h)], ALU.mult))
                        if m == 2:
                            rest(6)
                            rest(7)
                    conv_in(0)
                    conv_in(1)
                    for j in range(TAPS_IDX):
                        tap(j)
                        if j in (3, 4, 9, 10):
                            rest({3: 8, 4: 9, 9: 10, 10: 11}[j])
                    j = TAPS_IDX
                    for i in range(NT):
                        for x in range(IX_K):
                            piece(p)
                            p += 1
                            if x < TAPS_K[i]:
                                tap(j)
                                j += 1
                        kq_sum(i)
                    rest(14)
                    rest(15)
                    for i in range(NT):
                        for x in range(IX_Q):
                            piece(p)
                            p += 1
                            if x < TAPS_Q[i]:
                                tap(j)
                                j += 1
                        kq_sum(NT + i)
                        if i < 4:
                            topk_round((1, 2))
                    rest(18)
                    rest(19)
                    topk_round((1, 2))
                    assert j == CONV_W and p == len(PIECES) and acc_s.n == ACC_END
                    for c in range(2):
                        taps = prm[:, 16 + CONV_W * c:16 + CONV_W * (c + 1)].unsqueeze(1).broadcast_to([128, N_SAMPLE, CONV_W])
                        tmp = gt[:, c, 0:N_SAMPLE * CONV_W].rearrange("p (b j) -> p b j", b=N_SAMPLE)
                        conv_s.did(dve.tensor_tensor(tmp, uxs[:, c, :, :], taps, ALU.mult))
                    topk_round((1, 2))
                    for c in range(2):
                        tmp = gt[:, c, 0:N_SAMPLE * CONV_W].rearrange("p (b j) -> p b j", b=N_SAMPLE)
                        dve.wait_ge(conv_s.sem, 2 * CONV_W + 1 + c)
                        conv_s.did(dve.reduce_sum(wsum[:, c, :], tmp, AX.X))
                    topk_round((1, 2))
                    for c in range(2):
                        dve.wait_ge(conv_s.sem, 2 * CONV_W + 3 + c)
                        conv_s.did(dve.tensor_scalar(cc[:, c, NTOK:TOK], wsum[:, c, :], prm[:, 10 + c:11 + c], None, ALU.add))
                    for _ in range(NT + 2, ROUNDS):
                        topk_round((1, 2))
                    to_bias((1, 2))
                    tb12 = tk_s.n

                    rounds = [0]

                    def more_topk(n):
                        if rounds[0] < ROUNDS and n not in NO_ROUND:
                            topk_round((3, 4))
                            rounds[0] += 1

                    def gate(g):
                        u = GATES[g]
                        dve.wait_ge(gt_s.sem, g + 1)
                        dst = yT[:, u[1], tok(u[0][2])]
                        gate_s.did(stt(dst, gt[:, g % 2, :], 1.0, dst, ALU.add))

                    def gate_in(u, ch):
                        wait_unit(dve, u)
                        evD.did(dve.tensor_tensor(yT[:, ch, tok(u[2])], R[:, bank(u), 0:HALF], row[:, tok(u[2])], ALU.mult))

                    def take(u):
                        kind, m, h = u
                        src = R[:, bank(u), 0:HALF]
                        if u in GATE_OF:
                            gate_in(u, GATES[GATE_OF[u]][1])
                        elif kind == "ub":
                            wait_unit(dve, u)
                            if h == 0:
                                evD.did(dve.tensor_tensor(ubx[:, m, POOL_STATE:POOL_STATE + HALF], src, row[:, tok(0)], ALU.mult))
                            else:
                                k = NTOK - HALF
                                dve.tensor_tensor(ubx[:, m, POOL_STATE + HALF:POOL_STATE + NTOK], src[:, 0:k], row[:, HALF:NTOK], ALU.mult)
                                evD.did(dve.tensor_tensor(ubs[:, m, :, POOL_STATE], src[:, k:HALF], row[:, NTOK:TOK], ALU.mult))
                        elif kind == "mean":
                            wait_unit(dve, u)
                            dve.wait_ge(conv_s.sem, conv_s.n)
                            evD.did(stt(cc[:, :, tok(h)], src.unsqueeze(1).broadcast_to([128, 2, HALF]), -1.0 / D_C,
                                        cc[:, :, tok(h)], ALU.mult, ALU.add))
                        elif kind == "lnsum":
                            wait_unit(dve, u)
                            evD.did(dve.tensor_scalar(lnv[0:SR, 0:NT], R[0:SR, bank(u), 0:NT], 1.0 / D_C, EPS, ALU.mult, ALU.add))
                        elif kind == "pool":
                            wait_unit(dve, u)
                            dst = yT[:, 4 + m, tok(h)]
                            evD.did(stt(dst, src, prm_h[:, m:m + 1], dst))
                        elif kind == "out":
                            wait_unit(dve, u)
                            lo, hi = OUT_PART[h]
                            src = R[:, bank(u), 0:hi - lo]
                            part = (slice(None), m, slice(lo, hi))
                            new = gt[:, m % 2, 0:hi - lo]
                            if res_s.n > 3:
                                dve.wait_ge(res_s.sem, res_s.n - 3)
                            evD.did(dve.tensor_tensor(new, src, x_hi[part].bitcast(F32), ALU.add))
                            wait_evac(dve, u)
                            res_s.did(dve.tensor_tensor(new, new, x_lo[part].bitcast(F32), ALU.add))
                            dve.wait_ge(res_s.sem, res_s.n)
                            res_s.did(dve.tensor_copy(x_hi[part], new))
                            dve.wait_ge(res_s.sem, res_s.n)
                            res_s.did(dve.tensor_tensor(x_lo[part], new, x_hi[part].bitcast(F32), ALU.subtract))

                    def pool_differences(k):
                        dve.wait_ge(ps_s.sem, 4)
                        first = slice(POOL_STATE, 2 * POOL_STATE)
                        rest = slice(2 * POOL_STATE, POOL_STATE + NTOK)
                        for half, src in [((slice(0, 64), bufA), (slice(64, 128), bufB))[k]]:
                            cnt = cst[half, K_CNT:K_CNT + 32].rearrange("p (c t) -> p c t", c=2)[:, :, 0:POOL_STATE]
                            pd_s.did(dve.tensor_tensor(bufA[half, :, first], src[half, :, first], cnt, ALU.mult))
                            for c in range(2):
                                pd_s.did(stt(bufA[half, c, rest], src[half, c, rest], cst[half, K_WIN + c:K_WIN + c + 1],
                                             ubx[half, c, rest], ALU.mult, ALU.subtract))
                            dve.wait_ge(pd_s.sem, pd_s.n - 2)
                            pd_s.did(dve.tensor_tensor(bufA[half, :, first], bufA[half, :, first], ubx[half, :, first], ALU.subtract))
                        if k == 0:
                            return
                        for c in range(2):
                            for k in range(2):
                                rows = slice(64 * k, 64 * k + 64)
                                win = WINDOWS[2 * c + k]
                                pd_s.did(dve.reduce_sum(wsum[rows, c, :], ubs[rows, c, :, 16 - win:16], AX.X))
                        dve.wait_ge(pd_s.sem, pd_s.n)
                        for c in range(2):
                            pd_s.did(stt(bufA[:, c, POOL_STATE + NTOK:POOL_STATE + TOK], wsum[:, c, :], cst[:, K_WIN + c:K_WIN + c + 1],
                                         ubs[:, c, :, POOL_STATE], ALU.mult, ALU.subtract))
                        assert pd_s.n == PD_END

                    def page_scores(n):
                        dve.wait_ge(kp_s.sem, n + 1)
                        b, pg = divmod(n, 2)
                        kr_s.did(dve.reduce_sum(ssm[:, pg, 8 * b:8 * b + 8], KV[:, n % 4, :].rearrange("p (h d) -> p h d", h=HEADS), AX.X))

                    def swish(step):
                        for c in range(2):
                            if step == 0:
                                dve.wait_ge(lth_s.sem, c + 1)
                                ln_s.did(dve.tensor_scalar(cc[:, c, :], cc[:, c, :], prm[:, 12 + c:13 + c], prm[:, 14 + c:15 + c], ALU.mult, ALU.add))
                            elif step == 1:
                                dve.wait_ge(ln_s.sem, 2 + c)
                                ln_s.did(stt(qkT[:, c, :], qkT[:, c, :], 1.0, cc[:, c, :], ALU.add))
                            else:
                                dve.wait_ge(ln_s.sem, 4 + c)
                                ln_s.did(stt(yT[:, 6 + c, :], qkT[:, c, :], 0.25, yT[:, 6 + c, :]))

                    def sd(make, name=None):
                        if sd_s.n:
                            dve.wait_ge(sd_s.sem, sd_s.n)
                        sd_s.did(make())
                        if name:
                            assert SD[name] == sd_s.n, (name, sd_s.n)

                    flat = smp[:, 0:128].rearrange("p (g x) -> p g x", g=2)
                    t8 = bufB[0:8, 1, 0:512].rearrange("p (h d) -> p h d", h=8)
                    chosen = sc8[:, 0:PAST + 1]
                    logits = A[0:64, 3, 0:PAST + 1]

                    Rf = R[:, :, :].rearrange("p k n -> p (k n)")
                    dve.wait_ge(kx_s, 96)
                    dve.wait_ge(row_z, 16)
                    dve.wait_ge(acc_s.sem, ACC_END)
                    for n in range(len(ITEMS) + PIPE + 1):
                        if n < len(ITEMS):
                            i, h = ITEMS[n]
                            r, w = ROWS[i], WIDTH[i]
                            if n in (HEADS, 3 * HEADS):
                                dve.wait_ge(tk_s.sem, tb12 if n == HEADS else tb34)
                            dve.wait_ge(S_s.sem, n + 1)
                            if n >= 2:
                                dve.wait_ge(P_s.sem, n - 1)
                            b = tri[0:r, 0:r] if i == 0 else bias[0:r, i - 1, SENT:SENT + w]
                            lo = 1024 + (512 * (n % 2) if w <= 512 else 0)
                            ttr_s.did(dve.tensor_tensor_reduce(out=sb_scores[0:r, n % 2, 0:w], in0=Rf[0:r, lo:lo + w], in1=b,
                                                               scale=-0.125, scalar=BIG, op0=ALU.add, op1=ALU.min,
                                                               accum_out=mn[0:r, n % 2:n % 2 + 1]))
                        if n >= 11 and (n - 11) % 8 == 0:
                            i = (n - 11) // 8
                            r = ROWS[i]
                            dve.wait_ge(PV_s.sem, 8 * i + 8)
                            rec_s.did(dve.reciprocal(rrec[0:r, :], rsum[0:r, i % 2, :]))
                            dve.wait_ge(rec_s.sem, i + 1)
                            if i:
                                wait_unit(dve, ("turn", i - 1, 0))
                            on_s.did(dve.tensor_tensor(ksq[0:r, 0, :].rearrange("p (h d) -> p h d", h=HEADS),
                                                       A[0:r, 2, :].rearrange("p (h d) -> p h d", h=HEADS),
                                                       rrec[0:r, :].unsqueeze(2).broadcast_to([r, HEADS, HD]), ALU.mult))
                        if n and PLAN[n - 1] and PLAN[n - 1][0] in GATE_OF:
                            gate(GATE_OF[PLAN[n - 1][0]])
                        more_topk(n)
                        if n == ROUNDS + len(NO_ROUND):
                            assert rounds[0] == ROUNDS
                            to_bias((3, 4))
                            tb34 = tk_s.n
                        if n == SX["pool_diff"]:
                            pool_differences(0)
                        if n == SX["pool_diff2"]:
                            pool_differences(1)
                        if n == SX["ln_diag"]:
                            dve.wait_ge(lnp_s.sem, 1)
                            dve.wait_ge(pd_s.sem, PD_END)
                            for i in range(NT):
                                r = ROWS_P[i]
                                lnd_s.did(dve.tensor_scalar(ln_dg[0:r, i, 0:r], ident[0:r, 0:r], lnr[0:r, i:i + 1], None, ALU.mult))
                        if n == SX["ln_mul"]:
                            wait_evac(dve, ("lnrow", 0, 1))
                            ln_s.did(dve.tensor_tensor(cc[:, :, :], cc[:, :, :], lnrow.unsqueeze(1).broadcast_to([128, 2, TOK]), ALU.mult))
                        if 0 <= n - SX["swish"] < 3:
                            if n == SX["swish"]:
                                dve.wait_ge(gate_s.sem, GATE_OF["gc", 1, 1] + 1)
                            swish(n - SX["swish"])
                        b = n - SX["pages"]
                        if 0 <= b < 8:
                            dve.wait_ge(ixp_s.sem, b + 1)
                            ixr_s.did(dve.reduce_sum(ds[:, :, b, :], ixp.rearrange("p (g h d) -> p g h d", g=2, h=IH), AX.X))
                            page_scores(2 * b)
                            page_scores(2 * b + 1)
                        if n == SX["index"]:
                            dve.wait_ge(wbc_s, 16)
                            dve.wait_ge(ixr_s.sem, 8)
                            sd(lambda: stt(flat, flat, 0.0, wbc.unsqueeze(1).broadcast_to([128, 2, 64]), ALU.max))
                            sd(lambda: dve.reduce_sum(isc.rearrange("p (g b) -> p g b", g=2), ds[:, :, :, :], AX.X))
                            sd(lambda: dve.tensor_scalar(isc, isc, 1.0 / 16, None, ALU.mult), "isc")
                            dve.wait_ge(rows_s, 32)
                            sd(lambda: dve.tensor_tensor(t8[:, :, 0:ID], zis[:, 0:256].rearrange("p (h d) -> p h d", h=IH),
                                                         zis[:, 256:288].unsqueeze(1).broadcast_to([8, IH, ID]), ALU.mult))
                            sd(lambda: dve.reduce_sum(d8, t8[:, :, 0:ID], AX.X))
                            sd(lambda: stt(e8, d8, 0.0, zis[:, 384:392], ALU.max))
                            sd(lambda: dve.reduce_sum(sc8[:, 256:257], e8, AX.X))
                            sd(lambda: dve.tensor_scalar(sc8[:, 256:257], sc8[:, 256:257], 1.0 / 16, None, ALU.mult))
                        if n == SX["index_turn"]:
                            sd(lambda: dve.tensor_tensor(t8, rows8[:, 0:512].rearrange("p (h d) -> p h d", h=8),
                                                         rows8[:, 512:1024].rearrange("p (h d) -> p h d", h=8), ALU.mult))
                            sd(lambda: dve.reduce_sum(snw, t8, AX.X))
                            sd(lambda: dve.tensor_tensor(sn.rearrange("p (b h) -> p b h", b=8), E8.rearrange("p (b h) -> p b h", b=8),
                                                         snw.unsqueeze(1).broadcast_to([8, 8, 8]), ALU.mult))
                            dve.wait_ge(sit_s.sem, 1)
                            sd(lambda: dve.tensor_copy(sc8[:, 0:256], A[0:8, 3, 0:256]))
                        if 0 <= n - SX["topk"] < 4:
                            for _ in range(TOPK_S // 32):
                                sd(lambda: dve.max(m8s, chosen))
                                sd(lambda: dve.match_replace(chosen, m8s, chosen, GONE))
                        if n == SX["topk"] + 3:
                            sd(lambda: dve.tensor_scalar(chosen, chosen, CUT, NEG, ALU.is_gt, ALU.mult), "logit_in")
                        if n == SX["logits"]:
                            dve.wait_ge(slog_s.sem, 1)
                            sd(lambda: dve.reduce_max(smx, logits, AX.X))
                            sd(lambda: dve.tensor_scalar(snm, smx, -0.125, None, ALU.mult), "negmax")
                        if n == SX["norm"]:
                            dve.wait_ge(sexp_s.sem, 1)
                            sd(lambda: dve.reciprocal(srr, srs))
                            sd(lambda: dve.tensor_scalar(pn[:, 0:257], pn[:, 0:257], srr, None, ALU.mult))
                            sd(lambda: dve.tensor_scalar(etp, ET8, pn[:, 256:257], None, ALU.mult), "etp")
                        if n == SX["gate"]:
                            dve.wait_ge(spv_s.sem, 16)
                            for k in range(2):
                                rows = slice(64 * k, 64 * k + 64)
                                dst = yT[rows, 0:4, NTOK:TOK]
                                src = A[rows, 3, 0:64].rearrange("p (c b k) -> p c b k", c=4, b=8)[:, :, :, k]
                                ys_s.did(stt(dst, src, 0.5, dst))
                        if n < len(PLAN):
                            for u in PLAN[n]:
                                if u[0] not in ON_ACT:
                                    take(u)
                        for at, tile, lo, hi in ((30, 2, 0, HALF), (38, 3, HALF, START[4]), (45, 4, START[4], NTOK)):
                            if n == at:
                                wait_evac(dve, ("turn", tile, 0))
                                dve.wait_ge(gate_s.sem, len(GATES))
                                y_s.did(stt(yT[:, 0:4, lo:hi], qT[:, :, lo:hi], 0.5, yT[:, 0:4, lo:hi]))
                    for m in range(KC):
                        take(("out", m, 2))

        with nc.Block() as block:
            spans = [(N_META + 128 * i, 128) for i in range(4)] + [(NTOK, N_SAMPLE)]

            @block.gpsimd
            def _(pool):
                for kc in range(KC // 2, KC):
                    pool.tensor_tensor(yT[:, kc, :], x_hi[:, kc, :].bitcast(F32), x_lo[:, kc, :].bitcast(F32), ALU.add).then_inc(pre["post_sum_pool"], 1)

            @block.tensor
            def _(pe):
                n = 0
                pe.wait_ge(pre["post_sum_dve"], KC // 2)
                pe.wait_ge(pre["post_sum_pool"], KC // 2)
                for i, (c0, r) in enumerate(spans):
                    for g in range(2):
                        if n >= 4:
                            pe.wait_ge(pre["post_act"] if n % 2 else pre["post_dve"], (n - 4) // 2 + 1)
                        for j in range(4):
                            m = pe.transpose(R[0:r, n % 4, 128 * j:128 * j + 128], yT[:, 4 * g + j, c0:c0 + r], ident)
                        m.then_inc(pre["post_turned"], 1)
                        n += 1

            @block.vector
            def _(dve):
                for kc in range(KC // 2):
                    dve.tensor_tensor(yT[:, kc, :], x_hi[:, kc, :].bitcast(F32), x_lo[:, kc, :].bitcast(F32), ALU.add).then_inc(pre["post_sum_dve"], 1)
                for i, (c0, r) in enumerate(spans):
                    dve.wait_ge(pre["post_turned"], 2 * i + 1)
                    dve.tensor_copy(yout[0:r, i, 0:512], R[0:r, (2 * i) % 4, :]).then_inc(pre["post_dve"], 1)

            @block.scalar
            def _(act):
                for i, (c0, r) in enumerate(spans):
                    act.wait_ge(pre["post_turned"], 2 * i + 2)
                    act.activation(yout[0:r, i, 512:1024], R[0:r, (2 * i + 1) % 4, :], ACT.Copy).then_inc(pre["post_act"], 1)

            @block.sync
            def _(sp):
                for i, (c0, r) in enumerate(spans):
                    sp.wait_ge(pre["post_dve"], i + 1)
                    sp.wait_ge(pre["post_act"], i + 1)
                    dst = (o["y_prompt"].rearrange("b t d -> (b t) d")[128 * i:128 * i + 128] if i < 4
                           else o["y_sample"].rearrange("b t d -> (b t) d"))
                    sp.dma_start(dst, yout[0:r, i, :]).then_inc(pre["post_out"], 16)
                sp.wait_ge(pre["post_out"], 16 * len(spans))


_INS = ["x_prompt", "x_sample", "cache_k", "cache_v", "cache_kidx", "state_pool", "state_conv", "page_table",
        "meta_tokens", "norm_g", "w_in", "q_norm_g", "k_norm_g", "pool_w", "pool_scale", "conv_w", "conv_b",
        "conv_norm_g", "conv_norm_b", "w_out"]
_OUTS = [("y_prompt", (1, SEQ, D_MODEL)), ("y_sample", (N_SAMPLE, 1, D_MODEL)),
         ("new_k_prompt", (DEPTH, 1, NTOK, HEADS, HD)), ("new_v_prompt", (DEPTH, 1, NTOK, HEADS, HD)),
         ("new_kidx_prompt", (DEPTH, 1, NTOK, ID)), ("new_pool_prompt", (DEPTH, 1, POOL_STATE, D_B)),
         ("new_conv_prompt", (DEPTH, 1, CONV_STATE, D_C)), ("new_k_sample", (DEPTH, N_SAMPLE, 1, HEADS, HD)),
         ("new_v_sample", (DEPTH, N_SAMPLE, 1, HEADS, HD)), ("new_kidx_sample", (DEPTH, N_SAMPLE, 1, ID)),
         ("new_pool_sample", (DEPTH, N_SAMPLE, POOL_STATE, D_B)), ("new_conv_sample", (DEPTH, N_SAMPLE, CONV_STATE, D_C))]


def kernel(**inputs):
    import concourse.bacc as bacc
    from concourse.bass_utils import run_bass_kernel_spmd

    nc = bacc.Bacc("TRN2", target_bir_lowering=False, num_devices=1)
    arrays, a, o = {}, {}, {}
    given = {name: np.ascontiguousarray(inputs[name]) for name in _INS}
    given["consts"] = constants()
    for name, x in given.items():
        arrays[f"in_{name}"] = x
        a[name] = nc.dram_tensor(f"in_{name}", x.shape, mybir.dt.from_np(x.dtype), kind="ExternalInput").ap()
    for name, shape in _OUTS:
        o[name] = nc.dram_tensor(f"out_{name}", shape, F32, kind="ExternalOutput").ap()
    a["z_rows"] = nc.dram_tensor("z_rows", (N_SAMPLE, 392), F32, kind="Internal").ap()
    a["qkv_rows"] = nc.dram_tensor("qkv_rows", (3, N_SAMPLE, HEADS * HD), F32, kind="Internal").ap()
    program(nc, a, o)
    r = run_bass_kernel_spmd(nc, [arrays], core_ids=[0])
    return tuple(r.results[0][f"out_{name}"] for name, _ in _OUTS)
```
